# Optimizing a Trainium2 kernel written in Bass

```python
import math
import jax
import jax.numpy as jnp
from jax import lax

D_MODEL = 1024
BATCH = 1
SEQ = 512
DEPTH = 2

CHUNK = 64
NORM_EPS = 1e-6
CONV_K = 4
D_FF = 2816
N_MOD = 9

GDN_HEADS = 4
GDN_DK = 128
GDN_DV = 128
GDN_WIDTH = GDN_HEADS * GDN_DV
GDN_CONV_CH = 2 * GDN_HEADS * GDN_DK + GDN_WIDTH

MLA_HEADS = 4
MLA_Q_RANK = 384
MLA_KV_RANK = 256
MLA_NOPE = 128
MLA_ROPE = 64
MLA_DV = 128
MLA_WIDTH = MLA_HEADS * MLA_DV
ROPE_THETA = 10000.0
Q_BLOCK = 128

MIX_WIDTH = GDN_WIDTH + MLA_WIDTH
EVEN_SPLITS = (GDN_CONV_CH, GDN_WIDTH, GDN_HEADS, GDN_HEADS, MLA_Q_RANK, MLA_KV_RANK, MLA_ROPE)
EVEN_IN = GDN_CONV_CH + GDN_WIDTH + 2 * GDN_HEADS + MLA_Q_RANK + MLA_KV_RANK + MLA_ROPE

SSD_D_INNER = 2 * D_MODEL
SSD_HEADDIM = 64
SSD_HEADS = SSD_D_INNER // SSD_HEADDIM
SSD_GROUPS = 4
SSD_STATE = 128
SSD_CONV_CH = SSD_D_INNER + 2 * SSD_GROUPS * SSD_STATE
ODD_SPLITS = (SSD_D_INNER, SSD_CONV_CH, SSD_HEADS)
ODD_IN = SSD_D_INNER + SSD_CONV_CH + SSD_HEADS

N_EVEN = (DEPTH + 1) // 2
N_ODD = DEPTH // 2

kernel_name = "hybrid_gdn_mla_mamba2_macaron_adaln"

def split_cols(t, sizes):
    out, start = [], 0
    for n in sizes:
        out.append(t[..., start:start + n])
        start += n
    return out

def rmsnorm(x, g):
    xf = x.astype(jnp.float32)
    y = xf * lax.rsqrt(jnp.mean(xf * xf, axis=-1, keepdims=True) + NORM_EPS)
    return (y * g.astype(jnp.float32)).astype(x.dtype)

def l2norm(x):
    xf = x.astype(jnp.float32)
    return xf * lax.rsqrt(jnp.sum(xf * xf, axis=-1, keepdims=True) + NORM_EPS)

def adaln_norm(x, g, shift, scale):
    return rmsnorm(x, g) * (1.0 + scale[:, None, :]) + shift[:, None, :]

def swiglu(h, w1, w3, w2):
    return (jax.nn.silu(h @ w1) * (h @ w3)) @ w2

def causal_conv(x, w, b=None):
    k_w = w.shape[0]
    s = x.shape[1]
    xp = jnp.pad(x, ((0, 0), (k_w - 1, 0), (0, 0)))
    y = sum(w[j] * xp[:, j:j + s] for j in range(k_w))
    return y if b is None else y + b

def rope_tables(positions, dim):
    half = dim // 2
    inv_freq = ROPE_THETA ** (-jnp.arange(half, dtype=jnp.float32) / half)
    ang = positions.astype(jnp.float32)[..., None] * inv_freq
    return jnp.cos(ang), jnp.sin(ang)

def apply_rope(x, cos, sin):
    half = x.shape[-1] // 2
    x1, x2 = x[..., :half], x[..., half:]
    return jnp.concatenate([x1 * cos - x2 * sin, x2 * cos + x1 * sin], axis=-1).astype(x.dtype)

def gated_delta_rule(q, k, v, beta_logit, a, a_log, dt_bias):
    b_, s, h, _ = q.shape
    nc = s // CHUNK
    f32 = jnp.float32
    q = l2norm(q) * (GDN_DK ** -0.5)
    k = l2norm(k)
    v = v.astype(f32)
    beta = jax.nn.sigmoid(beta_logit.astype(f32))
    g = -jnp.exp(a_log.astype(f32)) * jax.nn.softplus(a.astype(f32) + dt_bias.astype(f32))

    def to_chunks(t):
        return jnp.swapaxes(t.reshape(b_, nc, CHUNK, h, *t.shape[3:]), 2, 3)

    qc, kc, vc, bc = to_chunks(q), to_chunks(k), to_chunks(v), to_chunks(beta)
    gc = jnp.cumsum(to_chunks(g), axis=-1)
    lower = jnp.tril(jnp.ones((CHUNK, CHUNK), dtype=bool))
    strict = jnp.tril(jnp.ones((CHUNK, CHUNK), dtype=bool), -1)
    decay = jnp.exp(jnp.where(lower, gc[..., :, None] - gc[..., None, :], -jnp.inf))
    kb = kc * bc[..., None]
    a_strict = jnp.where(strict, jnp.einsum("bnhid,bnhjd->bnhij", kb, kc) * decay, 0.0)
    t_mat = a_strict + jnp.eye(CHUNK, dtype=f32)
    rhs = jnp.concatenate([vc * bc[..., None], kb * jnp.exp(gc)[..., None]], axis=-1)
    sol = lax.linalg.triangular_solve(t_mat, rhs, left_side=True, lower=True, unit_diagonal=True)
    u, w = sol[..., :GDN_DV], sol[..., GDN_DV:]
    attn = jnp.einsum("bnhid,bnhjd->bnhij", qc, kc) * decay
    g_last = gc[..., -1]
    k_end = kc * jnp.exp(g_last[..., None] - gc)[..., None]
    q_start = qc * jnp.exp(gc)[..., None]

    def step(state, inp):
        u_i, w_i, q_i, k_i, a_i, gl_i = inp
        v_new = u_i - jnp.einsum("bhck,bhkv->bhcv", w_i, state)
        o_i = jnp.einsum("bhck,bhkv->bhcv", q_i, state) + jnp.einsum("bhij,bhjv->bhiv", a_i, v_new)
        state = state * jnp.exp(gl_i)[..., None, None] + jnp.einsum("bhck,bhcv->bhkv", k_i, v_new)
        return state, o_i

    s0 = jnp.zeros((b_, h, GDN_DK, GDN_DV), f32)
    xs = (jnp.moveaxis(u, 1, 0), jnp.moveaxis(w, 1, 0), jnp.moveaxis(q_start, 1, 0),
          jnp.moveaxis(k_end, 1, 0), jnp.moveaxis(attn, 1, 0), jnp.moveaxis(g_last, 1, 0))
    _, o = lax.scan(step, s0, xs)
    return jnp.transpose(o, (1, 0, 3, 2, 4)).reshape(b_, s, h, GDN_DV)

def latent_attention(c_q, c_kv, k_rope, positions, q_norm_g, w_uq, kv_norm_g, w_ukv):
    b_, s, _ = c_q.shape
    q = jnp.einsum("bsr,rhd->bshd", rmsnorm(c_q, q_norm_g), w_uq)
    q_nope, q_pe = q[..., :MLA_NOPE], q[..., MLA_NOPE:]
    kv = jnp.einsum("bsr,rhd->bshd", rmsnorm(c_kv, kv_norm_g), w_ukv)
    k_nope, v = kv[..., :MLA_NOPE], kv[..., MLA_NOPE:]
    cos, sin = rope_tables(positions, MLA_ROPE)
    q_pe = apply_rope(q_pe, cos[:, :, None, :], sin[:, :, None, :])
    k_pe = apply_rope(k_rope, cos, sin)
    scale = (MLA_NOPE + MLA_ROPE) ** -0.5
    key_chunk = jnp.arange(s) // CHUNK

    def query_block(i):
        start = i * Q_BLOCK
        qn = lax.dynamic_slice_in_dim(q_nope, start, Q_BLOCK, axis=1)
        qp = lax.dynamic_slice_in_dim(q_pe, start, Q_BLOCK, axis=1)
        sc = jnp.einsum("bqhd,bkhd->bhqk", qn, k_nope) + jnp.einsum("bqhd,bkd->bhqk", qp, k_pe)
        sc = sc.astype(jnp.float32) * scale
        q_chunk = (start + jnp.arange(Q_BLOCK)) // CHUNK
        mask = key_chunk[None, :] <= q_chunk[:, None]
        p = jax.nn.softmax(jnp.where(mask, sc, -jnp.inf), axis=-1).astype(v.dtype)
        return jnp.einsum("bhqk,bkhd->bqhd", p, v)

    out = lax.map(query_block, jnp.arange(s // Q_BLOCK))
    return jnp.swapaxes(out, 0, 1).reshape(b_, s, MLA_WIDTH)

def ssd_chunked(x, dt_raw, bm, cm, a_log, dt_bias, d_skip):
    b_, s, _ = x.shape
    nc = s // CHUNK
    r = SSD_HEADS // SSD_GROUPS
    f32 = jnp.float32
    xh = x.astype(f32).reshape(b_, s, SSD_HEADS, SSD_HEADDIM)
    dt = jax.nn.softplus(dt_raw.astype(f32) + dt_bias.astype(f32))
    da = dt * (-jnp.exp(a_log.astype(f32)))
    xc = (xh * dt[..., None]).reshape(b_, nc, CHUNK, SSD_GROUPS, r, SSD_HEADDIM)
    bc = bm.astype(f32).reshape(b_, nc, CHUNK, SSD_GROUPS, SSD_STATE)
    cc = cm.astype(f32).reshape(b_, nc, CHUNK, SSD_GROUPS, SSD_STATE)
    acs = jnp.cumsum(da.reshape(b_, nc, CHUNK, SSD_GROUPS, r), axis=2)
    acs = jnp.transpose(acs, (0, 1, 3, 4, 2))
    lower = jnp.tril(jnp.ones((CHUNK, CHUNK), dtype=bool))
    lmat = jnp.exp(jnp.where(lower, acs[..., :, None] - acs[..., None, :], -jnp.inf))
    cb = jnp.einsum("bclgn,bcsgn->bcgls", cc, bc)
    y_diag = jnp.einsum("bcgls,bcgrls,bcsgrp->bclgrp", cb, lmat, xc)
    d_start = jnp.exp(acs)
    d_end = jnp.exp(acs[..., -1:] - acs)
    c_decay = jnp.exp(acs[..., -1])

    def step(hs, inp):
        c_i, b_i, x_i, ds_i, de_i, cd_i = inp
        y_off = jnp.einsum("blgn,bgrpn,bgrl->blgrp", c_i, hs, ds_i)
        hs = hs * cd_i[..., None, None] + jnp.einsum("blgn,bgrl,blgrp->bgrpn", b_i, de_i, x_i)
        return hs, y_off

    h0 = jnp.zeros((b_, SSD_GROUPS, r, SSD_HEADDIM, SSD_STATE), f32)
    xs = (jnp.moveaxis(cc, 1, 0), jnp.moveaxis(bc, 1, 0), jnp.moveaxis(xc, 1, 0),
          jnp.moveaxis(d_start, 1, 0), jnp.moveaxis(d_end, 1, 0), jnp.moveaxis(c_decay, 1, 0))
    _, y_off = lax.scan(step, h0, xs)
    y = (y_diag + jnp.moveaxis(y_off, 0, 1)).reshape(b_, s, SSD_HEADS, SSD_HEADDIM)
    y = y + d_skip.astype(f32)[:, None] * xh
    return y.reshape(b_, s, SSD_D_INNER)

def even_mixer(h, positions, w_in, conv_w, a_log, dt_bias, gdn_g,
               q_norm_g, w_uq, kv_norm_g, w_ukv, w_out):
    b_, s, _ = h.shape
    qkv, z, beta_logit, a, c_q, c_kv, k_rope = split_cols(h @ w_in, EVEN_SPLITS)
    qkv = jax.nn.silu(causal_conv(qkv, conv_w))
    q, k, v = split_cols(qkv, (GDN_HEADS * GDN_DK, GDN_HEADS * GDN_DK, GDN_WIDTH))
    o_a = gated_delta_rule(q.reshape(b_, s, GDN_HEADS, GDN_DK), k.reshape(b_, s, GDN_HEADS, GDN_DK),
                           v.reshape(b_, s, GDN_HEADS, GDN_DV), beta_logit, a, a_log, dt_bias)
    o_a = rmsnorm(o_a, gdn_g) * jax.nn.silu(z.astype(jnp.float32).reshape(b_, s, GDN_HEADS, GDN_DV))
    o_b = latent_attention(c_q, c_kv, k_rope, positions, q_norm_g, w_uq, kv_norm_g, w_ukv)
    o = jnp.concatenate([o_a.reshape(b_, s, GDN_WIDTH).astype(h.dtype), o_b.astype(h.dtype)], axis=-1)
    return o @ w_out

def odd_mixer(h, w_in, conv_w, conv_b, a_log, dt_bias, d_skip, norm_g, w_out):
    b_, s, _ = h.shape
    z, xbc, dt_raw = split_cols(h @ w_in, ODD_SPLITS)
    xbc = jax.nn.silu(causal_conv(xbc, conv_w, conv_b))
    xs, bm, cm = split_cols(xbc, (SSD_D_INNER, SSD_GROUPS * SSD_STATE, SSD_GROUPS * SSD_STATE))
    y = ssd_chunked(xs, dt_raw, bm, cm, a_log, dt_bias, d_skip)
    y = y * jax.nn.silu(z.astype(jnp.float32))
    yg = y.reshape(b_, s, SSD_GROUPS, SSD_D_INNER // SSD_GROUPS)
    yg = yg * lax.rsqrt(jnp.mean(yg * yg, axis=-1, keepdims=True) + NORM_EPS)
    y = (yg.reshape(b_, s, SSD_D_INNER) * norm_g.astype(jnp.float32)).astype(h.dtype)
    return y @ w_out

def setup_inputs(seed: int = 0) -> dict:
    key = jax.random.key(seed)
    ks = jax.random.split(key, 27)
    f32 = jnp.float32

    def nrm(k, shape, scale):
        return jax.random.normal(k, shape, f32) * scale

    def gain(k, shape):
        return 1.0 + 0.05 * jax.random.normal(k, shape, f32)

    def a_log_init(k, shape):
        return jnp.log(jax.random.uniform(k, shape, f32, 1.0, 16.0))

    def dt_bias_init(k, shape):
        dt = jnp.exp(jax.random.uniform(k, shape, f32, math.log(1e-3), math.log(1e-1)))
        return dt + jnp.log(-jnp.expm1(-dt))

    positions = jnp.broadcast_to(jnp.arange(SEQ, dtype=jnp.int32), (BATCH, SEQ))
    return {
        "x": nrm(ks[0], (BATCH, SEQ, D_MODEL), 1.0),
        "c": nrm(ks[1], (BATCH, D_MODEL), 1.0),
        "positions": positions,
        "ada_w": nrm(ks[2], (DEPTH, D_MODEL, N_MOD * D_MODEL), 0.5 * D_MODEL ** -0.5),
        "ada_b": nrm(ks[3], (DEPTH, N_MOD * D_MODEL), 0.02),
        "norm_g": gain(ks[4], (DEPTH, 3, D_MODEL)),
        "ffn_w1": nrm(ks[5], (DEPTH, 2, D_MODEL, D_FF), D_MODEL ** -0.5),
        "ffn_w3": nrm(ks[6], (DEPTH, 2, D_MODEL, D_FF), D_MODEL ** -0.5),
        "ffn_w2": nrm(ks[7], (DEPTH, 2, D_FF, D_MODEL), D_FF ** -0.5),
        "ev_w_in": nrm(ks[8], (N_EVEN, D_MODEL, EVEN_IN), D_MODEL ** -0.5),
        "gdn_conv_w": nrm(ks[9], (N_EVEN, CONV_K, GDN_CONV_CH), CONV_K ** -0.5),
        "gdn_A_log": a_log_init(ks[10], (N_EVEN, GDN_HEADS)),
        "gdn_dt_bias": dt_bias_init(ks[11], (N_EVEN, GDN_HEADS)),
        "gdn_norm_g": gain(ks[12], (N_EVEN, GDN_DV)),
        "mla_q_norm_g": gain(ks[13], (N_EVEN, MLA_Q_RANK)),
        "mla_w_uq": nrm(ks[14], (N_EVEN, MLA_Q_RANK, MLA_HEADS, MLA_NOPE + MLA_ROPE), MLA_Q_RANK ** -0.5),
        "mla_kv_norm_g": gain(ks[15], (N_EVEN, MLA_KV_RANK)),
        "mla_w_ukv": nrm(ks[16], (N_EVEN, MLA_KV_RANK, MLA_HEADS, MLA_NOPE + MLA_DV), MLA_KV_RANK ** -0.5),
        "ev_w_out": nrm(ks[17], (N_EVEN, MIX_WIDTH, D_MODEL), MIX_WIDTH ** -0.5),
        "ssd_w_in": nrm(ks[18], (N_ODD, D_MODEL, ODD_IN), D_MODEL ** -0.5),
        "ssd_conv_w": nrm(ks[19], (N_ODD, CONV_K, SSD_CONV_CH), CONV_K ** -0.5),
        "ssd_conv_b": nrm(ks[20], (N_ODD, SSD_CONV_CH), 0.02),
        "ssd_A_log": a_log_init(ks[21], (N_ODD, SSD_HEADS)),
        "ssd_dt_bias": dt_bias_init(ks[22], (N_ODD, SSD_HEADS)),
        "ssd_D": gain(ks[23], (N_ODD, SSD_HEADS)),
        "ssd_norm_g": gain(ks[24], (N_ODD, SSD_D_INNER)),
        "ssd_w_out": nrm(ks[25], (N_ODD, SSD_D_INNER, D_MODEL), SSD_D_INNER ** -0.5),
        "final_g": gain(ks[26], (D_MODEL,)),
    }

def reference(x, c, positions, ada_w, ada_b, norm_g, ffn_w1, ffn_w3, ffn_w2,
              ev_w_in, gdn_conv_w, gdn_A_log, gdn_dt_bias, gdn_norm_g,
              mla_q_norm_g, mla_w_uq, mla_kv_norm_g, mla_w_ukv, ev_w_out,
              ssd_w_in, ssd_conv_w, ssd_conv_b, ssd_A_log, ssd_dt_bias, ssd_D, ssd_norm_g, ssd_w_out,
              final_g):
    b_ = x.shape[0]
    c_act = jax.nn.silu(c)
    for l in range(DEPTH):
        mod = (c_act @ ada_w[l] + ada_b[l]).reshape(b_, 3, 3, D_MODEL)
        shift, scale, gate = mod[:, :, 0], mod[:, :, 1], mod[:, :, 2]
        h = adaln_norm(x, norm_g[l, 0], shift[:, 0], scale[:, 0])
        x = x + 0.5 * gate[:, 0, None] * swiglu(h, ffn_w1[l, 0], ffn_w3[l, 0], ffn_w2[l, 0])
        h = adaln_norm(x, norm_g[l, 1], shift[:, 1], scale[:, 1])
        if l % 2 == 0:
            e = l // 2
            y = even_mixer(h, positions, ev_w_in[e], gdn_conv_w[e], gdn_A_log[e], gdn_dt_bias[e],
                           gdn_norm_g[e], mla_q_norm_g[e], mla_w_uq[e], mla_kv_norm_g[e],
                           mla_w_ukv[e], ev_w_out[e])
        else:
            o = l // 2
            y = odd_mixer(h, ssd_w_in[o], ssd_conv_w[o], ssd_conv_b[o], ssd_A_log[o],
                          ssd_dt_bias[o], ssd_D[o], ssd_norm_g[o], ssd_w_out[o])
        x = x + gate[:, 1, None] * y
        h = adaln_norm(x, norm_g[l, 2], shift[:, 2], scale[:, 2])
        x = x + 0.5 * gate[:, 2, None] * swiglu(h, ffn_w1[l, 1], ffn_w3[l, 1], ffn_w2[l, 1])
    return rmsnorm(x, final_g)


_drawn_inputs = setup_inputs


def setup_inputs(seed=0):
    import zlib

    import numpy as np

    out = dict(_drawn_inputs(seed))
    spreads = {}
    factors = {'gdn_norm_g': 8.0,
     'mla_q_norm_g': 8.0,
     'mla_kv_norm_g': 8.0,
     'ssd_conv_b': 7.695,
     'ssd_D': 94.778,
     'ssd_norm_g': 3.963,
     'ssd_A_log': 24.696,
     'ssd_dt_bias': 21.624}
    for name, (base, spread) in spreads.items():
        noise = np.random.default_rng([zlib.crc32(name.encode()), seed]).standard_normal(out[name].shape)
        drawn = base * np.exp(spread * noise) if base else spread * noise
        out[name] = jnp.asarray(drawn.astype(out[name].dtype))
    for name, factor in factors.items():
        out[name] = (out[name] * factor).astype(out[name].dtype)
    return out
```

```python
from contextlib import ExitStack

import numpy as np

import concourse.bass as bass
from concourse import mybir

F32 = mybir.dt.float32
F32R = mybir.dt.float32r
BF16 = mybir.dt.bfloat16
I32 = mybir.dt.int32
U8 = mybir.dt.uint8
ALU = mybir.AluOpType
ACT = mybir.ActivationFunctionType
AX_X = mybir.AxisListType.X

P = 128
D = 1024
SEQ = 512
DEPTH = 2
D_FF = 2816
EPS = 1e-6
KT = D // P
FT = D_FF // P
CH = 128
NB = SEQ // CH
HEADS = 4
GDN_TILES = 3 * HEADS
EV_TILES = GDN_TILES + HEADS + 1 + 3 + 2 + 1
MLA_RANKS = (384, 256)
SSD_H = 32
SSD_G = 4
SSD_XT = 16
SSD_CONV = SSD_XT + 2 * SSD_G
OD_TILES = SSD_CONV + SSD_XT + 1
RAW, HL = 4, 2
BIG_NEG = -3.0e38
LEVELS = [1, 2, 4, 8, 16, 32, 64]
PI = float(np.float32(3.1415925))
ROUND = 12582912.0

PHASES, _u = {}, 0
for _name, _n, _nk in (
        ("up0", 2 * FT, 8), ("down0", 16, 11),
        ("ev_in", EV_TILES, 8), ("uq", 3, 6), ("ukv", 2, 8), ("ev_out", 8, 8),
        ("up1", 2 * FT, 8), ("down1", 16, 11), ("up2", 2 * FT, 8), ("down2", 16, 11),
        ("od_in", OD_TILES, 8), ("od_out", 16, 8),
        ("up3", 2 * FT, 8), ("down3", 16, 11)):
    PHASES[_name] = (_u, _n, _nk)
    _u += _n

HI_AT, _a, _p = {}, 0, 0
for _name, (_u, _n, _nk) in PHASES.items():
    if _name[:2] in ("up", "do"):
        HI_AT[_name] = (_a, None)
        _a += _n
    else:
        HI_AT[_name] = (None, _p)
        _p += _n

ADA_COLS = 384
ADA_G = 3 * D // ADA_COLS
ADA_AT = {"down0": (8, 4), "down1": (24, 2), "down2": (32, 4)}

VEC, _c = {}, 0
for _name, _n in (("c", 8), ("ada_b", 144), ("norm_g", 48), ("final_g", 8), ("gconv", 48), ("gdn_g", 1),
                  ("q_g", 3), ("kv_g", 2), ("sconv", 96), ("sconv_b", 24), ("ssd_d", 16), ("ssd_g", 16),
                  ("g_alog", 4), ("g_dtb", 4), ("s_alog", 32), ("s_dtb", 32), ("inv_freq", 1)):
    VEC[_name] = _c
    _c += _n
NVEC = _c

Q0, K0, V0, Z0, QN0, QPE0, KN0, VM0, KPE, CQ0, VB0, MT0, AT0, ST = 0, 4, 8, 12, 16, 20, 22, 26, 30, 31, 31, 35, 39, 43
B0, C0, SZ0 = 16, 20, 24
MIDS = 44


class Tally:

    def __init__(self, sem, n=0):
        self.sem, self.n, self.k = sem, n, 0

    def inc(self, ins):
        ins.then_inc(self.sem, 1)
        self.n = self.n + 1
        self.k += 1

    def enter(self, i, per):
        self.base, self.per, self.k0 = self.n, per, self.k
        self.n = self.base + i * per

    def leave(self, count):
        assert self.k - self.k0 == self.per, (self.k - self.k0, self.per)
        self.n = self.base + count * self.per


def one(ap):
    return ap.rearrange("p a n -> p (a n)")


def build(nc, src, out, dbg):
    ctx = ExitStack()
    with ctx:
        def sb(name, shape, dt=F32):
            return ctx.enter_context(nc.sbuf_tensor(name, shape, dt))

        def sem(name):
            return ctx.enter_context(nc.semaphore(name))

        with nc.sbuf_tensor("h_f", [P, 16, SEQ], F32) as h_f:
            pass
        with nc.sbuf_tensor("ada_w_sb", [P, 2, KT, ADA_COLS], F32) as ada_sb:
            pass
        h_hi = sb("h_hi", [P, KT, SEQ], F32R)
        h_lo = sb("h_lo", [P, KT, SEQ], F32R)
        with nc.sbuf_tensor("mid_f", [P, MIDS, SEQ], F32) as mid:
            pass
        mid_hi = sb("mid_hi", [P, FT, SEQ], F32R)
        mid_lo = sb("mid_lo", [P, FT, SEQ], F32R)

        x = sb("x_sb", [P, KT, SEQ])
        raw = sb("weight_raw", [P, RAW, 11 * P])
        whi = sb("weight_hi", [P, HL, 11 * P], F32R)
        wlo = sb("weight_lo", [P, HL, 11 * P], F32R)
        ada_acc = sb("ada_acc", [P, 2, ADA_COLS])
        tmp = sb("tmp", [P, 2, SEQ])
        gate_s = sb("gate_s", [P, 2, SEQ])
        sq = sb("sq", [P, 2, SEQ])
        ssacc = sb("ssacc", [P, SEQ])
        rstd = sb("rstd", [P, SEQ])
        vec = sb("vec", [P, NVEC])
        mod = sb("mod", [P, 144])
        moda = sb("moda", [P, 48])
        cact = sb("cact", [P, KT])
        ident = sb("ident", [P, P])
        ones = sb("ones", [P, P])
        tri = sb("tri", [P, P])
        rot = sb("rot", [P, P])
        ident_b = sb("ident_b", [P, P], BF16)
        neg_b = sb("neg_b", [P, P], BF16)
        pos_b = sb("pos_b", [P, P], BF16)
        lvl = sb("lvl", [P, 2 * len(LEVELS), P], U8)
        qmask = sb("qmask", [P, P])
        pos = sb("pos", [P, SEQ], I32)
        small = sb("small", [P, 10, P])
        cols = sb("cols", [P, 16])
        hstate = sb("hstate", [P, NB - 1, SEQ])
        epsc = sb("epsc", [P, 4])
        ps = [ctx.enter_context(nc.psum_tensor(f"bank{i}", [P, SEQ], F32)) for i in range(8)]

        const_in = sem("const_in"); x_in = sem("x_in"); stored = sem("stored"); dbg_out = sem("dbg_out")
        raw_full = [sem(f"raw_full{i}") for i in range(RAW)]
        hi_done = sem("weight_hi_done"); lo_done = sem("weight_lo_done")
        unit_done = sem("unit_done"); act_hi = sem("act_weight_hi")
        ada_full = [sem("ada_full0"), sem("ada_full1")]
        ada_done = sem("ada_acc_done"); mod_sum = sem("mod_summed")
        consts = sem("consts_ready"); cact_done = sem("cact_done")
        x_ready = sem("x_ready"); sq_done = sem("sq_done"); ss_add = sem("ss_add"); ss_sum = sem("ss_summed")
        rstd_ready = sem("rstd_ready"); ln_ready = sem("ln_ready")
        ht_ready = sem("h_scaled"); hhi_done = sem("h_hi_done"); hlo_done = sem("h_lo_done")
        silu_done = sem("silu_done"); prod_done = sem("prod_done")
        midhi_done = sem("mid_hi_done"); midlo_done = sem("mid_lo_done")
        dve_step = sem("dve_step"); act_step = sem("act_step")
        out_ready = sem("out_ready")
        S = {}

        def named(*names):
            for n in names:
                S[n] = sem(n)

        named("evin_free", "evsilu", "gate_a", "dt_a", "l2sq", "l2ln", "l2sum", "l2r", "l2done", "ba_t", "ba_sb", "ba_e", "g_done",
              "gc_ps", "gc_sb", "gcrow_ps", "gcrow_sb", "glast_ps", "gcols", "gcols2",
              "rsq", "rsum", "rln", "rr", "rt", "rhi", "rlo", "pj_free",
              "pj_ps", "hd_ps", "hd_exp", "hd_free", "kt_free",
              "y_ps", "y_sb", "z_ps", "inv_up",
              "ks_ps", "r_sb", "vn_ps", "vn_sb", "su_ps", "s_up", "o_ps", "o_sb",
              "osq", "osum", "oln", "orr", "ot", "ohi", "olo",
              "trig_a", "trig_d", "rot_ps", "rope", "sc_ps", "sc_mask", "sc_exp", "sc_norm", "pt_ps", "pt_sb",
              "av_ps", "av_hi", "av_lo", "sc_max")
        named("odin_free", "odsilu", "dt_t", "dt_sb", "dt_e", "da_sb", "acs_ps", "acs_sb", "acr_ps", "acr_sb",
              "acl_ps", "acl_d", "acl_a", "tk_ps", "tk_sb", "cb_ps", "cb_sb", "xde", "st_ps", "st_up",
              "L_ps", "L_sb", "G_sb", "E_ps", "E_sb", "yd_ps", "yo_ps", "y_done",
              "ysq", "ysum", "yln", "yrr", "yt", "yhi", "ylo")

        def vcol(name, i=0):
            return vec[:, VEC[name] + i:VEC[name] + i + 1]

        block = ctx.enter_context(nc.Block())

        def used(u):
            return u + 1 + HL

        def x_at(n, m):
            return KT * n + m + 1

        def ss_at(n, m):
            return KT * n + m + 1 + 2

        def gd(name):
            i = ["beta", "g", "gc", "nbeta", "nbe", "ke", "egl", "ngc", "eg", "glast", "z", "t0", "t1", "t2", "t3",
                 "t4", "t5"].index(name)
            return small[:, i // 8, (i % 8) * 16:(i % 8) * 16 + 16]

        def sd(name):
            return small[:, ["dt", "da", "acs", "nacs", "de", "cd", "t0", "t1", "t2", "t3"].index(name), :]

        rows = gate_s[:, 0, :]
        gcrow = ssacc[0:HEADS, :]
        acrow = ssacc[0:SSD_H, :]
        acc_flat = ada_acc[:, :, :].rearrange("p a n -> p (a n)")[:, 0:SEQ]

        lvl_in = h_f[:, 12:16, :].rearrange("p a n -> p (a n)")[:, 0:2 * len(LEVELS) * P].bitcast(I32)

        def xde_at(q):
            return rstd[:, :] if q % 2 == 0 else acc_flat

        def hst(b):
            return hstate[:, b - 1, :]

        def chunk(b):
            return slice(b * CH, (b + 1) * CH)

        NQ = len(LEVELS) * HEADS
        inv_seq = [(lv, h) for lv in range(len(LEVELS)) for h in range(HEADS)]
        att_seq = [(h, b) for h in range(HEADS) for b in range(NB)]
        ev_ps = [ps[4 + m % 2] for m in range(KT)]

        def pj_ready(t):
            u, v = PHASES["uq"][0], PHASES["ukv"][0]
            if t < 6:
                return (unit_done, used(u + t // 2)) if t % 2 else (S["pj_ps"], t // 2 + 1)
            if t < 10:
                return (unit_done, used(v)) if t == 9 else (S["pj_ps"], t - 6 + 4)
            return (unit_done, used(v + 1)) if t == 13 else (S["pj_ps"], t - 10 + 7)

        @block.sync
        def _(sp):
            def unit(u, w_ap, nk):
                u0, di = u
                s = u0 % RAW
                sp.wait_ge(lo_done, u0 + di + 1)
                sp.dma_start(raw[:, s, 0:nk * P], w_ap).then_inc(raw_full[s], 16)

            def run(name, w, f=None, extra=None):
                u0, n, nk = PHASES[name]
                n4 = n // 4 if n >= 8 else 0

                def at(j):
                    a = w[f] if f is not None else w
                    return a[bass.ds(j, 1), :, :].rearrange("a p n -> (a p) n")
                if n4:
                    with sp.Fori(0, n4) as i:
                        for j in range(4):
                            unit((u0 + j, i * 4), at(i * 4 + j), nk)
                            if extra:
                                extra(i, j)
                for j in range(4 * n4, n):
                    unit((u0 + j, 0), w[f, j] if f is not None else w[j], nk)

            def ada(g0, gi):
                sp.wait_ge(ada_done, g0 + gi + 1)
                sp.dma_start(ada_sb[:, g0 % 2, :, :],
                             src["ada"][bass.ds(g0 + gi, 1), :, :].rearrange("a p (k n) -> (a p) k n", k=KT)
                             ).then_inc(ada_full[g0 % 2], 16)

            def ada_extra(name):
                g0, per = ADA_AT[name]
                u0 = PHASES[name][0]

                def extra(i, j):
                    if j == 1:
                        sp.wait_ge(unit_done, used(u0 - 1))
                    if j in (1, 3):
                        h = per // 2
                        for q in range(h):
                            ada(g0 + (j // 2) * h + q, i * per)
                return extra

            for g in range(ADA_G):
                if g == ADA_G - 2:
                    for j in range(4):
                        u0, n, nk = PHASES["up0"]
                        sp.dma_start(raw[:, j, 0:nk * P], src["up"][0, j]).then_inc(raw_full[j], 16)
                ada(g, 0)
            u0, n, nk = PHASES["up0"]
            with sp.Fori(1, n // 4) as i:
                for j in range(4):
                    unit((u0 + j, i * 4), src["up"][0][bass.ds(i * 4 + j, 1), :, :].rearrange("a p n -> (a p) n"), nk)
            run("down0", src["down"], 0, ada_extra("down0"))
            run("ev_in", src["ev_in"])
            run("uq", src["uq"])
            run("ukv", src["ukv"])
            run("ev_out", src["ev_out"])
            run("up1", src["up"], 1)
            run("down1", src["down"], 1, ada_extra("down1"))
            run("up2", src["up"], 2)
            run("down2", src["down"], 2, ada_extra("down2"))
            run("od_in", src["od_in"])
            run("od_out", src["od_out"])
            run("up3", src["up"], 3)
            run("down3", src["down"], 3)
            for kt in range(KT):
                sp.wait_ge(out_ready, kt + 1)
                sp.dma_start(out[kt], mid[:, kt, :]).then_inc(stored, 16)
            sp.wait_ge(stored, 16 * KT)

        @block.gpsimd
        def _(pool):
            pool.sem_inc(lo_done, RAW)

            def unit(u0, di, nk, a0, p0):
                s, h = u0 % RAW, u0 % HL
                if a0 is None:
                    pool.wait_ge(raw_full[s], (u0 // RAW + 1) * 16 + di * (16 // RAW))
                    pool.wait_ge(unit_done, u0 + di + 1)
                    pool.tensor_tensor(whi[:, h, 0:nk * P], raw[:, s, 0:nk * P], ones[:, 0:1].to_broadcast([P, nk * P]),
                                       ALU.mult).then_inc(hi_done, 1)
                    pool.wait_ge(hi_done, p0 + di + 1)
                else:
                    pool.wait_ge(act_hi, a0 + di + 1)
                pool.tensor_tensor(wlo[:, h, 0:nk * P], raw[:, s, 0:nk * P], whi[:, h, 0:nk * P].bitcast(F32),
                                   ALU.subtract).then_inc(lo_done, 1)
            for name, (u0, n, nk) in PHASES.items():
                n4 = n // 4 if n >= 8 else 0
                a0, p0 = HI_AT[name]

                def at(j, di):
                    unit(u0 + j, di, nk, None if a0 is None else a0 + j, None if p0 is None else p0 + j)
                if n4:
                    with pool.Fori(0, n4) as i:
                        for j in range(4):
                            at(j, i * 4)
                for j in range(4 * n4, n):
                    at(j, 0)

        @block.tensor
        def _(pe):
            mm = pe.matmul
            pe.sem_inc(unit_done, HL)
            pe.sem_inc(mod_sum, 2)
            pe.wait_ge(consts, 1)

            def split_ready(u0, di):
                pe.wait_ge(lo_done, u0 + di + 1 + RAW)

            def passes(bank, u0, k, hi, lo, start, stop, w_at=None):
                s = u0 % HL
                c = slice(k * P, (k + 1) * P) if w_at is None else w_at
                mm(bank, wlo[:, s, c], hi, start=start, stop=False)
                mm(bank, whi[:, s, c], lo, start=False, stop=False)
                return mm(bank, whi[:, s, c], hi, start=False, stop=stop)

            def ffn_up(f):
                u0, n, nk = PHASES[f"up{f}"]
                q0 = FT * f
                hl0 = KT * {0: 0, 1: 2, 2: 3, 3: 5}[f]

                def body(i, first):
                    for t in range(2):
                        pe.wait_ge(prod_done, q0 + i * 2 + t + 1)
                        for w in range(2):
                            uu = u0 + 2 * t + w
                            split_ready(uu, i * 4)
                            for k in range(KT):
                                if first and t == 0 and w == 0:
                                    pe.wait_ge(hlo_done, hl0 + k + 1)
                                last = passes(ps[2 * t + w][:, :], uu, k, h_hi[:, k, :], h_lo[:, k, :], k == 0, k == KT - 1)
                            last.then_inc(unit_done, 1)
                body(0, True)
                with pe.Fori(1, n // 4) as i:
                    body(i, False)

            def mod_group(g0, gi):
                pe.wait_ge(ada_done, g0 + gi + 1 + 2)
                for c in range(3):
                    last = mm(ps[6][:, bass.ds(3 * g0 + c + gi * 3, 1)],
                              ada_acc[:, g0 % 2, c * P:(c + 1) * P], ones[:, 0:1], start=True, stop=True)
                last.then_inc(mod_sum, 1)

            def ffn_down(f):
                name = f"down{f}"
                u0, n, nk = PHASES[name]
                nv = {0: 1, 1: 3, 2: 4, 3: 6}[f]

                def body(i, first):
                    for t in range(2):
                        pe.wait_ge(x_ready, x_at(nv, 0) + i * 2 + t - 2)
                        for w in range(2):
                            uu = u0 + 2 * t + w
                            split_ready(uu, i * 4)
                            if first and t == 0:
                                pe.wait_ge(midlo_done, FT * f + 11 * (w + 1))
                            for k in range(11):
                                kk = 11 * w + k
                                last = passes(ps[4 + t][:, :], uu, k, mid_hi[:, kk, :], mid_lo[:, kk, :], kk == 0, kk == 21)
                            last.then_inc(unit_done, 1)
                        if name in ADA_AT:
                            g0, per = ADA_AT[name]
                            for q in range(per // 2):
                                mod_group(g0 + t * (per // 2) + q, i * per)
                body(0, True)
                with pe.Fori(1, n // 4) as i:
                    body(i, False)

            def norm_sum(n):
                pe.wait_ge(ss_add, ss_at(n, KT - 1))
                mm(ps[7][:, :], ones[:, :], ssacc[:, :], start=True, stop=True).then_inc(ss_sum, 1)

            for g in range(ADA_G):
                mod_group(g, 0)
            norm_sum(0)
            ffn_up(0)
            ffn_down(0)
            norm_sum(1)
            u0, n, nk = PHASES["ev_in"]

            def proj_tile(u0, j, di, bank, free, freed, hl0=None):
                pe.wait_ge(free, freed + di + 1)
                split_ready(u0 + j, di)
                for k in range(KT):
                    if hl0 is not None:
                        pe.wait_ge(hlo_done, hl0 + k + 1)
                    last = passes(ps[bank][:, :], u0 + j, k, h_hi[:, k, :], h_lo[:, k, :], k == 0, k == KT - 1)
                last.then_inc(unit_done, 1)
            for j in range(4):
                proj_tile(u0, j, 0, j, S["evin_free"], j, KT * 1 if j == 0 else None)
            with pe.Fori(1, 5) as i:
                for j in range(4):
                    proj_tile(u0, j, i * 4, j, S["evin_free"], j)
            for j in range(20, EV_TILES):
                proj_tile(u0, j, 0, j % 4, S["evin_free"], j)
            for t in range(8):
                pe.wait_ge(S["l2sq"], t + 1)
                if t >= 2:
                    pe.wait_ge(S["l2ln"], t - 1)
                mm(ps[4 + t % 2][:, :], ones[:, :], sq[:, t % 2, :], start=True, stop=True).then_inc(S["l2sum"], 1)
            for a, nt in enumerate((3, 2)):
                for t in range(nt):
                    q = 3 * a + t
                    pe.wait_ge(S["rsq"], q + 1)
                    mm(ps[6][:, :], ones[:, :], sq[:, q % 2, :], start=t == 0, stop=t == nt - 1).then_inc(S["rsum"], 1)
                if a == 0:
                    pe.wait_ge(S["rln"], 1)
            pe.wait_ge(S["evin_free"], 4 + EV_TILES)
            for b in range(NB):
                last = pe.transpose(ps[7][:, 8 * b:8 * b + 8], rows[0:8, b * CH:(b + 1) * CH], ident[0:8, 0:8])
            last.then_inc(S["ba_t"], 1)
            u0 = PHASES["uq"][0]
            tile = 0
            for j in range(3):
                split_ready(u0 + j, 0)
                for t in range(2):
                    if tile >= 4:
                        pe.wait_ge(S["pj_free"], tile - 3)
                    for k in range(3):
                        if tile == 0:
                            pe.wait_ge(S["rlo"], k + 1)
                        last = passes(ps[tile % 4][:, :], u0 + j, 3 * t + k, h_hi[:, k, :], h_lo[:, k, :], k == 0, k == 2)
                    tile += 1
                    if t == 0:
                        last.then_inc(S["pj_ps"], 1)
                last.then_inc(unit_done, 1)
            u0 = PHASES["ukv"][0]
            split_ready(u0, 0)
            pe.wait_ge(S["rlo"], 5)
            for t in range(4):
                pe.wait_ge(S["pj_free"], tile - 3)
                for k in range(2):
                    last = passes(ps[tile % 4][:, :], u0, 2 * t + k, h_hi[:, 3 + k, :], h_lo[:, 3 + k, :], k == 0, k == 1)
                tile += 1
                last.then_inc(S["pj_ps"] if t < 3 else unit_done, 1)
            split_ready(u0 + 1, 0)
            s = (u0 + 1) % HL
            for b in range(NB):
                pe.wait_ge(S["pj_free"], tile - 3)
                bank = ps[tile % 4][:, :]
                for k in range(2):
                    c = slice(k * SEQ, (k + 1) * SEQ)
                    tok = chunk(b)
                    mm(bank, h_lo[:, 3 + k, tok], whi[:, s, c], start=k == 0, stop=False)
                    mm(bank, h_hi[:, 3 + k, tok], wlo[:, s, c], start=False, stop=False)
                    last = mm(bank, h_hi[:, 3 + k, tok], whi[:, s, c], start=False, stop=k == 1)
                tile += 1
                last.then_inc(S["pj_ps"] if b < 3 else unit_done, 1)
            pe.wait_ge(S["g_done"], 1)
            mm(ps[4][:, 0:16], tri[:, :], gd("g"), start=True, stop=True).then_inc(S["gc_ps"], 1)
            pe.wait_ge(S["gc_sb"], 1)
            for b in range(NB):
                last = pe.transpose(ps[5][0:4, b * CH:(b + 1) * CH], gd("gc")[:, 4 * b:4 * b + 4], ident[:, :])
            last.then_inc(S["gcrow_ps"], 1)
            mm(ps[6][:, 0:16], ident[:, P - 1:P].to_broadcast([P, P]), gd("gc"), start=True, stop=True
               ).then_inc(S["glast_ps"], 1)
            pe.wait_ge(S["gcrow_sb"], 1)
            pe.wait_ge(S["pj_free"], 14)
            pe.wait_ge(S["gcols"], 1)
            for h in range(HEADS):
                sel = ident[0:4, h:h + 1].to_broadcast([4, P])
                kh, qh, vh = mid[:, K0 + h, :], mid[:, Q0 + h, :], mid[:, V0 + h, :]
                if h:
                    pe.wait_ge(S["hd_exp"], 3 * h)
                mm(ps[0][:, :], sel, gcrow, start=True, stop=False)
                mm(ps[0][:, :], ident_b[:, :], pos_b[:, :].unsqueeze(1).to_broadcast([P, NB, P]), start=False, stop=True)
                mm(ps[1][:, :], sel, gcrow, start=True, stop=False)
                mm(ps[1][:, :], ident_b[:, :], neg_b[:, :].unsqueeze(1).to_broadcast([P, NB, P]), start=False, stop=True)
                mm(ps[2][:, :], sel, gcrow, start=True, stop=True).then_inc(S["hd_ps"], 1)
                if h:
                    pe.wait_ge(S["hd_free"], 4 * h)
                for b in range(NB):
                    tok = chunk(b)
                    mm(ps[3][:, tok], kh[:, tok], kh[:, tok], start=True, stop=True)
                for b in range(NB):
                    tok = chunk(b)
                    mm(ps[4][:, tok], kh[:, tok], qh[:, tok], start=True, stop=True)
                for b in range(NB):
                    tok = chunk(b)
                    pe.transpose(ps[5][:, tok], kh[:, tok], ident[:, :])
                for b in range(NB):
                    tok = chunk(b)
                    last = pe.transpose(ps[6][:, tok], vh[:, tok], ident[:, :])
                last.then_inc(S["hd_ps"], 1)
            pe.wait_ge(S["hd_free"], 4 * HEADS)
            pe.wait_ge(S["hd_exp"], 3 * HEADS)

            def inv_y(q):
                lv, h = inv_seq[q]
                pe.wait_ge(S["inv_up"], q + 1)
                if q >= 2:
                    pe.wait_ge(S["y_sb"], q - 1)
                for b in range(NB):
                    tok = chunk(b)
                    last = mm(ps[q % 2][:, tok], h_f[:, 0 + h, tok], mid[:, MT0 + h, tok], start=True, stop=True)
                last.then_inc(S["y_ps"], 1)

            def inv_z(q):
                lv, h = inv_seq[q]
                pe.wait_ge(S["y_sb"], q + 1)
                if q >= 2:
                    pe.wait_ge(S["inv_up"], q - 1 + HEADS)
                for b in range(NB):
                    if lv < len(LEVELS) - 1:
                        tok = chunk(b)
                        mm(ps[2 + q % 2][:, tok], h_f[:, 8 + h, tok], h_f[:, 4 + h, tok], start=True, stop=True)
                for b in range(NB):
                    tok = chunk(b)
                    last = mm(ps[4 + q % 2][:, tok], h_f[:, 4 + h, tok], h_f[:, 8 + h, tok], start=True, stop=True)
                last.then_inc(S["z_ps"], 1)
            for q in range(NQ + 1):
                if q < NQ:
                    inv_y(q)
                if q >= 1:
                    inv_z(q - 1)
            pe.wait_ge(S["inv_up"], NQ + HEADS)
            for b in range(NB):
                tok = chunk(b)
                if b:
                    pe.wait_ge(S["s_up"], b)
                    for h in range(HEADS):
                        last = mm(ps[0][:, h * P:(h + 1) * P], mid[:, K0 + h, tok], mid[:, ST, h * P:(h + 1) * P], start=True, stop=True)
                    last.then_inc(S["ks_ps"], 1)
                pe.wait_ge(S["r_sb"], b + 1)
                for h in range(HEADS):
                    last = mm(ps[1][:, h * P:(h + 1) * P], mid[:, MT0 + h, tok], tmp[:, 0, h * P:(h + 1) * P], start=True, stop=True)
                last.then_inc(S["vn_ps"], 1)
                pe.wait_ge(S["vn_sb"], b + 1)
                if b < NB - 1:
                    for h in range(HEADS):
                        last = mm(ps[2][:, h * P:(h + 1) * P], h_f[:, 12 + h, tok], tmp[:, 1, h * P:(h + 1) * P], start=True, stop=True)
                    last.then_inc(S["su_ps"], 1)
                if b:
                    pe.wait_ge(S["o_sb"], b)
                for h in range(HEADS):
                    hc = slice(h * P, (h + 1) * P)
                    last = mm(ps[3][:, hc], tmp[:, 1, hc], mid[:, AT0 + h, tok], start=True, stop=b == 0)
                    if b:
                        last = mm(ps[3][:, hc], mid[:, ST, hc], mid[:, Q0 + h, tok], start=False, stop=True)
                last.then_inc(S["o_ps"], 1)
            for h in range(HEADS):
                pe.wait_ge(S["osq"], h + 1)
                if h >= 2:
                    pe.wait_ge(S["oln"], h - 1)
                mm(ps[4 + h % 2][:, :], ones[:, :], sq[:, h % 2, :], start=True, stop=True).then_inc(S["osum"], 1)
            pe.wait_ge(S["o_sb"], NB)
            for r in range(3):
                mm(ps[r][:, :], rot[:, :], mid[:, (QPE0, QPE0 + 1, KPE)[r], :], start=True, stop=True).then_inc(S["rot_ps"], 1)
            pe.wait_ge(S["rope"], 3)
            pe.wait_ge(S["oln"], HEADS)

            def att_scores(q):
                h, b = att_seq[q]
                nk = (b + 1) * CH
                tok = chunk(b)
                half = slice(64 * (h % 2), 64 * (h % 2) + 64)
                if q >= 2:
                    pe.wait_ge(S["sc_exp"], q - 1)
                bank = ps[q % 2][:, 0:nk]
                mm(bank, mid[:, QN0 + h, tok], mid[:, KN0 + h, 0:nk], start=True, stop=False)
                mm(bank, mid[half, QPE0 + h // 2, tok], mid[half, KPE, 0:nk], start=False, stop=True).then_inc(S["sc_ps"], 1)

            def att_values(q):
                h, b = att_seq[q]
                tok = chunk(b)
                pe.wait_ge(S["sc_norm"], q + 1)
                if q >= 2:
                    pe.wait_ge(S["pt_sb"], q - 1)
                for kb in range(b + 1):
                    last = pe.transpose(ps[2 + q % 2][:, kb * CH:(kb + 1) * CH], mid[:, q % 2, kb * CH:(kb + 1) * CH], ident[:, :])
                last.then_inc(S["pt_ps"], 1)
                pe.wait_ge(S["pt_sb"], q + 1)
                if b == 0 and h >= 2:
                    pe.wait_ge(S["av_lo"], h - 1)
                for kb in range(b + 1):
                    last = mm(ps[4 + h % 2][:, tok], mid[:, VM0 + kb, h * P:(h + 1) * P], mid[:, 2 + q % 2, kb * CH:(kb + 1) * CH],
                              start=kb == 0, stop=kb == b)
                last.then_inc(S["av_ps"], 1)
            for q in range(len(att_seq) + 1):
                if q < len(att_seq):
                    att_scores(q)
                if q >= 1:
                    att_values(q - 1)
            u0 = PHASES["ev_out"][0]
            pe.wait_ge(S["olo"], HEADS)
            pe.wait_ge(S["av_lo"], HEADS)
            pe.wait_ge(S["av_hi"], HEADS)
            for m in range(KT):
                pe.wait_ge(x_ready, x_at(2, m) - 2)
                split_ready(u0 + m, 0)
                for k in range(KT):
                    last = passes(ps[4 + m % 2][:, :], u0 + m, k, h_hi[:, k, :], h_lo[:, k, :], k == 0, k == KT - 1)
                last.then_inc(unit_done, 1)
            norm_sum(2)
            ffn_up(1)
            ffn_down(1)
            norm_sum(3)
            ffn_up(2)
            ffn_down(2)
            norm_sum(4)
            u0, n, nk = PHASES["od_in"]
            for j in range(4):
                proj_tile(u0, j, 0, j, S["odin_free"], j, KT * 4 if j == 0 else None)
            with pe.Fori(1, 10) as i:
                for j in range(4):
                    proj_tile(u0, j, i * 4, j, S["odin_free"], j)
            proj_tile(u0, 40, 0, 0, S["odin_free"], 40)
            pe.wait_ge(S["odin_free"], 4 + OD_TILES)
            for b in range(NB):
                last = pe.transpose(ps[4][:, 32 * b:32 * b + 32], rows[0:32, b * CH:(b + 1) * CH], ident[0:32, 0:32])
            last.then_inc(S["dt_t"], 1)
            pe.wait_ge(S["odin_free"], 4 + OD_TILES)
            pe.wait_ge(S["odsilu"], SSD_CONV + SSD_XT)
            pe.wait_ge(S["da_sb"], 1)
            mm(ps[5][:, 0:P], tri[:, :], sd("da"), start=True, stop=True).then_inc(S["acs_ps"], 1)
            seq = [(b, g) for b in range(NB) for g in range(SSD_G)]
            for q, (b, g) in enumerate(seq):
                tok = chunk(b)
                if q >= 2:
                    pe.wait_ge(S["tk_sb"], q - 1)
                for t in range(4):
                    last = pe.transpose(ps[q % 2][:, t * P:(t + 1) * P], mid[:, 4 * g + t, tok], ident[:, :])
                last.then_inc(S["tk_ps"], 1)
            for b in range(NB):
                tok = chunk(b)
                pe.wait_ge(S["tk_sb"], 16 + b - 1)
                for g in range(SSD_G):
                    last = pe.transpose(ps[b % 2][:, g * P:(g + 1) * P], mid[:, B0 + g, tok], ident[:, :])
                last.then_inc(S["tk_ps"], 1)
            pe.wait_ge(S["acs_sb"], 1)
            for b in range(NB):
                last = pe.transpose(ps[6][0:32, b * CH:(b + 1) * CH], sd("acs")[:, 32 * b:32 * b + 32], ident[:, :])
            last.then_inc(S["acr_ps"], 1)
            mm(ps[7][:, 0:P], ident[:, P - 1:P].to_broadcast([P, P]), sd("acs"), start=True, stop=True).then_inc(S["acl_ps"], 1)
            for g in range(SSD_G):
                if g >= 2:
                    pe.wait_ge(S["cb_sb"], g - 1)
                for b in range(NB):
                    tok = chunk(b)
                    last = mm(ps[2 + g % 2][:, tok], mid[:, B0 + g, tok], mid[:, C0 + g, tok], start=True, stop=True)
                last.then_inc(S["cb_ps"], 1)
            pe.wait_ge(S["acr_sb"], 1)
            pe.wait_ge(S["acl_a"], 2)
            pe.wait_ge(S["cb_sb"], SSD_G)
            pe.wait_ge(S["tk_sb"], 20)

            def ssd_L(h):
                if h >= 2:
                    pe.wait_ge(S["L_sb"], h - 1)
                mm(ps[h % 2][:, :], ident[0:32, h:h + 1].to_broadcast([32, P]), acrow, start=True, stop=False)
                mm(ps[h % 2][:, :], ident_b[:, :], neg_b[:, :].unsqueeze(1).to_broadcast([P, NB, P]), start=False, stop=True
                   ).then_inc(S["L_ps"], 1)

            def ssd_E(j):
                if j:
                    pe.wait_ge(S["E_sb"], j)
                for par in range(2):
                    last = mm(ps[2][64 * par:64 * par + 64, CH:SEQ], ident[0:SSD_H, 2 * j + par:2 * j + par + 1].to_broadcast([SSD_H, 64]),
                              acrow[:, CH:SEQ], start=True, stop=True)
                last.then_inc(S["E_ps"], 1)

            def ssd_states(g):
                for b in range(NB - 1):
                    q = 3 * g + b
                    pe.wait_ge(S["xde"], q + 1)
                    if q:
                        pe.wait_ge(S["st_up"], q)
                    mm(ps[3][:, :], mid[:, MIDS - 4 + b, g * P:(g + 1) * P], xde_at(q), start=True, stop=True
                       ).then_inc(S["st_ps"], 1)

            def ssd_y(j):
                g = j // 4
                if j:
                    pe.wait_ge(S["y_done"], j)
                for par in range(2):
                    h = 2 * j + par
                    pe.wait_ge(S["G_sb"], h + 1)
                    for b in range(NB):
                        tok = chunk(b)
                        last = mm(ps[4][64 * par:64 * par + 64, tok], h_f[:, 4 * b + h // 8, (h % 8) * 64:(h % 8) * 64 + 64],
                                  gate_s[:, h % 2, tok], start=True, stop=True)
                    last.then_inc(S["yd_ps"], 1)
                pe.wait_ge(S["st_up"], 3 * g + 3)
                for b in range(1, NB):
                    tok = chunk(b)
                    last = mm(ps[5][:, tok], hst(b)[:, (j % 4) * P:(j % 4 + 1) * P], mid[:, C0 + g, tok], start=True, stop=True)
                last.then_inc(S["yo_ps"], 1)
            ssd_L(0)
            ssd_L(1)
            ssd_E(0)
            for j in range(SSD_XT):
                if j % 4 == 0:
                    ssd_states(j // 4)
                if j + 1 < SSD_XT:
                    ssd_L(2 * j + 2)
                    ssd_L(2 * j + 3)
                    ssd_E(j + 1)
                ssd_y(j)
            for g in range(SSD_G):
                for t in range(4):
                    q = 4 * g + t
                    pe.wait_ge(S["ysq"], q + 1)
                    if t == 0 and g >= 2:
                        pe.wait_ge(S["yln"], g - 1)
                    mm(ps[6 + g % 2][:, :], ones[:, :], sq[:, q % 2, :], start=t == 0, stop=t == 3).then_inc(S["ysum"], 1)
            u0 = PHASES["od_out"][0]
            for m in range(KT):
                pe.wait_ge(x_ready, x_at(5, m) - 2)
                for w in range(2):
                    uu = u0 + 2 * m + w
                    split_ready(uu, 0)
                    for k in range(8):
                        kk = 8 * w + k
                        if m == 0:
                            pe.wait_ge(S["ylo"], kk + 1)
                        last = passes(ps[4 + m % 2][:, :], uu, k, mid_hi[:, kk, :], mid_lo[:, kk, :], kk == 0, kk == 15)
                    last.then_inc(unit_done, 1)
            norm_sum(5)
            ffn_up(3)
            ffn_down(3)
            norm_sum(6)

        @block.scalar
        def _(act):
            fn = act.activation
            step = Tally(act_step)
            for d, a in ((vec[:, :], src["vec"]), (ident[:, :], src["ident"]), (ones[:, :], src["ones"]),
                         (tri[:, :], src["tri"]), (rot[:, :], src["rot"]), (qmask[:, :], src["qmask"]),
                         (tmp[:, 0, 0:P], src["neg"]), (tmp[:, 0, P:2 * P], src["pos_mask"]),
                         (lvl_in, src["lvl"])):
                act.dma_start(d, a).then_inc(const_in, 16)
            act.dma_start(pos[:, :], src["positions"].to_broadcast([P, SEQ])).then_inc(const_in, 16)
            for kt in range(KT):
                act.dma_start(x[:, kt, :], src["x"][kt]).then_inc(x_in, 16)
            act.wait_ge(const_in, 16 * 10)
            fn(cact[:, :], vec[:, VEC["c"]:VEC["c"] + KT], ACT.Silu).then_inc(cact_done, 1)
            act.wait_ge(x_in, 16 * KT)

            def squares(n, m, dm):
                act.wait_ge(x_ready, x_at(n, m) + dm)
                act.wait_ge(ss_add, KT * n + m + 1 + dm)
                fn(sq[:, m % 2, :], x[:, bass.ds(m + dm, 1), :].rearrange("p a n -> p (a n)"), ACT.Square
                   ).then_inc(sq_done, 1)

            def inv_root(dst, bank, n_mean, read, ready, count):
                fn(dst, bank, ACT.Ln, bias=epsc[:, 0:1], scale=1.0 / n_mean).then_inc(read, 1)
                act.wait_ge(read, count)
                fn(dst, dst, ACT.Exp, scale=-0.5).then_inc(ready, 1)

            def norm(n):
                act.wait_ge(ss_sum, n + 1)
                inv_root(rstd[:, :], ps[7][:, :], D, ln_ready, rstd_ready, n + 1)
                if n < 6:
                    for kt in range(KT):
                        act.wait_ge(ht_ready, KT * n + kt + 1)
                        fn(h_hi[:, kt, :], tmp[:, kt % 2, :], ACT.Identity,
                           bias=mod[:, 24 * n + kt:24 * n + kt + 1]).then_inc(hhi_done, 1)

            def weight_hi(name, j, di=0):
                u0, n, nk = PHASES[name]
                s = (u0 + j) % RAW
                act.wait_ge(raw_full[s], ((u0 + j) // RAW + 1) * 16 + di * (16 // RAW))
                act.wait_ge(unit_done, u0 + j + di + 1)
                act.copy(whi[:, (u0 + j) % HL, 0:nk * P], raw[:, s, 0:nk * P]).then_inc(act_hi, 1)

            def ffn_up(f):
                name = f"up{f}"
                u0, n, nk = PHASES[name]
                q0 = FT * f

                def body(i, ahead):
                    for t in range(2):
                        ahead(i, t, 0)
                        act.wait_ge(unit_done, used(u0 + 2 * t) + i * 4)
                        act.wait_ge(prod_done, q0 + t + 1 + i * 2)
                        fn(gate_s[:, t, :], ps[2 * t][:, :], ACT.Silu).then_inc(silu_done, 1)
                        ahead(i, t, 1)
                        act.wait_ge(prod_done, q0 + t + 3 + i * 2)
                        act.copy(one(mid_hi[:, bass.ds(i * 2 + t, 1), :]), tmp[:, t, :]).then_inc(midhi_done, 1)
                with act.Fori(0, n // 4 - 1) as i:
                    body(i, lambda i, t, w: weight_hi(name, 2 * t + w + 2, i * 4))
                last = n // 4 - 1
                body(last, lambda i, t, w: weight_hi(name, n - 2 + w) if t == 0 else weight_hi(f"down{f}", w))

            def first_hi(following, w):
                if following:
                    weight_hi(following, w)

            def ffn_down(f, nv, following):
                name = f"down{f}"
                with act.Fori(0, KT // 2 - 1) as i:
                    for t in range(2):
                        weight_hi(name, 2 * t + 2, i * 4)
                        weight_hi(name, 2 * t + 3, i * 4)
                        squares(nv, t, i * 2)
                weight_hi(name, 14)
                weight_hi(name, 15)
                squares(nv, KT - 2, 0)
                first_hi(following, 0)
                squares(nv, KT - 1, 0)
                first_hi(following, 1)

            for m in range(KT):
                squares(0, m, 0)
            first_hi("up0", 0)
            first_hi("up0", 1)
            norm(0)
            ffn_up(0)
            ffn_down(0, 1, None)
            norm(1)
            with act.Fori(0, 4) as i:
                for j in range(4):
                    t = mid[:, bass.ds(i * 4 + j, 1), :].rearrange("p a n -> p (a n)")
                    act.wait_ge(S["evin_free"], 4 + j + 1 + i * 4)
                    fn(t, t, ACT.Silu).then_inc(S["evsilu"], 1)
            for t in range(9):
                if t < 8:
                    act.wait_ge(S["evsilu"], t + 1)
                    if t >= 2:
                        act.wait_ge(S["l2sum"], t - 1)
                    fn(sq[:, t % 2, :], mid[:, t, :], ACT.Square).then_inc(S["l2sq"], 1)
                if t >= 1:
                    r = t - 1
                    act.wait_ge(S["l2sum"], r + 1)
                    if r >= 2:
                        act.wait_ge(S["l2done"], r - 1)
                    fn(tmp[:, r % 2, :], ps[4 + r % 2][:, :], ACT.Ln, bias=epsc[:, 0:1]).then_inc(S["l2ln"], 1)
                    act.wait_ge(S["l2ln"], r + 1)
                    fn(tmp[:, r % 2, :], tmp[:, r % 2, :], ACT.Exp, scale=-0.5,
                       bias=epsc[:, 1:2] if r < HEADS else epsc[:, 2:3]).then_inc(S["l2r"], 1)
            act.wait_ge(S["evin_free"], 4 + EV_TILES)
            act.wait_ge(S["l2sum"], 8)
            for a, nt in enumerate((3, 2)):
                for t in range(nt):
                    q = 3 * a + t
                    if q >= 2:
                        act.wait_ge(S["rsum"], q - 1)
                    fn(sq[:, q % 2, :], mid[:, CQ0 + q, :], ACT.Square).then_inc(S["rsq"], 1)
                act.wait_ge(S["rsum"], 3 * a + nt)
                inv_root((rstd, ssacc)[a][:, :], ps[6][:, :], MLA_RANKS[a], S["rln"], S["rr"], a + 1)
            for q in range(5):
                act.wait_ge(S["rt"], q + 1)
                act.copy(h_hi[:, q, :], tmp[:, q % 2, :]).then_inc(S["rhi"], 1)
            act.wait_ge(S["ba_e"], 1)
            baT = small[:, 9, 0:32].rearrange("p (b n) -> p b n", n=8)
            fn(gd("t1").rearrange("p (b n) -> p b n", n=4), baT[:, :, 0:4], ACT.Exp, scale=-1.0).then_inc(S["gate_a"], 1)
            fn(gd("t2"), gd("t0"), ACT.Exp, scale=-1.0).then_inc(S["gate_a"], 1)
            fn(cols[:, 0:4], vec[:, VEC["g_alog"]:VEC["g_alog"] + 4], ACT.Exp).then_inc(S["gate_a"], 1)
            act.wait_ge(S["gcols"], 1)
            fn(gd("ke"), gd("t0"), ACT.Exp).then_inc(S["gate_a"], 1)
            fn(gd("egl"), gd("glast"), ACT.Exp).then_inc(S["gate_a"], 1)
            fn(gd("eg"), gd("gc"), ACT.Exp).then_inc(S["gate_a"], 1)
            act.wait_ge(S["gate_a"], 6)
            for h in range(HEADS):
                act.wait_ge(S["hd_ps"], 2 * h + 1)
                if h >= 2:
                    act.wait_ge(S["hd_free"], 4 * (h - 1))
                for b in range(NB):
                    c = 4 * b + h
                    last = fn(sq[:, h % 2, chunk(b)], ps[0][:, chunk(b)], ACT.Exp, scale=-1.0, bias=gd("gc")[:, c:c + 1])
                last.then_inc(S["hd_exp"], 1)
                for b in range(NB):
                    c = 4 * b + h
                    last = fn(gate_s[:, h % 2, chunk(b)], ps[1][:, chunk(b)], ACT.Exp, bias=gd("ngc")[:, c:c + 1])
                last.then_inc(S["hd_exp"], 1)
                fn(tmp[:, h % 2, :], ps[2][:, :], ACT.Exp).then_inc(S["hd_exp"], 1)
            for q in range(NQ):
                act.wait_ge(S["y_ps"], q + 1)
                act.copy(h_f[:, 8 + q % HEADS, :], ps[q % 2][:, :]).then_inc(S["y_sb"], 1)
            for b in range(NB):
                act.wait_ge(S["vn_ps"], b + 1)
                if b:
                    act.wait_ge(S["o_ps"], b)
                act.copy(tmp[:, 1, :], ps[1][:, :]).then_inc(S["vn_sb"], 1)
                act.wait_ge(S["o_ps"], b + 1)
                act.copy(mid[:, V0:V0 + HEADS, chunk(b)], ps[3][:, :].rearrange("p (h n) -> p h n", h=HEADS)
                         ).then_inc(S["o_sb"], 1)
            act.wait_ge(S["o_sb"], NB)
            for h in range(HEADS + 1):
                if h < HEADS:
                    if h >= 2:
                        act.wait_ge(S["osum"], h - 1)
                    fn(sq[:, h % 2, :], mid[:, V0 + h, :], ACT.Square).then_inc(S["osq"], 1)
                    act.wait_ge(S["osum"], h + 1)
                    if h >= 2:
                        act.wait_ge(S["ot"], h - 1)
                    inv_root(gate_s[:, h % 2, :], ps[4 + h % 2][:, :], P, S["oln"], S["orr"], h + 1)
                if h >= 1:
                    act.wait_ge(S["ot"], h)
                    act.copy(h_hi[:, h - 1, :], tmp[:, (h - 1) % 2, :]).then_inc(S["ohi"], 1)
            for a in range(2):
                act.wait_ge(S["trig_d"], a + 1)
                fn(mid[:, 4 + a, :], mid[:, 2 + a, :], ACT.Sin).then_inc(S["trig_a"], 1)
            scale = float((128 + 64) ** -0.5)
            for q in range(len(att_seq) + 1):
                if q < len(att_seq):
                    h, b = att_seq[q]
                    nk = (b + 1) * CH
                    act.wait_ge(S["sc_mask"], q + 1)
                    if q >= 2:
                        act.wait_ge(S["pt_ps"], q - 1)
                    fn(mid[:, q % 2, 0:nk], ps[q % 2][:, 0:nk], ACT.Exp, bias=cols[:, 6 + q % 2:7 + q % 2],
                       scale=scale, accum_out=cols[:, 8 + q % 2:9 + q % 2]).then_inc(S["sc_exp"], 1)
                if q >= 1:
                    r = q - 1
                    h, b = att_seq[r]
                    nk = (b + 1) * CH
                    act.wait_ge(S["pt_ps"], r + 1)
                    if r >= 2:
                        act.wait_ge(S["av_ps"], r - 1)
                    act.copy(mid[:, 2 + r % 2, 0:nk], ps[2 + r % 2][:, 0:nk]).then_inc(S["pt_sb"], 1)
                    if b == NB - 1:
                        act.wait_ge(S["av_ps"], NB * (h + 1))
                        act.copy(h_hi[:, 4 + h, :], ps[4 + h % 2][:, :]).then_inc(S["av_hi"], 1)
            for m in range(KT):
                if m == KT - 1:
                    first_hi("up1", 0)
                squares(2, m, 0)
            first_hi("up1", 1)
            norm(2)
            ffn_up(1)
            ffn_down(1, 3, "up2")
            norm(3)
            ffn_up(2)
            ffn_down(2, 4, None)
            norm(4)
            with act.Fori(0, 10) as i:
                for j in range(4):
                    t = mid[:, bass.ds(i * 4 + j, 1), :].rearrange("p a n -> p (a n)")
                    act.wait_ge(S["odin_free"], 4 + j + 1 + i * 4)
                    fn(t, t, ACT.Silu).then_inc(S["odsilu"], 1)
            act.wait_ge(S["dt_e"], 1)
            fn(sd("t2"), sd("t1"), ACT.Exp, scale=-1.0).then_inc(S["dt_a"], 1)
            fn(sd("t3")[:, 0:SSD_H], vec[:, VEC["s_alog"]:VEC["s_alog"] + SSD_H], ACT.Exp).then_inc(S["dt_a"], 1)
            act.wait_ge(S["acl_d"], 1)
            fn(sd("de"), sd("t1"), ACT.Exp).then_inc(S["acl_a"], 1)
            fn(sd("cd"), sd("t0"), ACT.Exp).then_inc(S["acl_a"], 1)
            for g in range(SSD_G):
                act.wait_ge(S["cb_ps"], g + 1)
                act.copy(mid[:, B0 + g, :], ps[2 + g % 2][:, :]).then_inc(S["cb_sb"], 1)

            def ssd_L(h):
                act.wait_ge(S["L_ps"], h + 1)
                if h >= 2:
                    act.wait_ge(S["G_sb"], h - 1)
                for b in range(NB):
                    c = SSD_H * b + h
                    last = fn(tmp[:, h % 2, chunk(b)], ps[h % 2][:, chunk(b)], ACT.Exp, bias=sd("nacs")[:, c:c + 1])
                last.then_inc(S["L_sb"], 1)

            def ssd_E(j):
                act.wait_ge(S["E_ps"], j + 1)
                if j:
                    act.wait_ge(S["y_done"], j)
                fn(sq[:, 0, CH:SEQ], ps[2][:, CH:SEQ], ACT.Exp).then_inc(S["E_sb"], 1)
            ssd_L(0)
            ssd_L(1)
            ssd_E(0)
            for j in range(1, SSD_XT):
                ssd_L(2 * j)
                ssd_L(2 * j + 1)
                ssd_E(j)
            act.wait_ge(S["y_done"], SSD_XT)
            for g in range(SSD_G + 1):
                if g < SSD_G:
                    for t in range(4):
                        q = 4 * g + t
                        if q >= 2:
                            act.wait_ge(S["ysum"], q - 1)
                        fn(sq[:, q % 2, :], mid[:, q, :], ACT.Square).then_inc(S["ysq"], 1)
                    act.wait_ge(S["ysum"], 4 * g + 4)
                    if g >= 2:
                        act.wait_ge(S["yt"], 4 * (g - 1))
                    inv_root(gate_s[:, g % 2, :], ps[6 + g % 2][:, :], 4 * P, S["yln"], S["yrr"], g + 1)
                if g >= 1:
                    for q in range(4 * g - 4, 4 * g):
                        act.wait_ge(S["yt"], q + 1)
                        act.copy(mid_hi[:, q, :], tmp[:, q % 2, :]).then_inc(S["yhi"], 1)
            for m in range(KT):
                if m == KT - 1:
                    first_hi("up3", 0)
                squares(5, m, 0)
            first_hi("up3", 1)
            norm(5)
            ffn_up(3)
            ffn_down(3, 6, None)
            norm(6)

        @block.vector
        def _(dve):
            tt, ts, stt = dve.tensor_tensor, dve.tensor_scalar, dve.scalar_tensor_tensor
            step = Tally(dve_step)

            def own(ins):
                step.inc(ins)
                dve.wait_ge(step.sem, step.n)

            for sm, k in ((x_ready, KT), (ada_done, 2), (ss_add, 2), (prod_done, 2), (S["evin_free"], 4),
                          (S["odin_free"], 4)):
                dve.sem_inc(sm, k)
            dve.memset(epsc[:, 0:1], EPS)
            dve.memset(epsc[:, 1:2], float(-0.5 * np.log(128.0)))
            dve.memset(epsc[:, 2:3], 0.0)
            dve.wait_ge(const_in, 16 * 10)
            dve.tensor_copy(ident_b[:, :], ident[:, :])
            dve.tensor_copy(neg_b[:, :], tmp[:, 0, 0:P])
            dve.tensor_copy(pos_b[:, :], tmp[:, 0, P:2 * P])
            dve.tensor_copy(lvl[:, :, :].rearrange("p a n -> p (a n)"), lvl_in)
            own(dve.memset(ssacc[:, :], 0.0))
            dve.sem_inc(consts, 1)

            def add_square(n, m, dm):
                dve.wait_ge(sq_done, KT * n + m + 1 + dm)
                dve.wait_ge(ss_add, KT * n + m + 2 + dm)
                tt(ssacc[:, :], ssacc[:, :], sq[:, m % 2, :], ALU.add).then_inc(ss_add, 1)

            def ada_group(g0, gi):
                s = g0 % 2
                dve.wait_ge(ada_full[s], 16 * (g0 // 2 + 1) + gi * 8)
                dve.wait_ge(mod_sum, g0 + 1 + gi)
                acc = ada_acc[:, s, :]
                own(ts(acc, ada_sb[:, s, 0, :], cact[:, 0:1], None, ALU.mult))
                for k in range(1, KT):
                    ins = stt(out=acc, in0=ada_sb[:, s, k, :], scalar=cact[:, k:k + 1], in1=acc, op0=ALU.mult, op1=ALU.add)
                    if k < KT - 1:
                        own(ins)
                ins.then_inc(ada_done, 1)

            def take_mod(s, last):
                dve.wait_ge(mod_sum, ADA_G * (last + 1) + 2)
                c = slice(24 * s, 24 * s + 24)
                b0 = VEC["ada_b"] + 24 * s
                own(tt(mod[:, c], ps[6][:, c], vec[:, b0:b0 + 24], ALU.add))
                g0 = VEC["norm_g"] + KT * s
                own(stt(out=moda[:, KT * s:KT * s + KT], in0=mod[:, 24 * s + 8:24 * s + 16], scalar=1.0,
                        in1=vec[:, g0:g0 + KT], op0=ALU.add, op1=ALU.mult))
                if s not in (1, 4):
                    g = mod[:, 24 * s + 16:24 * s + 24]
                    own(ts(g, g, 0.5, None, ALU.mult))

            def residual(nv, bank, m, dm):
                xm = one(x[:, bass.ds(m + dm, 1), :])
                g0 = 24 * (nv - 1) + 16 + m
                stt(out=xm, in0=bank, scalar=mod[:, bass.ds(g0 + dm, 1)], in1=xm, op0=ALU.mult, op1=ALU.add
                    ).then_inc(x_ready, 1)

            def norm(n):
                dve.wait_ge(rstd_ready, n + 1)
                if n == 6:
                    for kt in range(KT):
                        stt(out=mid[:, kt, :], in0=x[:, kt, :], scalar=vcol("final_g", kt), in1=rstd[:, :],
                            op0=ALU.mult, op1=ALU.mult).then_inc(out_ready, 1)
                    return

                def low(kt):
                    dve.wait_ge(hhi_done, KT * n + kt + 1)
                    stt(out=h_lo[:, kt, :], in0=tmp[:, kt % 2, :], scalar=mod[:, 24 * n + kt:24 * n + kt + 1],
                        in1=h_hi[:, kt, :].bitcast(F32), op0=ALU.add, op1=ALU.subtract).then_inc(hlo_done, 1)
                for kt in range(KT):
                    if kt >= 2:
                        low(kt - 2)
                        dve.wait_ge(hlo_done, KT * n + kt - 1)
                    stt(out=tmp[:, kt % 2, :], in0=x[:, kt, :], scalar=moda[:, KT * n + kt:KT * n + kt + 1], in1=rstd[:, :],
                        op0=ALU.mult, op1=ALU.mult).then_inc(ht_ready, 1)
                low(KT - 2)
                low(KT - 1)

            def ffn_up(f):
                u0, n, nk = PHASES[f"up{f}"]
                q0 = FT * f
                with dve.Fori(0, n // 4) as i:
                    for t in range(2):
                        dve.wait_ge(silu_done, q0 + t + 1 + i * 2)
                        dve.wait_ge(unit_done, used(u0 + 2 * t + 1) + i * 4)
                        tt(tmp[:, t, :], gate_s[:, t, :], ps[2 * t + 1][:, :], ALU.mult).then_inc(prod_done, 1)
                        dve.wait_ge(midhi_done, q0 + t + 1 + i * 2)
                        k = bass.ds(i * 2 + t, 1)
                        tt(one(mid_lo[:, k, :]), tmp[:, t, :], one(mid_hi[:, k, :]).bitcast(F32), ALU.subtract
                           ).then_inc(midlo_done, 1)
                        dve.wait_ge(midlo_done, q0 + t + 1 + i * 2)

            def ffn_down(f):
                name = f"down{f}"
                u0 = PHASES[name][0]
                nv = {0: 1, 1: 3, 2: 4, 3: 6}[f]
                dve.wait_ge(ss_sum, nv)
                own(dve.memset(ssacc[:, :], 0.0))
                g0, per = ADA_AT.get(name, (0, 0))
                with dve.Fori(0, KT // 2) as i:
                    step.enter(i, per * (KT - 1))
                    for t in range(2):
                        for q in range(per // 2):
                            ada_group(g0 + t * (per // 2) + q, i * per)
                        dve.wait_ge(unit_done, used(u0 + 2 * t + 1) + i * 4)
                        residual(nv, ps[4 + t][:, :], t, i * 2)
                        add_square(nv, t, i * 2)
                    step.leave(KT // 2)
                made = {"down0": (1, 2), "down1": (3,), "down2": (4, 5)}.get(name, ())
                for s in made:
                    take_mod(s, made[-1])

            def conv(bank, t, tile, w, n_tiles, bias):
                def tap(j):
                    return vec[:, bass.ds(VEC[w] + j * n_tiles + tile, 1)]
                own(ts(t, bank, tap(3), None if bias is None else vec[:, bass.ds(VEC[bias] + tile, 1)],
                       ALU.mult, ALU.add) if bias is not None else ts(t, bank, tap(3), None, ALU.mult))
                for j in (2, 1, 0):
                    d = 3 - j
                    ins = stt(out=t[:, d:SEQ], in0=bank[:, 0:SEQ - d], scalar=tap(j), in1=t[:, d:SEQ],
                              op0=ALU.mult, op1=ALU.add)
                    if j:
                        own(ins)
                return ins

            def softplus(dst, z, u, a, b, c, m):
                own(ts(a, u, 2.0, None, ALU.add))
                own(dve.reciprocal(b, a))
                own(tt(a, u, b, ALU.mult))
                own(tt(b, a, a, ALU.mult))
                own(ts(c, b, 1.0 / 15, None, ALU.mult))
                for k in (13, 11, 9, 7, 5, 3):
                    own(stt(out=c, in0=c, scalar=1.0 / k, in1=b, op0=ALU.add, op1=ALU.mult))
                own(stt(out=c, in0=c, scalar=1.0, in1=a, op0=ALU.add, op1=ALU.mult))
                own(ts(m, z, 0.0, None, ALU.max))
                own(stt(out=dst, in0=c, scalar=2.0, in1=m, op0=ALU.mult, op1=ALU.add))

            for m in range(KT):
                add_square(0, m, 0)
            dve.wait_ge(cact_done, 1)
            for g in range(ADA_G):
                ada_group(g, 0)
            take_mod(0, 0)
            norm(0)
            ffn_up(0)
            ffn_down(0)
            norm(1)
            u0 = PHASES["ev_in"][0]
            with dve.Fori(0, 3) as i:
                step.enter(i, 12)
                for j in range(4):
                    dve.wait_ge(unit_done, used(u0 + j) + i * 4)
                    conv(ps[j][:, :], one(mid[:, bass.ds(i * 4 + j, 1), :]), i * 4 + j, "gconv", GDN_TILES, None
                         ).then_inc(S["evin_free"], 1)
                step.leave(3)
            for j in range(GDN_TILES, EV_TILES):
                dve.wait_ge(unit_done, used(u0 + j))
                if j < 16:
                    dst = mid[:, j, :]
                elif j == 16:
                    dst = rows
                elif j < 22:
                    dst = mid[:, CQ0 + j - 17, :]
                else:
                    dst = mid[:, KPE, :]
                dve.tensor_copy(dst, ps[j % 4][:, :]).then_inc(S["evin_free"], 1)
            for t in range(8):
                dve.wait_ge(S["l2r"], t + 1)
                tt(mid[:, t, :], mid[:, t, :], tmp[:, t % 2, :], ALU.mult).then_inc(S["l2done"], 1)

            def latent_low(q):
                dve.wait_ge(S["rhi"], q + 1)
                tt(h_lo[:, q, :], tmp[:, q % 2, :], h_hi[:, q, :].bitcast(F32), ALU.subtract).then_inc(S["rlo"], 1)
            dve.wait_ge(S["l2done"], 8)
            for q in range(5):
                dve.wait_ge(S["rr"], 1 if q < 3 else 2)
                if q >= 2:
                    latent_low(q - 2)
                    dve.wait_ge(S["rlo"], q - 1)
                gain = vcol("q_g", q) if q < 3 else vcol("kv_g", q - 3)
                stt(out=tmp[:, q % 2, :], in0=mid[:, CQ0 + q, :], scalar=gain, in1=(rstd if q < 3 else ssacc)[:, :],
                    op0=ALU.mult, op1=ALU.mult).then_inc(S["rt"], 1)
            latent_low(3)
            latent_low(4)
            dve.wait_ge(S["ba_t"], 1)
            baT = small[:, 9, 0:32]
            own(dve.tensor_copy(baT, ps[7][:, 0:32]))
            baT = baT.rearrange("p (b n) -> p b n", n=8)

            def g4(ap):
                return ap.rearrange("p (b n) -> p b n", n=HEADS)

            def per_head(ap, n=HEADS):
                return ap.unsqueeze(1).to_broadcast([P, NB, n])
            own(tt(g4(gd("z")), baT[:, :, 4:8], per_head(vec[:, VEC["g_dtb"]:VEC["g_dtb"] + 4]), ALU.add))
            stt(out=gd("t0"), in0=gd("z"), scalar=-1.0, in1=gd("z"), op0=ALU.mult, op1=ALU.max).then_inc(S["ba_e"], 1)
            dve.wait_ge(S["gate_a"], 3)
            own(ts(gd("t1"), gd("t1"), 1.0, None, ALU.add))
            own(dve.reciprocal(gd("beta"), gd("t1")))
            softplus(gd("t3"), gd("z"), gd("t2"), gd("t1"), gd("t4"), gd("t5"), gd("t0"))
            stt(out=g4(gd("g")), in0=g4(gd("t3")), scalar=-1.0, in1=per_head(cols[:, 0:4]), op0=ALU.mult, op1=ALU.mult
                ).then_inc(S["g_done"], 1)
            for t in range(14):
                sm, v = pj_ready(t)
                dve.wait_ge(sm, v)
                dve.tensor_copy(mid[:, QN0 + t, :], ps[t % 4][:, :]).then_inc(S["pj_free"], 1)
            dve.wait_ge(S["gc_ps"], 1)
            dve.tensor_copy(gd("gc"), ps[4][:, 0:16]).then_inc(S["gc_sb"], 1)
            dve.wait_ge(S["gcrow_ps"], 1)
            dve.tensor_copy(gcrow, ps[5][0:HEADS, :]).then_inc(S["gcrow_sb"], 1)
            dve.wait_ge(S["glast_ps"], 1)
            dve.wait_ge(S["gc_sb"], 1)
            own(dve.tensor_copy(gd("glast"), ps[6][:, 0:16]))
            own(tt(gd("t0"), gd("glast"), gd("gc"), ALU.subtract))
            own(ts(gd("nbeta"), gd("beta"), -1.0, None, ALU.mult))
            ts(gd("ngc"), gd("gc"), -1.0, None, ALU.mult).then_inc(S["gcols"], 1)
            dve.wait_ge(S["gate_a"], 6)
            own(tt(gd("nbe"), gd("nbeta"), gd("eg"), ALU.mult))
            for h in range(HEADS):
                dve.wait_ge(S["hd_ps"], 2 * h + 2)
                dve.wait_ge(S["hd_exp"], 3 * h + 1)
                for b in range(NB):
                    c = 4 * b + h
                    last = stt(out=h_f[:, h, chunk(b)], in0=ps[3][:, chunk(b)], scalar=gd("nbeta")[:, c:c + 1],
                               in1=sq[:, h % 2, chunk(b)], op0=ALU.mult, op1=ALU.mult)
                last.then_inc(S["hd_free"], 1)
                dve.wait_ge(S["hd_exp"], 3 * h + 3)
                tt(mid[:, AT0 + h, :], ps[4][:, :], gate_s[:, h % 2, :], ALU.mult).then_inc(S["hd_free"], 1)
                tt(mid[:, Q0 + h, :], mid[:, Q0 + h, :], tmp[:, h % 2, :], ALU.mult)
                for b in range(NB):
                    c = 4 * b + h
                    last = ts(h_f[:, 12 + h, chunk(b)], ps[5][:, chunk(b)], gd("ke")[:, c:c + 1], None, ALU.mult)
                last.then_inc(S["hd_free"], 1)
                for b in range(NB):
                    c = 4 * b + h
                    last = ts(mid[:, VB0 + h, chunk(b)], ps[6][:, chunk(b)], gd("beta")[:, c:c + 1], None, ALU.mult)
                last.then_inc(S["hd_free"], 1)
            idb = ident[:, :].unsqueeze(1).to_broadcast([P, NB, P])

            def blocks(ap):
                return ap.rearrange("p (b n) -> p b n", b=NB)
            for h in range(HEADS):
                own(dve.tensor_copy(blocks(h_f[:, 4 + h, :]), idb))
                dve.tensor_copy(blocks(mid[:, MT0 + h, :]), idb).then_inc(S["inv_up"], 1)
            for q in range(NQ):
                lv, h = inv_seq[q]
                dve.wait_ge(S["z_ps"], q + 1)
                dve.wait_ge(S["inv_up"], q + 1)
                if lv < len(LEVELS) - 1:
                    m = lvl[:, 2 * lv:2 * lv + 1, :].to_broadcast([P, NB, P])
                    own(dve.copy_predicated(blocks(h_f[:, 4 + h, :]), m, blocks(ps[2 + q % 2][:, :])))
                m = lvl[:, 2 * lv + 1:2 * lv + 2, :].to_broadcast([P, NB, P])
                dve.copy_predicated(blocks(mid[:, MT0 + h, :]), m, blocks(ps[4 + q % 2][:, :])).then_inc(S["inv_up"], 1)
            for b in range(NB):
                if b:
                    dve.wait_ge(S["ks_ps"], b)
                    dve.wait_ge(S["vn_ps"], b)
                else:
                    dve.wait_ge(S["hd_free"], 4 * HEADS)
                for h in range(HEADS):
                    hc = slice(h * P, (h + 1) * P)
                    c = 4 * b + h
                    if b:
                        last = stt(out=tmp[:, 0, hc], in0=ps[0][:, hc], scalar=gd("nbe")[:, c:c + 1],
                                   in1=mid[:, VB0 + h, chunk(b)], op0=ALU.mult, op1=ALU.add)
                    else:
                        last = dve.tensor_copy(tmp[:, 0, hc], mid[:, VB0 + h, chunk(b)])
                last.then_inc(S["r_sb"], 1)
                if b < NB - 1:
                    dve.wait_ge(S["su_ps"], b + 1)
                    dve.wait_ge(S["o_ps"], b + 1)
                    if b:
                        dve.wait_ge(S["s_up"], b)
                    for h in range(HEADS):
                        hc = slice(h * P, (h + 1) * P)
                        c = 4 * b + h
                        if b:
                            last = stt(out=mid[:, ST, hc], in0=mid[:, ST, hc], scalar=gd("egl")[:, c:c + 1],
                                       in1=ps[2][:, hc], op0=ALU.mult, op1=ALU.add)
                        else:
                            last = dve.tensor_copy(mid[:, ST, hc], ps[2][:, hc])
                    last.then_inc(S["s_up"], 1)

            def out_low(h):
                dve.wait_ge(S["ohi"], h + 1)
                tt(h_lo[:, h, :], tmp[:, h % 2, :], h_hi[:, h, :].bitcast(F32), ALU.subtract).then_inc(S["olo"], 1)
            for h in range(HEADS):
                dve.wait_ge(S["orr"], h + 1)
                own(stt(out=tmp[:, h % 2, :], in0=mid[:, V0 + h, :], scalar=vcol("gdn_g"), in1=gate_s[:, h % 2, :],
                        op0=ALU.mult, op1=ALU.mult))
                tt(tmp[:, h % 2, :], tmp[:, h % 2, :], mid[:, Z0 + h, :], ALU.mult).then_inc(S["ot"], 1)
                out_low(h)
                dve.wait_ge(S["olo"], h + 1)
            dve.wait_ge(S["o_ps"], NB)
            ang, k, r = mid[:, 0, :], mid[:, 1, :], None
            own(dve.tensor_copy(ang, pos[:, :]))
            own(ts(ang, ang, vcol("inv_freq"), None, ALU.mult))
            c1 = 6.28125
            c2 = 4059.0 / 2097152
            c3 = 2 * np.pi - c1 - c2
            for a in range(2):
                r = mid[:, 2 + a, :]
                own(ts(k, ang, float(1 / (2 * np.pi)), 0.25 * a, ALU.mult, ALU.add))
                own(ts(k, k, ROUND, None, ALU.add))
                own(ts(k, k, ROUND, None, ALU.subtract))
                own(stt(out=r, in0=k, scalar=-c1, in1=ang, op0=ALU.mult, op1=ALU.add))
                own(stt(out=r, in0=k, scalar=-c2, in1=r, op0=ALU.mult, op1=ALU.add))
                own(stt(out=r, in0=k, scalar=float(-c3), in1=r, op0=ALU.mult, op1=ALU.add))
                own(ts(r, r, float(np.pi / 2) * a, None, ALU.add))
                ts(r, r, PI, -PI, ALU.min, ALU.max).then_inc(S["trig_d"], 1)
            sin, cos = mid[:, 4, :], mid[:, 5, :]
            dve.wait_ge(S["trig_a"], 2)
            for n in range(3):
                t = mid[:, (QPE0, QPE0 + 1, KPE)[n], :]
                dve.wait_ge(S["rot_ps"], n + 1)
                if n:
                    dve.wait_ge(S["rope"], n)
                own(tt(tmp[:, 0, :], ps[n][:, :], sin, ALU.mult))
                own(tt(t, t, cos, ALU.mult))
                tt(t, t, tmp[:, 0, :], ALU.add).then_inc(S["rope"], 1)
            scale = float((128 + 64) ** -0.5)
            for q in range(len(att_seq) + 1):
                if q < len(att_seq):
                    h, b = att_seq[q]
                    nk = (b + 1) * CH
                    dve.wait_ge(S["sc_ps"], q + 1)
                    own(tt(ps[q % 2][:, chunk(b)], ps[q % 2][:, chunk(b)], qmask[:, :], ALU.add))
                    own(dve.tensor_reduce(cols[:, 4 + q % 2:5 + q % 2], ps[q % 2][:, 0:nk], AX_X, ALU.max))
                    ts(cols[:, 6 + q % 2:7 + q % 2], cols[:, 4 + q % 2:5 + q % 2], -scale, None, ALU.mult
                       ).then_inc(S["sc_mask"], 1)
                if q >= 1:
                    r = q - 1
                    h, b = att_seq[r]
                    nk = (b + 1) * CH
                    dve.wait_ge(S["sc_exp"], r + 1)
                    own(dve.reciprocal(cols[:, 10 + r % 2:11 + r % 2], cols[:, 8 + r % 2:9 + r % 2]))
                    ts(mid[:, r % 2, 0:nk], mid[:, r % 2, 0:nk], cols[:, 10 + r % 2:11 + r % 2], None, ALU.mult
                       ).then_inc(S["sc_norm"], 1)
                    if b == NB - 1:
                        dve.wait_ge(S["av_hi"], h + 1)
                        tt(h_lo[:, 4 + h, :], ps[4 + h % 2][:, :], h_hi[:, 4 + h, :].bitcast(F32), ALU.subtract
                           ).then_inc(S["av_lo"], 1)
            u0 = PHASES["ev_out"][0]
            own(dve.memset(ssacc[:, :], 0.0))
            for m in range(KT):
                dve.wait_ge(unit_done, used(u0 + m))
                residual(2, ps[4 + m % 2][:, :], m, 0)
                add_square(2, m, 0)
            norm(2)
            ffn_up(1)
            ffn_down(1)
            norm(3)
            ffn_up(2)
            ffn_down(2)
            norm(4)
            u0 = PHASES["od_in"][0]
            with dve.Fori(0, 6) as i:
                step.enter(i, 12)
                for j in range(4):
                    dve.wait_ge(unit_done, used(u0 + j) + i * 4)
                    conv(ps[j][:, :], one(mid[:, bass.ds(i * 4 + j, 1), :]), i * 4 + j, "sconv", SSD_CONV, "sconv_b"
                         ).then_inc(S["odin_free"], 1)
                step.leave(6)
            with dve.Fori(6, 10) as i:
                for j in range(4):
                    dve.wait_ge(unit_done, used(u0 + j) + i * 4)
                    dve.tensor_copy(one(mid[:, bass.ds(i * 4 + j, 1), :]), ps[j][:, :]).then_inc(S["odin_free"], 1)
            dve.wait_ge(unit_done, used(u0 + 40))
            dve.tensor_copy(rows, ps[0][:, :]).then_inc(S["odin_free"], 1)
            dve.wait_ge(S["dt_t"], 1)

            def s32(ap):
                return ap.rearrange("p (b n) -> p b n", n=SSD_H)
            own(tt(s32(sd("t0")), s32(ps[4][:, 0:P]), per_head(vec[:, VEC["s_dtb"]:VEC["s_dtb"] + SSD_H], SSD_H), ALU.add))
            stt(out=sd("t1"), in0=sd("t0"), scalar=-1.0, in1=sd("t0"), op0=ALU.mult, op1=ALU.max).then_inc(S["dt_e"], 1)
            dve.wait_ge(S["dt_a"], 2)
            softplus(sd("dt"), sd("t0"), sd("t2"), sd("t1"), sd("de"), sd("cd"), sd("acs"))
            stt(out=s32(sd("da")), in0=s32(sd("dt")), scalar=-1.0, in1=per_head(sd("t3")[:, 0:SSD_H], SSD_H),
                op0=ALU.mult, op1=ALU.mult).then_inc(S["da_sb"], 1)
            dve.wait_ge(S["acs_ps"], 1)
            own(dve.tensor_copy(sd("acs"), ps[5][:, 0:P]))
            ts(sd("nacs"), sd("acs"), -1.0, None, ALU.mult).then_inc(S["acs_sb"], 1)

            def heads8(ap):
                return ap.rearrange("p (r n) -> p r n", r=8)

            def by_head(ap):
                return ap.unsqueeze(2).to_broadcast([P, 8, 64])
            for q in range(16):
                b, g = divmod(q, SSD_G)
                dve.wait_ge(S["tk_ps"], q + 1)
                tt(heads8(h_f[:, 4 * b + g, :]), heads8(ps[q % 2][:, :]), by_head(sd("dt")[:, 32 * b + 8 * g:32 * b + 8 * g + 8]),
                   ALU.mult).then_inc(S["tk_sb"], 1)
            for b in range(NB):
                dve.wait_ge(S["tk_ps"], 17 + b)
                dve.tensor_copy(mid[:, MIDS - 4 + b, :], ps[b % 2][:, :]).then_inc(S["tk_sb"], 1)
            dve.wait_ge(S["acr_ps"], 1)
            dve.tensor_copy(acrow, ps[6][0:SSD_H, :]).then_inc(S["acr_sb"], 1)
            dve.wait_ge(S["acl_ps"], 1)
            own(dve.tensor_copy(sd("t0"), ps[7][:, 0:P]))
            tt(sd("t1"), sd("t0"), sd("acs"), ALU.subtract).then_inc(S["acl_d"], 1)
            dve.wait_ge(S["acl_a"], 2)
            dve.wait_ge(S["cb_sb"], SSD_G)

            def ssd_states(g):
                for b in range(NB - 1):
                    q = 3 * g + b
                    c = 32 * b + 8 * g
                    if q >= 2:
                        dve.wait_ge(S["st_ps"], q - 1)
                    tt(heads8(xde_at(q)), heads8(h_f[:, 4 * b + g, :]), by_head(sd("de")[:, c:c + 8]), ALU.mult
                       ).then_inc(S["xde"], 1)
                    dve.wait_ge(S["st_ps"], q + 1)
                    if b:
                        dve.wait_ge(S["st_up"], q)
                        own(tt(heads8(hst(b + 1)), heads8(hst(b)), by_head(sd("cd")[:, c:c + 8]), ALU.mult))
                        tt(hst(b + 1), hst(b + 1), ps[3][:, :], ALU.add).then_inc(S["st_up"], 1)
                    else:
                        dve.tensor_copy(hst(1), ps[3][:, :]).then_inc(S["st_up"], 1)

            def ssd_G(h):
                dve.wait_ge(S["L_sb"], h + 1)
                if h >= 2:
                    dve.wait_ge(S["yd_ps"], h - 1)
                tt(gate_s[:, h % 2, :], tmp[:, h % 2, :], mid[:, B0 + h // 8, :], ALU.mult).then_inc(S["G_sb"], 1)
            for j in range(SSD_XT):
                if j % 4 == 0:
                    ssd_states(j // 4)
                ssd_G(2 * j)
                ssd_G(2 * j + 1)
                dve.wait_ge(S["yo_ps"], j + 1)
                dve.wait_ge(S["E_sb"], j + 1)
                off = slice(CH, SEQ)
                own(tt(sq[:, 1, off], ps[5][:, off], sq[:, 0, off], ALU.mult))
                y = mid[:, j, :]
                own(stt(out=y, in0=y, scalar=vcol("ssd_d", j), in1=ps[4][:, :], op0=ALU.mult, op1=ALU.add))
                own(tt(y[:, off], y[:, off], sq[:, 1, off], ALU.add))
                tt(y, y, mid[:, SZ0 + j, :], ALU.mult).then_inc(S["y_done"], 1)

            def y_low(q):
                dve.wait_ge(S["yhi"], q + 1)
                tt(mid_lo[:, q, :], tmp[:, q % 2, :], mid_hi[:, q, :].bitcast(F32), ALU.subtract).then_inc(S["ylo"], 1)
            dve.wait_ge(S["y_done"], SSD_XT)
            for q in range(16):
                dve.wait_ge(S["yrr"], q // 4 + 1)
                if q >= 2:
                    y_low(q - 2)
                    dve.wait_ge(S["ylo"], q - 1)
                stt(out=tmp[:, q % 2, :], in0=mid[:, q, :], scalar=vcol("ssd_g", q), in1=gate_s[:, (q // 4) % 2, :],
                    op0=ALU.mult, op1=ALU.mult).then_inc(S["yt"], 1)
            y_low(14)
            y_low(15)
            u0 = PHASES["od_out"][0]
            own(dve.memset(ssacc[:, :], 0.0))
            for m in range(KT):
                dve.wait_ge(unit_done, used(u0 + 2 * m + 1))
                residual(5, ps[4 + m % 2][:, :], m, 0)
                add_square(5, m, 0)
            norm(5)
            ffn_up(3)
            ffn_down(3)
            norm(6)


def kernel(**inputs):
    import concourse.bacc as bacc
    from concourse.bass_utils import run_bass_kernel_spmd as run

    def tiles(w):
        k, m = w.shape
        return np.ascontiguousarray(w.reshape(k // P, P, m // P, P).transpose(2, 1, 0, 3)).reshape(m // P, P, k)

    def cols(v):
        return v.reshape(-1, P).T

    def everywhere(v):
        return np.broadcast_to(v.reshape(1, -1), (P, v.size))

    a = {k: np.asarray(v) for k, v in inputs.items()}
    f32 = np.float32
    up, down = [], []
    for l in range(DEPTH):
        for j in range(2):
            up.append(np.stack([tiles(a["ffn_w1"][l, j]), tiles(a["ffn_w3"][l, j])], 1).reshape(2 * FT, P, KT * P))
            down.append(tiles(a["ffn_w2"][l, j]).reshape(KT, P, 2, 11 * P).transpose(0, 2, 1, 3).reshape(16, P, 11 * P))
    w = a["ev_w_in"][0]
    ev_in = np.concatenate([w[:, 0:2048], w[:, 2048:2056], np.zeros((D, P - 8), f32), w[:, 2056:2696],
                            w[:, 2696:2760], w[:, 2696:2760]], 1)
    w = a["mla_w_uq"][0]
    uq = np.concatenate([w[:, :, 0:P].reshape(-1, HEADS * P), w[:, :, P:].reshape(-1, HEADS * 64)], 1)
    uq = tiles(uq).reshape(3, 2, P, 3 * P).transpose(0, 2, 1, 3).reshape(3, P, 6 * P)
    w = a["mla_w_ukv"][0]
    ukv = np.stack([tiles(w[:, :, 0:P].reshape(-1, HEADS * P)).transpose(1, 0, 2).reshape(P, 8 * P),
                    w[:, :, P:].reshape(2, P, HEADS * P).transpose(1, 0, 2).reshape(P, 8 * P)])
    w = a["ssd_w_in"][0]
    od_in = np.concatenate([w[:, 2048:5120], w[:, 0:2048], w[:, 5120:5152], np.zeros((D, P - 32), f32)], 1)
    ada = np.concatenate([a["ada_w"][l].reshape(KT, P, 3 * ADA_G, ADA_COLS).transpose(2, 1, 0, 3).reshape(3 * ADA_G, P, KT * ADA_COLS)
                          for l in range(DEPTH)])
    i = np.arange(P)
    freq = (f32(10000.0) ** (-np.arange(32, dtype=f32) / f32(32))).astype(f32)
    vec = np.concatenate([
        cols(a["c"]), cols(a["ada_b"]), cols(a["norm_g"]), cols(a["final_g"]), cols(a["gdn_conv_w"]), cols(a["gdn_norm_g"]),
        cols(a["mla_q_norm_g"]), cols(a["mla_kv_norm_g"]), cols(a["ssd_conv_w"]), cols(a["ssd_conv_b"]),
        cols(np.repeat(a["ssd_D"][0], 64)), cols(a["ssd_norm_g"]), everywhere(a["gdn_A_log"]), everywhere(a["gdn_dt_bias"]),
        everywhere(a["ssd_A_log"]), everywhere(a["ssd_dt_bias"]), freq[i % 32].reshape(P, 1)], 1)
    assert vec.shape[1] == NVEC
    rot = np.zeros((P, P), f32)
    for m in range(P):
        if m % 64 < 32:
            rot[m + 32, m] = -1.0
        else:
            rot[m - 32, m] = 1.0
    lvl = []
    for s in LEVELS:
        m = ((i[:, None] // s) % 2 == 1) & (i[None, :] // s == i[:, None] // s - 1)
        lvl += [m, m.T]
    arrays = {
        "x": a["x"][0].T.reshape(KT, P, SEQ), "positions": a["positions"].astype(np.int32),
        "ada": ada, "up": np.stack(up), "down": np.stack(down), "ev_in": tiles(ev_in), "uq": uq, "ukv": ukv,
        "ev_out": tiles(a["ev_w_out"][0]), "od_in": tiles(od_in),
        "od_out": tiles(a["ssd_w_out"][0]).reshape(KT, P, 2, 8 * P).transpose(0, 2, 1, 3).reshape(16, P, 8 * P),
        "vec": vec, "ident": np.eye(P, dtype=f32), "ones": np.ones((P, P), f32),
        "tri": np.triu(np.ones((P, P), f32)), "rot": rot,
        "neg": np.where(i[None, :] >= i[:, None], 0.0, BIG_NEG).astype(f32),
        "pos_mask": np.where(i[None, :] < i[:, None], 0.0, -BIG_NEG).astype(f32),
        "qmask": np.where(i[None, :] // 64 <= i[:, None] // 64, 0.0, BIG_NEG).astype(f32),
        "lvl": np.stack(lvl, 1).astype(np.int32).reshape(P, -1),
    }
    nc = bacc.Bacc("TRN2", target_bir_lowering=False, num_devices=1, dynamic_dma_scratch_size=1024)
    arrays = {f"in_{k}": np.ascontiguousarray(v) for k, v in arrays.items()}
    src = {k[3:]: nc.dram_tensor(k, v.shape, mybir.dt.from_np(v.dtype), kind="ExternalInput").ap() for k, v in arrays.items()}
    out = nc.dram_tensor("out", (KT, P, SEQ), F32, kind="ExternalOutput").ap()
    build(nc, src, out, None)
    r = run(nc, [arrays], core_ids=[0])
    return np.ascontiguousarray(r.results[0]["out"].reshape(D, SEQ).T).reshape(1, SEQ, D)
```

```python
from contextlib import ExitStack

import numpy as np

import concourse.bass as bass
from concourse import mybir

F32 = mybir.dt.float32
F32R = mybir.dt.float32r
BF16 = mybir.dt.bfloat16
I32 = mybir.dt.int32
U8 = mybir.dt.uint8
ALU = mybir.AluOpType
ACT = mybir.ActivationFunctionType
AX_X = mybir.AxisListType.X

P = 128
D = 1024
SEQ = 512
DEPTH = 2
D_FF = 2816
EPS = 1e-6
KT = D // P
FT = D_FF // P
CH = 128
NB = SEQ // CH
HEADS = 4
GDN_TILES = 3 * HEADS
EV_FIRST = 1 + 3 + 2 + 1
EV_TILES = EV_FIRST + GDN_TILES + HEADS
MLA_RANKS = (384, 256)
SSD_H = 32
SSD_G = 4
SSD_XT = 16
SSD_CONV = SSD_XT + 2 * SSD_G
OD_TILES = 1 + SSD_CONV + SSD_XT
RAW, HL = 4, 2
BIG_NEG = -3.0e38
LEVELS = [1, 2, 4, 8, 16, 32, 64]
PI = float(np.float32(3.1415925))
ROUND = 12582912.0

PHASES, _u = {}, 0
for _name, _n, _nk in (
        ("up0", 2 * FT, 8), ("down0", 16, 11),
        ("ev_in", EV_TILES, 8), ("uq", 3, 6), ("ukv", 2, 8), ("ev_out", 8, 8),
        ("up1", 2 * FT, 8), ("down1", 16, 11), ("up2", 2 * FT, 8), ("down2", 16, 11),
        ("od_in", OD_TILES, 8), ("od_out", 16, 8),
        ("up3", 2 * FT, 8), ("down3", 16, 11)):
    PHASES[_name] = (_u, _n, _nk)
    _u += _n

HI_AT, _a, _p = {}, 0, 0
for _name, (_u, _n, _nk) in PHASES.items():
    if _name[:2] in ("up", "do"):
        HI_AT[_name] = (_a, None)
        _a += _n
    else:
        HI_AT[_name] = (None, _p)
        _p += _n

ADA_COLS = 384
ADA_G = 3 * D // ADA_COLS
ADA_AT = {"down0": (8, 4), "down1": (24, 2), "down2": (32, 4)}

VEC, _c = {}, 0
for _name, _n in (("c", 8), ("ada_b", 144), ("norm_g", 48), ("final_g", 8), ("gconv", 48), ("gdn_g", 1),
                  ("q_g", 3), ("kv_g", 2), ("sconv", 96), ("sconv_b", 24), ("ssd_d", 16), ("ssd_g", 16),
                  ("g_alog", 4), ("g_dtb", 4), ("s_alog", 32), ("s_dtb", 32), ("inv_freq", 1)):
    VEC[_name] = _c
    _c += _n
NVEC = _c

Q0, K0, V0, Z0, VB0, ST, QN0, QPE0, KN0, VM0, KPE, MT0, AT0 = 0, 4, 8, 12, 16, 20, 21, 25, 27, 31, 35, 36, 40
LAT_HI, CQ0, L2 = 16, 36, 21
B0, C0, SZ0 = 16, 20, 24
MIDS = 44


class Tally:

    def __init__(self, sem, n=0):
        self.sem, self.n, self.k = sem, n, 0

    def inc(self, ins):
        ins.then_inc(self.sem, 1)
        self.n = self.n + 1
        self.k += 1

    def enter(self, i, per):
        self.base, self.per, self.k0 = self.n, per, self.k
        self.n = self.base + i * per

    def leave(self, count):
        assert self.k - self.k0 == self.per, (self.k - self.k0, self.per)
        self.n = self.base + count * self.per


def one(ap):
    return ap.rearrange("p a n -> p (a n)")


def build(nc, src, out, dbg):
    ctx = ExitStack()
    with ctx:
        def sb(name, shape, dt=F32):
            return ctx.enter_context(nc.sbuf_tensor(name, shape, dt))

        def sem(name):
            return ctx.enter_context(nc.semaphore(name))

        with nc.sbuf_tensor("h_f", [P, 16, SEQ], F32) as h_f:
            pass
        with nc.sbuf_tensor("ada_w_sb", [P, 2, KT, ADA_COLS], F32) as ada_sb:
            pass
        h_hi = sb("h_hi", [P, KT, SEQ], F32R)
        h_lo = sb("h_lo", [P, KT, SEQ], F32R)
        with nc.sbuf_tensor("mid_f", [P, MIDS, SEQ], F32) as mid:
            pass
        mid_hi = sb("mid_hi", [P, FT, SEQ], F32R)
        mid_lo = sb("mid_lo", [P, FT, SEQ], F32R)

        x = sb("x_sb", [P, KT, SEQ])
        raw = sb("weight_raw", [P, RAW, 11 * P])
        whi = sb("weight_hi", [P, HL, 11 * P], F32R)
        wlo = sb("weight_lo", [P, HL, 11 * P], F32R)
        ada_acc = sb("ada_acc", [P, 2, ADA_COLS])
        tmp = sb("tmp", [P, 2, SEQ])
        gate_s = sb("gate_s", [P, 2, SEQ])
        sq = sb("sq", [P, 2, SEQ])
        ssacc = sb("ssacc", [P, SEQ])
        rstd = sb("rstd", [P, SEQ])
        vec = sb("vec", [P, NVEC])
        mod = sb("mod", [P, 144])
        moda = sb("moda", [P, 48])
        cact = sb("cact", [P, KT])
        ident = sb("ident", [P, P])
        ones = sb("ones", [P, P])
        tri = sb("tri", [P, P])
        rot = sb("rot", [P, P])
        ident_b = sb("ident_b", [P, P], BF16)
        neg_b = sb("neg_b", [P, P], BF16)
        pos_b = sb("pos_b", [P, P], BF16)
        lvl = sb("lvl", [P, 2 * len(LEVELS), P], U8)
        qmask = sb("qmask", [P, P])
        pos = sb("pos", [P, SEQ], I32)
        small = sb("small", [P, 10, P])
        cols = sb("cols", [P, 16])
        hstate = sb("hstate", [P, NB - 1, SEQ])
        epsc = sb("epsc", [P, 4])
        pick = sb("pick", [96, 32], BF16)
        ps = [ctx.enter_context(nc.psum_tensor(f"bank{i}", [P, SEQ], F32)) for i in range(8)]

        const_in = sem("const_in"); x_in = sem("x_in"); stored = sem("stored"); dbg_out = sem("dbg_out")
        raw_full = [sem(f"raw_full{i}") for i in range(RAW)]
        hi_done = sem("weight_hi_done"); lo_done = sem("weight_lo_done")
        unit_done = sem("unit_done"); act_hi = sem("act_weight_hi")
        ada_full = [sem("ada_full0"), sem("ada_full1")]
        ada_done = sem("ada_acc_done"); mod_sum = sem("mod_summed")
        consts = sem("consts_ready"); cact_done = sem("cact_done")
        x_ready = sem("x_ready"); sq_done = sem("sq_done"); ss_add = sem("ss_add"); ss_sum = sem("ss_summed")
        rstd_ready = sem("rstd_ready"); ln_ready = sem("ln_ready")
        ht_ready = sem("h_scaled"); hhi_done = sem("h_hi_done"); hlo_done = sem("h_lo_done")
        silu_done = sem("silu_done"); prod_done = sem("prod_done")
        midhi_done = sem("mid_hi_done"); midlo_done = sem("mid_lo_done")
        dve_step = sem("dve_step"); act_step = sem("act_step")
        out_ready = sem("out_ready")
        S = {}

        def named(*names):
            for n in names:
                S[n] = sem(n)

        named("evin_free", "evsilu", "z_silu", "gate_a", "l2sq", "l2ln", "l2sum", "l2r", "l2done", "ba_t", "ba_sb", "ba_e", "g_done",
              "gc_ps", "gc_sb", "gcrow_ps", "gcrow_sb", "glast_ps", "gcols", "gcols2",
              "rsq", "rsum", "rln", "rr", "rt", "rhi", "rlo", "pj_free",
              "pj_ps", "hd_ps", "hd_exp", "hd_free", "kt_free",
              "y_ps", "y_sb", "z_ps", "inv_up",
              "ks_ps", "r_sb", "vn_ps", "vn_sb", "su_ps", "s_up", "o_ps", "o_sb",
              "osq", "osum", "oln", "orr", "ot", "ohi", "olo",
              "trig_a", "trig_d", "rot_ps", "rope", "sc_ps", "sc_mask", "sc_exp", "sc_norm", "pt_ps", "pt_sb",
              "av_ps", "av_hi", "av_lo", "sc_max")
        named("odin_free", "odsilu", "z_free", "dt_t", "dt_a", "dt_e", "da_sb", "acs_ps", "acs_sb", "acr_ps", "acr_sb",
              "acl_ps", "acl_d", "acl_a", "bt_ps", "bt_sb", "cb_ps", "cb_sb", "xde", "aux_ps", "aux_sb",
              "L_ps", "L_sb", "G_sb", "E_ps", "E_sb", "yd_ps", "yd_read", "yo_ps", "yo_read", "y_done",
              "ysq", "yss", "ysum", "yln", "yrr", "yt", "yhi", "ylo")

        def vcol(name, i=0):
            return vec[:, VEC[name] + i:VEC[name] + i + 1]

        block = ctx.enter_context(nc.Block())

        def used(u):
            return u + 1 + HL

        def x_at(n, m):
            return KT * n + m + 1

        def ss_at(n, m):
            return KT * n + m + 1 + 2

        def gd(name):
            i = ["beta", "g", "gc", "nbeta", "nbe", "ke", "egl", "ngc", "eg", "glast", "z", "t0", "t1", "t2", "t3",
                 "t4", "t5"].index(name)
            return small[:, i // 8, (i % 8) * 16:(i % 8) * 16 + 16]

        def sd(name):
            return small[:, ["dt", "da", "acs", "nacs", "de", "cd", "t0", "t1", "t2", "t3"].index(name), :]

        rows = gate_s[:, 0, :]
        decay_rows = ssacc[0:96, :].bitcast(BF16)[:, 0:SEQ]
        acc_flat = ada_acc[:, :, :].rearrange("p a n -> p (a n)")[:, 0:SEQ]

        lvl_in = h_f[:, 12:16, :].rearrange("p a n -> p (a n)")[:, 0:2 * len(LEVELS) * P].bitcast(I32)

        def xde_at(q):
            return rstd[:, :] if q % 2 == 0 else acc_flat

        def hst(g, b):
            return h_f[:, 8 + 3 * (g % 2) + b - 1, :]

        def xtok(g, b):
            return h_f[:, 4 * (g % 2) + b, :]

        def g_at(h):
            return gate_s[:, h % 4, :] if h % 4 < 2 else h_f[:, 12 + h % 4, :]

        aux_first = [("tok", 0, b) for b in range(NB)] + [("state", 0, b) for b in range(NB - 1)]
        aux_of = {}
        for _g in range(SSD_G):
            for _t, _items in enumerate(((("tok", 0), ("tok", 1)), (("tok", 2), ("state", 0)), (("tok", 3), ("state", 1)),
                                         (("state", 2),))):
                aux_of[4 * _g + _t] = [(kind, _g + 1, b) for kind, b in _items] if _g + 1 < SSD_G else []
        aux_all = aux_first + [a for j in range(SSD_XT) for a in aux_of[j]]

        def aux_bank(n):
            return ps[3 if n % 2 == 0 else 7]

        def state_no(g, b):
            return 3 * g + b

        def chunk(b):
            return slice(b * CH, (b + 1) * CH)

        NQ = len(LEVELS) * HEADS
        inv_seq = [(lv, h) for lv in range(len(LEVELS)) for h in range(HEADS)]
        def lat_hi(q):
            return mid_hi[:, LAT_HI + q, :]

        def lat_lo(q):
            return mid_lo[:, CQ0 + q - FT, :]

        sine, cosine, rope_t = hstate[:, 0, :], hstate[:, 1, :], hstate[:, 2, :]
        att_seq = [(h, b) for h in range(HEADS) for b in range(NB)]
        ev_ps = [ps[4 + m % 2] for m in range(KT)]

        def pj_ready(t):
            u, v = PHASES["uq"][0], PHASES["ukv"][0]
            if t < 6:
                return (unit_done, used(u + t // 2)) if t % 2 else (S["pj_ps"], t // 2 + 1)
            if t < 10:
                return (unit_done, used(v)) if t == 9 else (S["pj_ps"], t - 6 + 4)
            return (unit_done, used(v + 1)) if t == 13 else (S["pj_ps"], t - 10 + 7)

        @block.sync
        def _(sp):
            def unit(u, w_ap, nk):
                u0, di = u
                s = u0 % RAW
                sp.wait_ge(lo_done, u0 + di + 1)
                sp.dma_start(raw[:, s, 0:nk * P], w_ap).then_inc(raw_full[s], 16)

            def run(name, w, f=None, extra=None):
                u0, n, nk = PHASES[name]
                n4 = n // 4 if n >= 8 else 0

                def at(j):
                    a = w[f] if f is not None else w
                    return a[bass.ds(j, 1), :, :].rearrange("a p n -> (a p) n")
                if n4:
                    with sp.Fori(0, n4) as i:
                        for j in range(4):
                            unit((u0 + j, i * 4), at(i * 4 + j), nk)
                            if extra:
                                extra(i, j)
                for j in range(4 * n4, n):
                    unit((u0 + j, 0), w[f, j] if f is not None else w[j], nk)

            def ada(g0, gi):
                sp.wait_ge(ada_done, g0 + gi + 1)
                sp.dma_start(ada_sb[:, g0 % 2, :, :],
                             src["ada"][bass.ds(g0 + gi, 1), :, :].rearrange("a p (k n) -> (a p) k n", k=KT)
                             ).then_inc(ada_full[g0 % 2], 16)

            def ada_extra(name):
                g0, per = ADA_AT[name]
                u0 = PHASES[name][0]

                def extra(i, j):
                    if j == 1:
                        sp.wait_ge(unit_done, used(u0 - 1))
                    if j in (1, 3):
                        h = per // 2
                        for q in range(h):
                            ada(g0 + (j // 2) * h + q, i * per)
                return extra

            for g in range(ADA_G):
                if g == ADA_G - 2:
                    for j in range(4):
                        u0, n, nk = PHASES["up0"]
                        sp.dma_start(raw[:, j, 0:nk * P], src["up"][0, j]).then_inc(raw_full[j], 16)
                ada(g, 0)
            u0, n, nk = PHASES["up0"]
            with sp.Fori(1, n // 4) as i:
                for j in range(4):
                    unit((u0 + j, i * 4), src["up"][0][bass.ds(i * 4 + j, 1), :, :].rearrange("a p n -> (a p) n"), nk)
            run("down0", src["down"], 0, ada_extra("down0"))
            run("ev_in", src["ev_in"])
            run("uq", src["uq"])
            run("ukv", src["ukv"])
            run("ev_out", src["ev_out"])
            run("up1", src["up"], 1)
            run("down1", src["down"], 1, ada_extra("down1"))
            run("up2", src["up"], 2)
            run("down2", src["down"], 2, ada_extra("down2"))
            run("od_in", src["od_in"])
            run("od_out", src["od_out"])
            run("up3", src["up"], 3)
            run("down3", src["down"], 3)
            for kt in range(KT):
                sp.wait_ge(out_ready, kt + 1)
                sp.dma_start(out[kt], mid[:, kt, :]).then_inc(stored, 16)
            sp.wait_ge(stored, 16 * KT)

        @block.gpsimd
        def _(pool):
            pool.sem_inc(lo_done, RAW)

            def unit(u0, di, nk, a0, p0):
                s, h = u0 % RAW, u0 % HL
                if a0 is None:
                    pool.wait_ge(raw_full[s], (u0 // RAW + 1) * 16 + di * (16 // RAW))
                    pool.wait_ge(unit_done, u0 + di + 1)
                    pool.tensor_tensor(whi[:, h, 0:nk * P], raw[:, s, 0:nk * P], ones[:, 0:1].to_broadcast([P, nk * P]),
                                       ALU.mult).then_inc(hi_done, 1)
                    pool.wait_ge(hi_done, p0 + di + 1)
                else:
                    pool.wait_ge(act_hi, a0 + di + 1)
                pool.tensor_tensor(wlo[:, h, 0:nk * P], raw[:, s, 0:nk * P], whi[:, h, 0:nk * P].bitcast(F32),
                                   ALU.subtract).then_inc(lo_done, 1)

            def ssd_core():
                pool.wait_ge(S["cb_sb"], SSD_G)

                def add(j):
                    g, t = divmod(j, 4)
                    pool.wait_ge(S["ysq"], j + 1)
                    if t:
                        if t > 1:
                            pool.wait_ge(S["yss"], 3 * g + t - 1)
                        acc = mid[:, SZ0 + 4 * g, :]
                        pool.tensor_tensor(acc, acc, mid[:, SZ0 + j, :], ALU.add).then_inc(S["yss"], 1)
                for j in range(SSD_XT):
                    for h in (2 * j, 2 * j + 1):
                        pool.wait_ge(S["L_sb"], h + 1)
                        if h >= 4:
                            pool.wait_ge(S["yd_ps"], h - 3)
                        pool.tensor_tensor(g_at(h), tmp[:, h % 2, :], mid[:, B0 + h // 8, :], ALU.mult).then_inc(S["G_sb"], 1)
                    if j >= 2:
                        add(j - 2)
                add(SSD_XT - 2)
                add(SSD_XT - 1)
            for name, (u0, n, nk) in PHASES.items():
                n4 = n // 4 if n >= 8 else 0
                a0, p0 = HI_AT[name]

                def at(j, di):
                    unit(u0 + j, di, nk, None if a0 is None else a0 + j, None if p0 is None else p0 + j)
                first = 0
                if name == "od_out":
                    at(0, 0)
                    at(1, 0)
                    ssd_core()
                    at(2, 0)
                    at(3, 0)
                    first = 1
                if n4:
                    with pool.Fori(first, n4) as i:
                        for j in range(4):
                            at(j, i * 4)
                for j in range(4 * n4, n):
                    at(j, 0)

        @block.tensor
        def _(pe):
            mm = pe.matmul
            pe.sem_inc(unit_done, HL)
            pe.sem_inc(mod_sum, 2)
            pe.wait_ge(consts, 1)

            def split_ready(u0, di):
                pe.wait_ge(lo_done, u0 + di + 1 + RAW)

            def passes(bank, u0, k, hi, lo, start, stop, w_at=None):
                s = u0 % HL
                c = slice(k * P, (k + 1) * P) if w_at is None else w_at
                mm(bank, wlo[:, s, c], hi, start=start, stop=False)
                mm(bank, whi[:, s, c], lo, start=False, stop=False)
                return mm(bank, whi[:, s, c], hi, start=False, stop=stop)

            def ffn_up(f):
                u0, n, nk = PHASES[f"up{f}"]
                q0 = FT * f
                hl0 = KT * {0: 0, 1: 2, 2: 3, 3: 5}[f]

                def body(i, first):
                    for t in range(2):
                        pe.wait_ge(prod_done, q0 + i * 2 + t + 1)
                        for w in range(2):
                            uu = u0 + 2 * t + w
                            split_ready(uu, i * 4)
                            for k in range(KT):
                                if first and t == 0 and w == 0:
                                    pe.wait_ge(hlo_done, hl0 + k + 1)
                                last = passes(ps[2 * t + w][:, :], uu, k, h_hi[:, k, :], h_lo[:, k, :], k == 0, k == KT - 1)
                            last.then_inc(unit_done, 1)
                body(0, True)
                with pe.Fori(1, n // 4) as i:
                    body(i, False)

            def mod_group(g0, gi):
                pe.wait_ge(ada_done, g0 + gi + 1 + 2)
                for c in range(3):
                    last = mm(ps[6][:, bass.ds(3 * g0 + c + gi * 3, 1)],
                              ada_acc[:, g0 % 2, c * P:(c + 1) * P], ones[:, 0:1], start=True, stop=True)
                last.then_inc(mod_sum, 1)

            def ffn_down(f):
                name = f"down{f}"
                u0, n, nk = PHASES[name]
                nv = {0: 1, 1: 3, 2: 4, 3: 6}[f]

                def body(i, first):
                    for t in range(2):
                        pe.wait_ge(x_ready, x_at(nv, 0) + i * 2 + t - 2)
                        for w in range(2):
                            uu = u0 + 2 * t + w
                            split_ready(uu, i * 4)
                            if first and t == 0:
                                pe.wait_ge(midlo_done, FT * f + 11 * (w + 1))
                            for k in range(11):
                                kk = 11 * w + k
                                last = passes(ps[4 + t][:, :], uu, k, mid_hi[:, kk, :], mid_lo[:, kk, :], kk == 0, kk == 21)
                            last.then_inc(unit_done, 1)
                        if name in ADA_AT:
                            g0, per = ADA_AT[name]
                            for q in range(per // 2):
                                mod_group(g0 + t * (per // 2) + q, i * per)
                body(0, True)
                with pe.Fori(1, n // 4) as i:
                    body(i, False)

            def norm_sum(n):
                pe.wait_ge(ss_add, ss_at(n, KT - 1))
                mm(ps[7][:, :], ones[:, :], ssacc[:, :], start=True, stop=True).then_inc(ss_sum, 1)

            for g in range(ADA_G):
                mod_group(g, 0)
            norm_sum(0)
            ffn_up(0)
            ffn_down(0)
            norm_sum(1)
            u0, n, nk = PHASES["ev_in"]

            def proj_tile(u0, j, di, bank, free, freed, hl0=None):
                pe.wait_ge(free, freed + di + 1)
                split_ready(u0 + j, di)
                for k in range(KT):
                    if hl0 is not None:
                        pe.wait_ge(hlo_done, hl0 + k + 1)
                    last = passes(ps[bank][:, :], u0 + j, k, h_hi[:, k, :], h_lo[:, k, :], k == 0, k == KT - 1)
                last.then_inc(unit_done, 1)
            def latent_sum(a, nt):
                for t in range(nt):
                    q = 3 * a + t
                    pe.wait_ge(S["rsq"], q + 1)
                    if q >= 3:
                        pe.wait_ge(S["rln"], 1)
                    mm(ps[6][:, :], ones[:, :], sq[:, q % 2, :], start=t == 0, stop=t == nt - 1).then_inc(S["rsum"], 1)
            for j in range(EV_FIRST):
                proj_tile(u0, j, 0, j % 4, S["evin_free"], j, KT * 1 if j == 0 else None)
                if j == 4:
                    latent_sum(0, 3)
            for b in range(NB):
                last = pe.transpose(ps[7][:, 8 * b:8 * b + 8], rows[0:8, b * CH:(b + 1) * CH], ident[0:8, 0:8])
            last.then_inc(S["ba_t"], 1)
            latent_sum(1, 2)
            with pe.Fori(0, 3) as i:
                for j in range(4):
                    proj_tile(u0, EV_FIRST + j, i * 4, (EV_FIRST + j) % 4, S["evin_free"], EV_FIRST + j)

            def l2_sums(t0):
                for t in range(t0, t0 + 4):
                    pe.wait_ge(S["l2sq"], t + 1)
                    if t >= 4:
                        pe.wait_ge(S["l2ln"], t - 3)
                    mm(ps[4 + t % 4][:, :], ones[:, :], mid[:, L2 + t, :], start=True, stop=True).then_inc(S["l2sum"], 1)
            pe.wait_ge(S["g_done"], 1)
            mm(ps[4][:, 0:16], tri[:, :], gd("g"), start=True, stop=True).then_inc(S["gc_ps"], 1)
            for k in range(HEADS):
                j = EV_FIRST + GDN_TILES + k
                proj_tile(u0, j, 0, j % 4, S["evin_free"], j)
                if k == 0:
                    pe.wait_ge(S["gc_sb"], 1)
                    for r in (0, 32, 64):
                        for b in range(NB):
                            last = mm(ps[5][r:r + HEADS, chunk(b)], gd("gc")[:, HEADS * b:HEADS * (b + 1)], ident[:, :],
                                      start=True, stop=True)
                    last.then_inc(S["gcrow_ps"], 1)
                    mm(ps[6][:, 0:16], ident[:, P - 1:P].to_broadcast([P, P]), gd("gc"), start=True, stop=True
                       ).then_inc(S["glast_ps"], 1)
                elif k == 2:
                    pe.wait_ge(S["gcols"], 1)
                    pe.wait_ge(S["gcrow_sb"], 1)
                    l2_sums(0)
            l2_sums(4)
            u0 = PHASES["uq"][0]
            tile = 0

            def pj_bank():
                if tile >= 4:
                    pe.wait_ge(S["pj_free"], tile - 3)
                else:
                    pe.wait_ge(S["l2ln"], 5 + tile)
                return ps[4 + tile % 4][:, :]
            for j in range(3):
                split_ready(u0 + j, 0)
                for t in range(2):
                    bank = pj_bank()
                    for k in range(3):
                        if tile == 0:
                            pe.wait_ge(S["rlo"], k + 1)
                        last = passes(bank, u0 + j, 3 * t + k, lat_hi(k), lat_lo(k), k == 0, k == 2)
                    tile += 1
                    if t == 0:
                        last.then_inc(S["pj_ps"], 1)
                last.then_inc(unit_done, 1)
            u0 = PHASES["ukv"][0]
            split_ready(u0, 0)
            pe.wait_ge(S["rlo"], 5)
            for t in range(4):
                bank = pj_bank()
                for k in range(2):
                    last = passes(bank, u0, 2 * t + k, lat_hi(3 + k), lat_lo(3 + k), k == 0, k == 1)
                tile += 1
                last.then_inc(S["pj_ps"] if t < 3 else unit_done, 1)
            split_ready(u0 + 1, 0)
            s = (u0 + 1) % HL
            for b in range(NB):
                bank = pj_bank()
                for k in range(2):
                    c = slice(k * SEQ, (k + 1) * SEQ)
                    tok = chunk(b)
                    mm(bank, lat_lo(3 + k)[:, tok], whi[:, s, c], start=k == 0, stop=False)
                    mm(bank, lat_hi(3 + k)[:, tok], wlo[:, s, c], start=False, stop=False)
                    last = mm(bank, lat_hi(3 + k)[:, tok], whi[:, s, c], start=False, stop=k == 1)
                tile += 1
                last.then_inc(S["pj_ps"] if b < 3 else unit_done, 1)
            pe.wait_ge(S["z_silu"], HEADS)
            pe.wait_ge(S["l2done"], 8)
            pe.wait_ge(S["pj_free"], 14)
            for h in range(HEADS):
                sel = pick[:, h:h + 1].to_broadcast([96, P])
                kh, qh, vh = mid[:, K0 + h, :], mid[:, Q0 + h, :], mid[:, V0 + h, :]
                if h:
                    pe.wait_ge(S["hd_exp"], 3 * h)
                mm(ps[0][:, :], sel, decay_rows, start=True, stop=False)
                mm(ps[0][:, :], ident_b[:, :], pos_b[:, :].unsqueeze(1).to_broadcast([P, NB, P]), start=False, stop=True)
                mm(ps[1][:, :], sel, decay_rows, start=True, stop=False)
                mm(ps[1][:, :], ident_b[:, :], neg_b[:, :].unsqueeze(1).to_broadcast([P, NB, P]), start=False, stop=True)
                mm(ps[2][:, :], sel, decay_rows, start=True, stop=True).then_inc(S["hd_ps"], 1)
                if h:
                    pe.wait_ge(S["hd_free"], 4 * h)
                for b in range(NB):
                    tok = chunk(b)
                    mm(ps[3][:, tok], kh[:, tok], kh[:, tok], start=True, stop=True)
                for b in range(NB):
                    tok = chunk(b)
                    mm(ps[4][:, tok], kh[:, tok], qh[:, tok], start=True, stop=True)
                for b in range(NB):
                    tok = chunk(b)
                    pe.transpose(ps[5][:, tok], kh[:, tok], ident[:, :])
                for b in range(NB):
                    tok = chunk(b)
                    last = pe.transpose(ps[6][:, tok], vh[:, tok], ident[:, :])
                last.then_inc(S["hd_ps"], 1)
                if h < 3:
                    if h:
                        pe.wait_ge(S["rope"], h)
                    mm(ps[7][:, :], rot[:, :], mid[:, (QPE0, QPE0 + 1, KPE)[h], :], start=True, stop=True).then_inc(S["rot_ps"], 1)
            pe.wait_ge(S["hd_free"], 4 * HEADS)
            pe.wait_ge(S["hd_exp"], 3 * HEADS)

            def inv_y(q):
                lv, h = inv_seq[q]
                pe.wait_ge(S["inv_up"], q + 1)
                if q >= 2:
                    pe.wait_ge(S["y_sb"], q - 1)
                for b in range(NB):
                    tok = chunk(b)
                    last = mm(ps[q % 2][:, tok], h_f[:, 0 + h, tok], mid[:, MT0 + h, tok], start=True, stop=True)
                last.then_inc(S["y_ps"], 1)

            def inv_z(q):
                lv, h = inv_seq[q]
                pe.wait_ge(S["y_sb"], q + 1)
                if q >= 2:
                    pe.wait_ge(S["inv_up"], q - 1 + HEADS)
                for b in range(NB):
                    if lv < len(LEVELS) - 1:
                        tok = chunk(b)
                        mm(ps[2 + q % 2][:, tok], h_f[:, 8 + h, tok], h_f[:, 4 + h, tok], start=True, stop=True)
                for b in range(NB):
                    tok = chunk(b)
                    last = mm(ps[4 + q % 2][:, tok], h_f[:, 4 + h, tok], h_f[:, 8 + h, tok], start=True, stop=True)
                last.then_inc(S["z_ps"], 1)
            for q in range(NQ + 1):
                if q < NQ:
                    inv_y(q)
                if q >= 1:
                    inv_z(q - 1)
            pe.wait_ge(S["inv_up"], NQ + HEADS)
            for b in range(NB):
                tok = chunk(b)
                if b:
                    pe.wait_ge(S["s_up"], b)
                    for h in range(HEADS):
                        last = mm(ps[0][:, h * P:(h + 1) * P], mid[:, K0 + h, tok], mid[:, ST, h * P:(h + 1) * P], start=True, stop=True)
                    last.then_inc(S["ks_ps"], 1)
                pe.wait_ge(S["r_sb"], b + 1)
                for h in range(HEADS):
                    last = mm(ps[1][:, h * P:(h + 1) * P], mid[:, MT0 + h, tok], tmp[:, 0, h * P:(h + 1) * P], start=True, stop=True)
                last.then_inc(S["vn_ps"], 1)
                pe.wait_ge(S["vn_sb"], b + 1)
                if b < NB - 1:
                    for h in range(HEADS):
                        last = mm(ps[2][:, h * P:(h + 1) * P], h_f[:, 12 + h, tok], tmp[:, 1, h * P:(h + 1) * P], start=True, stop=True)
                    last.then_inc(S["su_ps"], 1)
                if b:
                    pe.wait_ge(S["o_sb"], b)
                for h in range(HEADS):
                    hc = slice(h * P, (h + 1) * P)
                    last = mm(ps[3][:, hc], tmp[:, 1, hc], mid[:, AT0 + h, tok], start=True, stop=b == 0)
                    if b:
                        last = mm(ps[3][:, hc], mid[:, ST, hc], mid[:, Q0 + h, tok], start=False, stop=True)
                last.then_inc(S["o_ps"], 1)
            for h in range(HEADS):
                pe.wait_ge(S["osq"], h + 1)
                if h >= 2:
                    pe.wait_ge(S["oln"], h - 1)
                mm(ps[4 + h % 2][:, :], ones[:, :], sq[:, h % 2, :], start=True, stop=True).then_inc(S["osum"], 1)
            pe.wait_ge(S["o_sb"], NB)
            pe.wait_ge(S["rope"], 3)
            pe.wait_ge(S["oln"], HEADS)

            def att_scores(q):
                h, b = att_seq[q]
                nk = (b + 1) * CH
                tok = chunk(b)
                half = slice(64 * (h % 2), 64 * (h % 2) + 64)
                if q >= 2:
                    pe.wait_ge(S["sc_exp"], q - 1)
                bank = ps[q % 2][:, 0:nk]
                mm(bank, mid[:, QN0 + h, tok], mid[:, KN0 + h, 0:nk], start=True, stop=False)
                mm(bank, mid[half, QPE0 + h // 2, tok], mid[half, KPE, 0:nk], start=False, stop=True).then_inc(S["sc_ps"], 1)

            def att_values(q):
                h, b = att_seq[q]
                tok = chunk(b)
                pe.wait_ge(S["sc_norm"], q + 1)
                if q >= 2:
                    pe.wait_ge(S["pt_sb"], q - 1)
                for kb in range(b + 1):
                    last = pe.transpose(ps[2 + q % 2][:, kb * CH:(kb + 1) * CH], mid[:, q % 2, kb * CH:(kb + 1) * CH], ident[:, :])
                last.then_inc(S["pt_ps"], 1)
                pe.wait_ge(S["pt_sb"], q + 1)
                if b == 0 and h >= 2:
                    pe.wait_ge(S["av_lo"], h - 1)
                for kb in range(b + 1):
                    last = mm(ps[4 + h % 2][:, tok], mid[:, VM0 + kb, h * P:(h + 1) * P], mid[:, 2 + q % 2, kb * CH:(kb + 1) * CH],
                              start=kb == 0, stop=kb == b)
                last.then_inc(S["av_ps"], 1)
            for q in range(len(att_seq) + 1):
                if q < len(att_seq):
                    att_scores(q)
                if q >= 1:
                    att_values(q - 1)
            u0 = PHASES["ev_out"][0]
            pe.wait_ge(S["olo"], HEADS)
            pe.wait_ge(S["av_lo"], HEADS)
            pe.wait_ge(S["av_hi"], HEADS)
            for m in range(KT):
                pe.wait_ge(x_ready, x_at(2, m) - 2)
                split_ready(u0 + m, 0)
                for k in range(KT):
                    last = passes(ps[4 + m % 2][:, :], u0 + m, k, h_hi[:, k, :], h_lo[:, k, :], k == 0, k == KT - 1)
                last.then_inc(unit_done, 1)
            norm_sum(2)
            ffn_up(1)
            ffn_down(1)
            norm_sum(3)
            ffn_up(2)
            ffn_down(2)
            norm_sum(4)
            u0, n, nk = PHASES["od_in"]
            proj_tile(u0, 0, 0, 0, S["odin_free"], 0, KT * 4)
            with pe.Fori(0, 6) as i:
                for j in range(4):
                    proj_tile(u0, 1 + j, i * 4, (1 + j) % 4, S["odin_free"], 1 + j)
            for b in range(NB):
                last = pe.transpose(ps[4][:, 32 * b:32 * b + 32], rows[0:32, b * CH:(b + 1) * CH], ident[0:32, 0:32])
            last.then_inc(S["dt_t"], 1)

            def before_core(k):
                if k == 1:
                    pe.wait_ge(S["da_sb"], 1)
                    mm(ps[5][:, 0:P], tri[:, :], sd("da"), start=True, stop=True).then_inc(S["acs_ps"], 1)
                elif k == 2:
                    pe.wait_ge(S["acs_sb"], 1)
                    for r in (0, 32, 64):
                        for b in range(NB):
                            last = mm(ps[6][r:r + SSD_H, chunk(b)], sd("acs")[:, SSD_H * b:SSD_H * (b + 1)], ident[:, :],
                                      start=True, stop=True)
                    last.then_inc(S["acr_ps"], 1)
                    mm(ps[7][:, 0:P], ident[:, P - 1:P].to_broadcast([P, P]), sd("acs"), start=True, stop=True).then_inc(S["acl_ps"], 1)
                elif 4 <= k < 4 + NB - 1:
                    b = k - 4
                    pe.wait_ge(S["odsilu"], SSD_CONV)
                    if b >= 2:
                        pe.wait_ge(S["bt_sb"], b - 1)
                    for g in range(SSD_G):
                        last = pe.transpose(ps[4 + b % 2][:, g * P:(g + 1) * P], mid[:, B0 + g, chunk(b)], ident[:, :])
                    last.then_inc(S["bt_ps"], 1)
                elif 8 <= k < 8 + SSD_G:
                    g = k - 8
                    pe.wait_ge(S["acr_sb"], 1)
                    pe.wait_ge(S["acl_d"], 1)
                    if g >= 2:
                        pe.wait_ge(S["cb_sb"], g - 1)
                    for b in range(NB):
                        tok = chunk(b)
                        last = mm(ps[6 + g % 2][:, tok], mid[:, B0 + g, tok], mid[:, C0 + g, tok], start=True, stop=True)
                    last.then_inc(S["cb_ps"], 1)
            for k in range(SSD_XT):
                n_odd = 1 + SSD_CONV + k
                if k < 4:
                    proj_tile(u0, n_odd, 0, n_odd % 4, S["odin_free"], n_odd)
                else:
                    proj_tile(u0, n_odd, 0, n_odd % 4, S["z_free"], k - 4)
                before_core(k)
            pe.wait_ge(S["z_free"], SSD_XT)
            pe.wait_ge(S["cb_sb"], SSD_G)
            pe.wait_ge(S["bt_sb"], NB - 1)
            pe.wait_ge(S["acl_a"], 2)

            def ssd_L(h):
                if h >= 2:
                    pe.wait_ge(S["L_sb"], h - 1)
                mm(ps[h % 2][:, :], pick[:, h:h + 1].to_broadcast([96, P]), decay_rows, start=True, stop=False)
                mm(ps[h % 2][:, :], ident_b[:, :], neg_b[:, :].unsqueeze(1).to_broadcast([P, NB, P]), start=False, stop=True
                   ).then_inc(S["L_ps"], 1)

            def ssd_E(j):
                if j:
                    pe.wait_ge(S["E_sb"], j)
                if j % 4 == 0 and j > 4:
                    pe.wait_ge(S["yln"], j // 4 - 1)
                for par in range(2):
                    last = mm(ps[2][64 * par:64 * par + 64, CH:SEQ], pick[:, 2 * j + par:2 * j + par + 1].to_broadcast([96, 64]),
                              decay_rows[:, CH:SEQ], start=True, stop=True)
                last.then_inc(S["E_ps"], 1)

            def aux(n):
                kind, g, b = aux_all[n]
                if n >= 2:
                    pe.wait_ge(S["aux_sb"], n - 1)
                if kind == "tok":
                    for t in range(4):
                        last = pe.transpose(aux_bank(n)[:, t * P:(t + 1) * P], mid[:, 4 * g + t, chunk(b)], ident[:, :])
                else:
                    pe.wait_ge(S["xde"], state_no(g, b) + 1)
                    last = mm(aux_bank(n)[:, :], mid[:, MIDS - 4 + b, g * P:(g + 1) * P], xde_at(state_no(g, b)), start=True, stop=True)
                last.then_inc(S["aux_ps"], 1)

            def ssd_y(j):
                g = j // 4
                if j >= 2:
                    pe.wait_ge(S["yd_read"], j - 1)
                for par in range(2):
                    h = 2 * j + par
                    pe.wait_ge(S["G_sb"], h + 1)
                    for b in range(NB):
                        tok = chunk(b)
                        last = mm(ps[4 + j % 2][64 * par:64 * par + 64, tok], xtok(g, b)[:, (h % 8) * 64:(h % 8) * 64 + 64],
                                  g_at(h)[:, tok], start=True, stop=True)
                    last.then_inc(S["yd_ps"], 1)
                if j:
                    pe.wait_ge(S["yo_read"], j)
                for b in range(1, NB):
                    tok = chunk(b)
                    last = mm(ps[6][:, tok], hst(g, b)[:, (j % 4) * P:(j % 4 + 1) * P], mid[:, C0 + g, tok], start=True, stop=True)
                last.then_inc(S["yo_ps"], 1)

            def group_sum(g):
                pe.wait_ge(S["yss"], 3 * g + 3)
                pe.wait_ge(S["E_sb"], min(4 * g + 8, SSD_XT))
                mm(ps[2][:, :], ones[:, :], mid[:, SZ0 + 4 * g, :], start=True, stop=True).then_inc(S["ysum"], 1)
            ssd_L(0)
            ssd_L(1)
            ssd_E(0)
            for n in range(len(aux_first)):
                aux(n)
            n_aux = len(aux_first)
            pe.wait_ge(S["aux_sb"], n_aux)
            for j in range(SSD_XT):
                if j + 1 < SSD_XT:
                    ssd_L(2 * j + 2)
                    ssd_L(2 * j + 3)
                    ssd_E(j + 1)
                for n in range(len(aux_of[j])):
                    aux(n_aux)
                    n_aux += 1
                if j % 4 == 2 and j > 3:
                    group_sum(j // 4 - 1)
                if j % 4 == 0 and j:
                    pe.wait_ge(S["aux_sb"], n_aux - len(aux_of[j]))
                ssd_y(j)
            group_sum(SSD_G - 1)
            u0 = PHASES["od_out"][0]
            for m in range(KT):
                pe.wait_ge(x_ready, x_at(5, m) - 2)
                for w in range(2):
                    uu = u0 + 2 * m + w
                    split_ready(uu, 0)
                    for k in range(8):
                        kk = 8 * w + k
                        if m == 0:
                            pe.wait_ge(S["ylo"], kk + 1)
                        last = passes(ps[4 + m % 2][:, :], uu, k, mid_hi[:, kk, :], mid_lo[:, kk, :], kk == 0, kk == 15)
                    last.then_inc(unit_done, 1)
            norm_sum(5)
            ffn_up(3)
            ffn_down(3)
            norm_sum(6)

        @block.scalar
        def _(act):
            fn = act.activation
            step = Tally(act_step)
            for d, a in ((vec[:, :], src["vec"]), (ident[:, :], src["ident"]), (ones[:, :], src["ones"]),
                         (tri[:, :], src["tri"]), (rot[:, :], src["rot"]), (qmask[:, :], src["qmask"]),
                         (tmp[:, 0, 0:P], src["neg"]), (tmp[:, 0, P:2 * P], src["pos_mask"]),
                         (lvl_in, src["lvl"])):
                act.dma_start(d, a).then_inc(const_in, 16)
            act.dma_start(pos[:, :], src["positions"].to_broadcast([P, SEQ])).then_inc(const_in, 16)
            for kt in range(KT):
                act.dma_start(x[:, kt, :], src["x"][kt]).then_inc(x_in, 16)
            act.wait_ge(const_in, 16 * 10)
            fn(cact[:, :], vec[:, VEC["c"]:VEC["c"] + KT], ACT.Silu).then_inc(cact_done, 1)
            act.wait_ge(x_in, 16 * KT)

            def squares(n, m, dm):
                act.wait_ge(x_ready, x_at(n, m) + dm)
                act.wait_ge(ss_add, KT * n + m + 1 + dm)
                fn(sq[:, m % 2, :], x[:, bass.ds(m + dm, 1), :].rearrange("p a n -> p (a n)"), ACT.Square
                   ).then_inc(sq_done, 1)

            def inv_root(dst, bank, n_mean, read, ready, count):
                fn(dst, bank, ACT.Ln, bias=epsc[:, 0:1], scale=1.0 / n_mean).then_inc(read, 1)
                act.wait_ge(read, count)
                fn(dst, dst, ACT.Exp, scale=-0.5).then_inc(ready, 1)

            def norm(n):
                act.wait_ge(ss_sum, n + 1)
                inv_root(rstd[:, :], ps[7][:, :], D, ln_ready, rstd_ready, n + 1)
                if n < 6:
                    for kt in range(KT):
                        act.wait_ge(ht_ready, KT * n + kt + 1)
                        fn(h_hi[:, kt, :], tmp[:, kt % 2, :], ACT.Identity,
                           bias=mod[:, 24 * n + kt:24 * n + kt + 1]).then_inc(hhi_done, 1)

            def weight_hi(name, j, di=0):
                u0, n, nk = PHASES[name]
                s = (u0 + j) % RAW
                act.wait_ge(raw_full[s], ((u0 + j) // RAW + 1) * 16 + di * (16 // RAW))
                act.wait_ge(unit_done, u0 + j + di + 1)
                act.copy(whi[:, (u0 + j) % HL, 0:nk * P], raw[:, s, 0:nk * P]).then_inc(act_hi, 1)

            def ffn_up(f):
                name = f"up{f}"
                u0, n, nk = PHASES[name]
                q0 = FT * f

                def body(i, ahead):
                    for t in range(2):
                        ahead(i, t, 0)
                        act.wait_ge(unit_done, used(u0 + 2 * t) + i * 4)
                        act.wait_ge(prod_done, q0 + t + 1 + i * 2)
                        fn(gate_s[:, t, :], ps[2 * t][:, :], ACT.Silu).then_inc(silu_done, 1)
                        ahead(i, t, 1)
                        act.wait_ge(prod_done, q0 + t + 3 + i * 2)
                        act.copy(one(mid_hi[:, bass.ds(i * 2 + t, 1), :]), tmp[:, t, :]).then_inc(midhi_done, 1)
                with act.Fori(0, n // 4 - 1) as i:
                    body(i, lambda i, t, w: weight_hi(name, 2 * t + w + 2, i * 4))
                last = n // 4 - 1
                body(last, lambda i, t, w: weight_hi(name, n - 2 + w) if t == 0 else weight_hi(f"down{f}", w))

            def first_hi(following, w):
                if following:
                    weight_hi(following, w)

            def ffn_down(f, nv, following):
                name = f"down{f}"
                with act.Fori(0, KT // 2 - 1) as i:
                    for t in range(2):
                        weight_hi(name, 2 * t + 2, i * 4)
                        weight_hi(name, 2 * t + 3, i * 4)
                        squares(nv, t, i * 2)
                weight_hi(name, 14)
                weight_hi(name, 15)
                squares(nv, KT - 2, 0)
                first_hi(following, 0)
                squares(nv, KT - 1, 0)
                first_hi(following, 1)

            for m in range(KT):
                squares(0, m, 0)
            first_hi("up0", 0)
            first_hi("up0", 1)
            norm(0)
            ffn_up(0)
            for a in range(2):
                act.wait_ge(S["trig_d"], a + 1)
                fn((sine, cosine)[a], (sine, cosine)[a], ACT.Sin).then_inc(S["trig_a"], 1)
            ffn_down(0, 1, None)
            norm(1)
            for a, nt in enumerate((3, 2)):
                for t in range(nt):
                    q = 3 * a + t
                    act.wait_ge(S["evin_free"], 4 + 1 + q + 1)
                    if q >= 2:
                        act.wait_ge(S["rsum"], q - 1)
                    fn(sq[:, q % 2, :], mid[:, CQ0 + q, :], ACT.Square).then_inc(S["rsq"], 1)
                act.wait_ge(S["rsum"], 3 * a + nt)
                inv_root((rstd, ssacc)[a][:, :], ps[6][:, :], MLA_RANKS[a], S["rln"], S["rr"], a + 1)
            for q in range(5):
                act.wait_ge(S["rt"], q + 1)
                act.copy(lat_hi(q), mid[:, CQ0 + q, :]).then_inc(S["rhi"], 1)
            act.wait_ge(S["ba_e"], 1)
            baT = small[:, 9, 0:32].rearrange("p (b n) -> p b n", n=8)
            fn(gd("t1").rearrange("p (b n) -> p b n", n=4), baT[:, :, 0:4], ACT.Exp, scale=-1.0).then_inc(S["gate_a"], 1)
            fn(gd("t2"), gd("t0"), ACT.Exp, scale=-1.0).then_inc(S["gate_a"], 1)
            fn(cols[:, 0:4], vec[:, VEC["g_alog"]:VEC["g_alog"] + 4], ACT.Exp).then_inc(S["gate_a"], 1)
            with act.Fori(0, 3) as i:
                for j in range(4):
                    t = mid[:, bass.ds(i * 4 + j, 1), :].rearrange("p a n -> p (a n)")
                    act.wait_ge(S["evin_free"], 4 + EV_FIRST + j + 1 + i * 4)
                    fn(t, t, ACT.Silu).then_inc(S["evsilu"], 1)
            for t in range(8):
                act.wait_ge(S["evsilu"], t + 1)
                fn(mid[:, L2 + t, :], mid[:, t, :], ACT.Square).then_inc(S["l2sq"], 1)
            for t in range(8):
                act.wait_ge(S["l2sum"], t + 1)
                fn(mid[:, L2 + t, :], ps[4 + t % 4][:, :], ACT.Ln, bias=epsc[:, 0:1]).then_inc(S["l2ln"], 1)
            for t in range(8):
                act.wait_ge(S["l2ln"], t + 1)
                fn(mid[:, L2 + t, :], mid[:, L2 + t, :], ACT.Exp, scale=-0.5,
                   bias=epsc[:, 1:2] if t < HEADS else epsc[:, 2:3]).then_inc(S["l2r"], 1)
            act.wait_ge(S["gcols"], 1)
            fn(gd("ke"), gd("t0"), ACT.Exp).then_inc(S["gate_a"], 1)
            fn(gd("egl"), gd("glast"), ACT.Exp).then_inc(S["gate_a"], 1)
            fn(gd("eg"), gd("gc"), ACT.Exp).then_inc(S["gate_a"], 1)
            act.wait_ge(S["gate_a"], 6)
            for k in range(HEADS):
                j = EV_FIRST + GDN_TILES + k
                act.wait_ge(unit_done, used(PHASES["ev_in"][0] + j))
                fn(mid[:, Z0 + k, :], ps[j % 4][:, :], ACT.Silu).then_inc(S["z_silu"], 1)
            for h in range(HEADS):
                act.wait_ge(S["hd_ps"], 2 * h + 1)
                if h >= 2:
                    act.wait_ge(S["hd_free"], 4 * (h - 1))
                for b in range(NB):
                    c = 4 * b + h
                    last = fn(sq[:, h % 2, chunk(b)], ps[0][:, chunk(b)], ACT.Exp, scale=-1.0, bias=gd("gc")[:, c:c + 1])
                last.then_inc(S["hd_exp"], 1)
                for b in range(NB):
                    c = 4 * b + h
                    last = fn(gate_s[:, h % 2, chunk(b)], ps[1][:, chunk(b)], ACT.Exp, bias=gd("ngc")[:, c:c + 1])
                last.then_inc(S["hd_exp"], 1)
                fn(tmp[:, h % 2, :], ps[2][:, :], ACT.Exp).then_inc(S["hd_exp"], 1)
            for q in range(NQ):
                act.wait_ge(S["y_ps"], q + 1)
                act.copy(h_f[:, 8 + q % HEADS, :], ps[q % 2][:, :]).then_inc(S["y_sb"], 1)
            for b in range(NB):
                act.wait_ge(S["vn_ps"], b + 1)
                if b:
                    act.wait_ge(S["o_ps"], b)
                act.copy(tmp[:, 1, :], ps[1][:, :]).then_inc(S["vn_sb"], 1)
                act.wait_ge(S["o_ps"], b + 1)
                act.copy(mid[:, V0:V0 + HEADS, chunk(b)], ps[3][:, :].rearrange("p (h n) -> p h n", h=HEADS)
                         ).then_inc(S["o_sb"], 1)
            act.wait_ge(S["o_sb"], NB)
            for h in range(HEADS + 1):
                if h < HEADS:
                    if h >= 2:
                        act.wait_ge(S["osum"], h - 1)
                    fn(sq[:, h % 2, :], mid[:, V0 + h, :], ACT.Square).then_inc(S["osq"], 1)
                    act.wait_ge(S["osum"], h + 1)
                    if h >= 2:
                        act.wait_ge(S["ot"], h - 1)
                    inv_root(gate_s[:, h % 2, :], ps[4 + h % 2][:, :], P, S["oln"], S["orr"], h + 1)
                if h >= 1:
                    act.wait_ge(S["ot"], h)
                    act.copy(h_hi[:, h - 1, :], tmp[:, (h - 1) % 2, :]).then_inc(S["ohi"], 1)
            scale = float((128 + 64) ** -0.5)
            for q in range(len(att_seq) + 1):
                if q < len(att_seq):
                    h, b = att_seq[q]
                    nk = (b + 1) * CH
                    act.wait_ge(S["sc_mask"], q + 1)
                    if q >= 2:
                        act.wait_ge(S["pt_ps"], q - 1)
                    fn(mid[:, q % 2, 0:nk], ps[q % 2][:, 0:nk], ACT.Exp, bias=cols[:, 6 + q % 2:7 + q % 2],
                       scale=scale, accum_out=cols[:, 8 + q % 2:9 + q % 2]).then_inc(S["sc_exp"], 1)
                if q >= 1:
                    r = q - 1
                    h, b = att_seq[r]
                    nk = (b + 1) * CH
                    act.wait_ge(S["pt_ps"], r + 1)
                    if r >= 2:
                        act.wait_ge(S["av_ps"], r - 1)
                    act.copy(mid[:, 2 + r % 2, 0:nk], ps[2 + r % 2][:, 0:nk]).then_inc(S["pt_sb"], 1)
                    if b == NB - 1:
                        act.wait_ge(S["av_ps"], NB * (h + 1))
                        act.copy(h_hi[:, 4 + h, :], ps[4 + h % 2][:, :]).then_inc(S["av_hi"], 1)
            for m in range(KT):
                if m == KT - 1:
                    first_hi("up1", 0)
                squares(2, m, 0)
            first_hi("up1", 1)
            norm(2)
            ffn_up(1)
            ffn_down(1, 3, "up2")
            norm(3)
            ffn_up(2)
            ffn_down(2, 4, None)
            norm(4)
            with act.Fori(0, 6) as i:
                for j in range(4):
                    t = mid[:, bass.ds(i * 4 + j, 1), :].rearrange("p a n -> p (a n)")
                    act.wait_ge(S["odin_free"], 4 + 1 + j + 1 + i * 4)
                    fn(t, t, ACT.Silu).then_inc(S["odsilu"], 1)
            act.wait_ge(S["dt_e"], 1)
            fn(sd("t2"), sd("t1"), ACT.Exp, scale=-1.0).then_inc(S["dt_a"], 1)
            fn(sd("t3")[:, 0:SSD_H], vec[:, VEC["s_alog"]:VEC["s_alog"] + SSD_H], ACT.Exp).then_inc(S["dt_a"], 1)
            for k in range(SSD_XT):
                n_odd = 1 + SSD_CONV + k
                act.wait_ge(unit_done, used(PHASES["od_in"][0] + n_odd))
                fn(mid[:, SZ0 + k, :], ps[n_odd % 4][:, :], ACT.Silu).then_inc(S["z_free"], 1)
                if k == 3:
                    act.wait_ge(S["acl_d"], 1)
                    fn(sd("de"), sd("t1"), ACT.Exp).then_inc(S["acl_a"], 1)
                    fn(sd("cd"), sd("t0"), ACT.Exp).then_inc(S["acl_a"], 1)
                elif 9 <= k < 9 + SSD_G:
                    g = k - 9
                    act.wait_ge(S["cb_ps"], g + 1)
                    act.copy(mid[:, B0 + g, :], ps[6 + g % 2][:, :]).then_inc(S["cb_sb"], 1)

            def ssd_L(h):
                act.wait_ge(S["L_ps"], h + 1)
                if h >= 2:
                    act.wait_ge(S["G_sb"], h - 1)
                for b in range(NB):
                    c = SSD_H * b + h
                    last = fn(tmp[:, h % 2, chunk(b)], ps[h % 2][:, chunk(b)], ACT.Exp, bias=sd("nacs")[:, c:c + 1])
                last.then_inc(S["L_sb"], 1)

            def ssd_E(j):
                act.wait_ge(S["E_ps"], j + 1)
                if j >= 2:
                    act.wait_ge(S["y_done"], j - 1)
                fn(sq[:, j % 2, CH:SEQ], ps[2][:, CH:SEQ], ACT.Exp).then_inc(S["E_sb"], 1)

            def ssd_square(j):
                act.wait_ge(S["y_done"], j + 1)
                fn(mid[:, SZ0 + j, :], mid[:, j, :], ACT.Square).then_inc(S["ysq"], 1)

            def group_root(g):
                act.wait_ge(S["ysum"], g + 1)
                inv_root(mid[:, SZ0 + 4 * g + 1, :], ps[2][:, :], 4 * P, S["yln"], S["yrr"], g + 1)
            ssd_L(0)
            ssd_L(1)
            ssd_E(0)
            for j in range(SSD_XT):
                if j + 1 < SSD_XT:
                    ssd_L(2 * j + 2)
                    ssd_L(2 * j + 3)
                    ssd_E(j + 1)
                if j:
                    ssd_square(j - 1)
                if j % 4 == 2 and j > 3:
                    group_root(j // 4 - 1)
            ssd_square(SSD_XT - 1)
            for q in range(SSD_XT):
                if q == 6:
                    group_root(SSD_G - 1)
                act.wait_ge(S["yt"], q + 1)
                act.copy(mid_hi[:, q, :], h_f[:, q, :]).then_inc(S["yhi"], 1)
            for m in range(KT):
                if m == KT - 1:
                    first_hi("up3", 0)
                squares(5, m, 0)
            first_hi("up3", 1)
            norm(5)
            ffn_up(3)
            ffn_down(3, 6, None)
            norm(6)

        @block.vector
        def _(dve):
            tt, ts, stt = dve.tensor_tensor, dve.tensor_scalar, dve.scalar_tensor_tensor
            step = Tally(dve_step)

            def own(ins):
                step.inc(ins)
                dve.wait_ge(step.sem, step.n)

            for sm, k in ((x_ready, KT), (ada_done, 2), (ss_add, 2), (prod_done, 2), (S["evin_free"], 4),
                          (S["odin_free"], 4)):
                dve.sem_inc(sm, k)
            dve.memset(epsc[:, 0:1], EPS)
            dve.memset(epsc[:, 1:2], float(-0.5 * np.log(128.0)))
            dve.memset(epsc[:, 2:3], 0.0)
            dve.wait_ge(const_in, 16 * 10)
            dve.tensor_copy(ident_b[:, :], ident[:, :])
            dve.tensor_copy(neg_b[:, :], tmp[:, 0, 0:P])
            dve.tensor_copy(pos_b[:, :], tmp[:, 0, P:2 * P])
            dve.tensor_copy(lvl[:, :, :].rearrange("p a n -> p (a n)"), lvl_in)
            own(tt(hstate[0:96, 0, 0:32], ident[0:96, 0:32], ident[0:96, 32:64], ALU.add))
            own(tt(pick[:, :], hstate[0:96, 0, 0:32], ident[0:96, 64:96], ALU.add))
            own(dve.memset(ssacc[:, :], 0.0))
            dve.sem_inc(consts, 1)

            def add_square(n, m, dm):
                dve.wait_ge(sq_done, KT * n + m + 1 + dm)
                dve.wait_ge(ss_add, KT * n + m + 2 + dm)
                tt(ssacc[:, :], ssacc[:, :], sq[:, m % 2, :], ALU.add).then_inc(ss_add, 1)

            def ada_group(g0, gi):
                s = g0 % 2
                dve.wait_ge(ada_full[s], 16 * (g0 // 2 + 1) + gi * 8)
                dve.wait_ge(mod_sum, g0 + 1 + gi)
                acc = ada_acc[:, s, :]
                own(ts(acc, ada_sb[:, s, 0, :], cact[:, 0:1], None, ALU.mult))
                for k in range(1, KT):
                    ins = stt(out=acc, in0=ada_sb[:, s, k, :], scalar=cact[:, k:k + 1], in1=acc, op0=ALU.mult, op1=ALU.add)
                    if k < KT - 1:
                        own(ins)
                ins.then_inc(ada_done, 1)

            def take_mod(s, last):
                dve.wait_ge(mod_sum, ADA_G * (last + 1) + 2)
                c = slice(24 * s, 24 * s + 24)
                b0 = VEC["ada_b"] + 24 * s
                own(tt(mod[:, c], ps[6][:, c], vec[:, b0:b0 + 24], ALU.add))
                g0 = VEC["norm_g"] + KT * s
                own(stt(out=moda[:, KT * s:KT * s + KT], in0=mod[:, 24 * s + 8:24 * s + 16], scalar=1.0,
                        in1=vec[:, g0:g0 + KT], op0=ALU.add, op1=ALU.mult))
                if s not in (1, 4):
                    g = mod[:, 24 * s + 16:24 * s + 24]
                    own(ts(g, g, 0.5, None, ALU.mult))

            def residual(nv, bank, m, dm):
                xm = one(x[:, bass.ds(m + dm, 1), :])
                g0 = 24 * (nv - 1) + 16 + m
                stt(out=xm, in0=bank, scalar=mod[:, bass.ds(g0 + dm, 1)], in1=xm, op0=ALU.mult, op1=ALU.add
                    ).then_inc(x_ready, 1)

            def norm(n):
                dve.wait_ge(rstd_ready, n + 1)
                if n == 6:
                    for kt in range(KT):
                        stt(out=mid[:, kt, :], in0=x[:, kt, :], scalar=vcol("final_g", kt), in1=rstd[:, :],
                            op0=ALU.mult, op1=ALU.mult).then_inc(out_ready, 1)
                    return

                def low(kt):
                    dve.wait_ge(hhi_done, KT * n + kt + 1)
                    stt(out=h_lo[:, kt, :], in0=tmp[:, kt % 2, :], scalar=mod[:, 24 * n + kt:24 * n + kt + 1],
                        in1=h_hi[:, kt, :].bitcast(F32), op0=ALU.add, op1=ALU.subtract).then_inc(hlo_done, 1)
                for kt in range(KT):
                    if kt >= 2:
                        low(kt - 2)
                        dve.wait_ge(hlo_done, KT * n + kt - 1)
                    stt(out=tmp[:, kt % 2, :], in0=x[:, kt, :], scalar=moda[:, KT * n + kt:KT * n + kt + 1], in1=rstd[:, :],
                        op0=ALU.mult, op1=ALU.mult).then_inc(ht_ready, 1)
                low(KT - 2)
                low(KT - 1)

            def ffn_up(f):
                u0, n, nk = PHASES[f"up{f}"]
                q0 = FT * f
                with dve.Fori(0, n // 4) as i:
                    for t in range(2):
                        dve.wait_ge(silu_done, q0 + t + 1 + i * 2)
                        dve.wait_ge(unit_done, used(u0 + 2 * t + 1) + i * 4)
                        tt(tmp[:, t, :], gate_s[:, t, :], ps[2 * t + 1][:, :], ALU.mult).then_inc(prod_done, 1)
                        dve.wait_ge(midhi_done, q0 + t + 1 + i * 2)
                        k = bass.ds(i * 2 + t, 1)
                        tt(one(mid_lo[:, k, :]), tmp[:, t, :], one(mid_hi[:, k, :]).bitcast(F32), ALU.subtract
                           ).then_inc(midlo_done, 1)
                        dve.wait_ge(midlo_done, q0 + t + 1 + i * 2)

            def ffn_down(f):
                name = f"down{f}"
                u0 = PHASES[name][0]
                nv = {0: 1, 1: 3, 2: 4, 3: 6}[f]
                dve.wait_ge(ss_sum, nv)
                own(dve.memset(ssacc[:, :], 0.0))
                g0, per = ADA_AT.get(name, (0, 0))
                with dve.Fori(0, KT // 2) as i:
                    step.enter(i, per * (KT - 1))
                    for t in range(2):
                        for q in range(per // 2):
                            ada_group(g0 + t * (per // 2) + q, i * per)
                        dve.wait_ge(unit_done, used(u0 + 2 * t + 1) + i * 4)
                        residual(nv, ps[4 + t][:, :], t, i * 2)
                        add_square(nv, t, i * 2)
                    step.leave(KT // 2)
                made = {"down0": (1, 2), "down1": (3,), "down2": (4, 5)}.get(name, ())
                for s in made:
                    take_mod(s, made[-1])

            def conv(bank, t, tile, w, n_tiles, bias):
                def tap(j):
                    return vec[:, bass.ds(VEC[w] + j * n_tiles + tile, 1)]
                own(ts(t, bank, tap(3), None if bias is None else vec[:, bass.ds(VEC[bias] + tile, 1)],
                       ALU.mult, ALU.add) if bias is not None else ts(t, bank, tap(3), None, ALU.mult))
                for j in (2, 1, 0):
                    d = 3 - j
                    ins = stt(out=t[:, d:SEQ], in0=bank[:, 0:SEQ - d], scalar=tap(j), in1=t[:, d:SEQ],
                              op0=ALU.mult, op1=ALU.add)
                    if j:
                        own(ins)
                return ins

            def split_rows(bank, n, done):
                part = [slice(r, r + n) for r in (0, 32, 64)]
                own(dve.memset(decay_rows, 0.0))
                for r in part:
                    own(dve.tensor_copy(decay_rows[r, :], bank[r, :]))
                for r in part[1:]:
                    own(tt(sq[r, 0, :], bank[r, :], decay_rows[r, :], ALU.subtract))
                    own(dve.tensor_copy(decay_rows[r, :], sq[r, 0, :]))
                r = part[2]
                own(tt(sq[r, 0, :], sq[r, 0, :], decay_rows[r, :], ALU.subtract))
                dve.tensor_copy(decay_rows[r, :], sq[r, 0, :]).then_inc(done, 1)

            def softplus(dst, z, u, a, b, c, m):
                own(ts(a, u, 2.0, None, ALU.add))
                own(dve.reciprocal(b, a))
                own(tt(a, u, b, ALU.mult))
                own(tt(b, a, a, ALU.mult))
                own(ts(c, b, 1.0 / 15, None, ALU.mult))
                for k in (13, 11, 9, 7, 5, 3):
                    own(stt(out=c, in0=c, scalar=1.0 / k, in1=b, op0=ALU.add, op1=ALU.mult))
                own(stt(out=c, in0=c, scalar=1.0, in1=a, op0=ALU.add, op1=ALU.mult))
                own(ts(m, z, 0.0, None, ALU.max))
                own(stt(out=dst, in0=c, scalar=2.0, in1=m, op0=ALU.mult, op1=ALU.add))

            for m in range(KT):
                add_square(0, m, 0)
            dve.wait_ge(cact_done, 1)
            for g in range(ADA_G):
                ada_group(g, 0)
            take_mod(0, 0)
            norm(0)
            ang, k = rope_t, mid[:, MIDS - 1, :]
            own(dve.tensor_copy(ang, pos[:, :]))
            own(ts(ang, ang, vcol("inv_freq"), None, ALU.mult))
            c1 = 6.28125
            c2 = 4059.0 / 2097152
            c3 = 2 * np.pi - c1 - c2
            for a, r in enumerate((sine, cosine)):
                own(ts(k, ang, float(1 / (2 * np.pi)), 0.25 * a, ALU.mult, ALU.add))
                own(ts(k, k, ROUND, None, ALU.add))
                own(ts(k, k, ROUND, None, ALU.subtract))
                own(stt(out=r, in0=k, scalar=-c1, in1=ang, op0=ALU.mult, op1=ALU.add))
                own(stt(out=r, in0=k, scalar=-c2, in1=r, op0=ALU.mult, op1=ALU.add))
                own(stt(out=r, in0=k, scalar=float(-c3), in1=r, op0=ALU.mult, op1=ALU.add))
                own(ts(r, r, float(np.pi / 2) * a, None, ALU.add))
                ts(r, r, PI, -PI, ALU.min, ALU.max).then_inc(S["trig_d"], 1)
            ffn_up(0)
            ffn_down(0)
            norm(1)
            u0 = PHASES["ev_in"][0]
            for j in range(EV_FIRST):
                dve.wait_ge(unit_done, used(u0 + j))
                dst = rows if j == 0 else mid[:, CQ0 + j - 1, :] if j < 6 else mid[:, KPE, :]
                dve.tensor_copy(dst, ps[j % 4][:, :]).then_inc(S["evin_free"], 1)
            for q in range(5):
                dve.wait_ge(S["rr"], 1 if q < 3 else 2)
                gain = vcol("q_g", q) if q < 3 else vcol("kv_g", q - 3)
                t = mid[:, CQ0 + q, :]
                stt(out=t, in0=t, scalar=gain, in1=(rstd if q < 3 else ssacc)[:, :], op0=ALU.mult, op1=ALU.mult
                    ).then_inc(S["rt"], 1)
            for q in range(5):
                dve.wait_ge(S["rhi"], q + 1)
                tt(lat_lo(q), mid[:, CQ0 + q, :], lat_hi(q).bitcast(F32), ALU.subtract).then_inc(S["rlo"], 1)
            dve.wait_ge(S["ba_t"], 1)
            baT = small[:, 9, 0:32]
            own(dve.tensor_copy(baT, ps[7][:, 0:32]))
            baT = baT.rearrange("p (b n) -> p b n", n=8)

            def g4(ap):
                return ap.rearrange("p (b n) -> p b n", n=HEADS)

            def per_head(ap, n=HEADS):
                return ap.unsqueeze(1).to_broadcast([P, NB, n])
            own(tt(g4(gd("z")), baT[:, :, 4:8], per_head(vec[:, VEC["g_dtb"]:VEC["g_dtb"] + 4]), ALU.add))
            stt(out=gd("t0"), in0=gd("z"), scalar=-1.0, in1=gd("z"), op0=ALU.mult, op1=ALU.max).then_inc(S["ba_e"], 1)
            dve.wait_ge(S["gate_a"], 3)
            own(ts(gd("t1"), gd("t1"), 1.0, None, ALU.add))
            own(dve.reciprocal(gd("beta"), gd("t1")))
            softplus(gd("t3"), gd("z"), gd("t2"), gd("t1"), gd("t4"), gd("t5"), gd("t0"))
            stt(out=g4(gd("g")), in0=g4(gd("t3")), scalar=-1.0, in1=per_head(cols[:, 0:4]), op0=ALU.mult, op1=ALU.mult
                ).then_inc(S["g_done"], 1)
            with dve.Fori(0, 3) as i:
                step.enter(i, 12)
                for j in range(4):
                    dve.wait_ge(unit_done, used(u0 + EV_FIRST + j) + i * 4)
                    conv(ps[(EV_FIRST + j) % 4][:, :], one(mid[:, bass.ds(i * 4 + j, 1), :]), i * 4 + j, "gconv", GDN_TILES, None
                         ).then_inc(S["evin_free"], 1)
                step.leave(3)
            dve.wait_ge(S["gc_ps"], 1)
            dve.tensor_copy(gd("gc"), ps[4][:, 0:16]).then_inc(S["gc_sb"], 1)
            dve.wait_ge(S["gcrow_ps"], 1)
            split_rows(ps[5], HEADS, S["gcrow_sb"])
            dve.wait_ge(S["glast_ps"], 1)
            dve.wait_ge(S["gc_sb"], 1)
            own(dve.tensor_copy(gd("glast"), ps[6][:, 0:16]))
            own(tt(gd("t0"), gd("glast"), gd("gc"), ALU.subtract))
            own(ts(gd("nbeta"), gd("beta"), -1.0, None, ALU.mult))
            ts(gd("ngc"), gd("gc"), -1.0, None, ALU.mult).then_inc(S["gcols"], 1)
            for t in range(8):
                dve.wait_ge(S["l2r"], t + 1)
                tt(mid[:, t, :], mid[:, t, :], mid[:, L2 + t, :], ALU.mult).then_inc(S["l2done"], 1)
            for t in range(14):
                sm, v = pj_ready(t)
                dve.wait_ge(sm, v)
                if t == 0:
                    dve.wait_ge(S["l2done"], 8)
                dve.tensor_copy(mid[:, QN0 + t, :], ps[4 + t % 4][:, :]).then_inc(S["pj_free"], 1)
            dve.wait_ge(S["gate_a"], 6)
            own(tt(gd("nbe"), gd("nbeta"), gd("eg"), ALU.mult))
            for h in range(HEADS):
                dve.wait_ge(S["hd_ps"], 2 * h + 2)
                dve.wait_ge(S["hd_exp"], 3 * h + 1)
                for b in range(NB):
                    c = 4 * b + h
                    last = stt(out=h_f[:, h, chunk(b)], in0=ps[3][:, chunk(b)], scalar=gd("nbeta")[:, c:c + 1],
                               in1=sq[:, h % 2, chunk(b)], op0=ALU.mult, op1=ALU.mult)
                last.then_inc(S["hd_free"], 1)
                dve.wait_ge(S["hd_exp"], 3 * h + 3)
                tt(mid[:, AT0 + h, :], ps[4][:, :], gate_s[:, h % 2, :], ALU.mult).then_inc(S["hd_free"], 1)
                tt(mid[:, Q0 + h, :], mid[:, Q0 + h, :], tmp[:, h % 2, :], ALU.mult)
                for b in range(NB):
                    c = 4 * b + h
                    last = ts(h_f[:, 12 + h, chunk(b)], ps[5][:, chunk(b)], gd("ke")[:, c:c + 1], None, ALU.mult)
                last.then_inc(S["hd_free"], 1)
                for b in range(NB):
                    c = 4 * b + h
                    last = ts(mid[:, VB0 + h, chunk(b)], ps[6][:, chunk(b)], gd("beta")[:, c:c + 1], None, ALU.mult)
                last.then_inc(S["hd_free"], 1)
                if h < 3:
                    t = mid[:, (QPE0, QPE0 + 1, KPE)[h], :]
                    dve.wait_ge(S["trig_a"], 2)
                    dve.wait_ge(S["rot_ps"], h + 1)
                    if h:
                        dve.wait_ge(S["rope"], h)
                    own(tt(rope_t, ps[7][:, :], sine, ALU.mult))
                    own(tt(t, t, cosine, ALU.mult))
                    tt(t, t, rope_t, ALU.add).then_inc(S["rope"], 1)
            idb = ident[:, :].unsqueeze(1).to_broadcast([P, NB, P])

            def blocks(ap):
                return ap.rearrange("p (b n) -> p b n", b=NB)
            for h in range(HEADS):
                own(dve.tensor_copy(blocks(h_f[:, 4 + h, :]), idb))
                dve.tensor_copy(blocks(mid[:, MT0 + h, :]), idb).then_inc(S["inv_up"], 1)
            for q in range(NQ):
                lv, h = inv_seq[q]
                dve.wait_ge(S["z_ps"], q + 1)
                dve.wait_ge(S["inv_up"], q + 1)
                if lv < len(LEVELS) - 1:
                    m = lvl[:, 2 * lv:2 * lv + 1, :].to_broadcast([P, NB, P])
                    own(dve.copy_predicated(blocks(h_f[:, 4 + h, :]), m, blocks(ps[2 + q % 2][:, :])))
                m = lvl[:, 2 * lv + 1:2 * lv + 2, :].to_broadcast([P, NB, P])
                dve.copy_predicated(blocks(mid[:, MT0 + h, :]), m, blocks(ps[4 + q % 2][:, :])).then_inc(S["inv_up"], 1)
            for b in range(NB):
                if b:
                    dve.wait_ge(S["ks_ps"], b)
                    dve.wait_ge(S["vn_ps"], b)
                else:
                    dve.wait_ge(S["hd_free"], 4 * HEADS)
                for h in range(HEADS):
                    hc = slice(h * P, (h + 1) * P)
                    c = 4 * b + h
                    if b:
                        last = stt(out=tmp[:, 0, hc], in0=ps[0][:, hc], scalar=gd("nbe")[:, c:c + 1],
                                   in1=mid[:, VB0 + h, chunk(b)], op0=ALU.mult, op1=ALU.add)
                    else:
                        last = dve.tensor_copy(tmp[:, 0, hc], mid[:, VB0 + h, chunk(b)])
                last.then_inc(S["r_sb"], 1)
                if b < NB - 1:
                    dve.wait_ge(S["su_ps"], b + 1)
                    dve.wait_ge(S["o_ps"], b + 1)
                    if b:
                        dve.wait_ge(S["s_up"], b)
                    for h in range(HEADS):
                        hc = slice(h * P, (h + 1) * P)
                        c = 4 * b + h
                        if b:
                            last = stt(out=mid[:, ST, hc], in0=mid[:, ST, hc], scalar=gd("egl")[:, c:c + 1],
                                       in1=ps[2][:, hc], op0=ALU.mult, op1=ALU.add)
                        else:
                            last = dve.tensor_copy(mid[:, ST, hc], ps[2][:, hc])
                    last.then_inc(S["s_up"], 1)

            def out_low(h):
                dve.wait_ge(S["ohi"], h + 1)
                tt(h_lo[:, h, :], tmp[:, h % 2, :], h_hi[:, h, :].bitcast(F32), ALU.subtract).then_inc(S["olo"], 1)
            for h in range(HEADS):
                dve.wait_ge(S["orr"], h + 1)
                own(stt(out=tmp[:, h % 2, :], in0=mid[:, V0 + h, :], scalar=vcol("gdn_g"), in1=gate_s[:, h % 2, :],
                        op0=ALU.mult, op1=ALU.mult))
                tt(tmp[:, h % 2, :], tmp[:, h % 2, :], mid[:, Z0 + h, :], ALU.mult).then_inc(S["ot"], 1)
                out_low(h)
                dve.wait_ge(S["olo"], h + 1)
            scale = float((128 + 64) ** -0.5)
            for q in range(len(att_seq) + 1):
                if q < len(att_seq):
                    h, b = att_seq[q]
                    nk = (b + 1) * CH
                    dve.wait_ge(S["sc_ps"], q + 1)
                    own(tt(ps[q % 2][:, chunk(b)], ps[q % 2][:, chunk(b)], qmask[:, :], ALU.add))
                    own(dve.tensor_reduce(cols[:, 4 + q % 2:5 + q % 2], ps[q % 2][:, 0:nk], AX_X, ALU.max))
                    ts(cols[:, 6 + q % 2:7 + q % 2], cols[:, 4 + q % 2:5 + q % 2], -scale, None, ALU.mult
                       ).then_inc(S["sc_mask"], 1)
                if q >= 1:
                    r = q - 1
                    h, b = att_seq[r]
                    nk = (b + 1) * CH
                    dve.wait_ge(S["sc_exp"], r + 1)
                    own(dve.reciprocal(cols[:, 10 + r % 2:11 + r % 2], cols[:, 8 + r % 2:9 + r % 2]))
                    ts(mid[:, r % 2, 0:nk], mid[:, r % 2, 0:nk], cols[:, 10 + r % 2:11 + r % 2], None, ALU.mult
                       ).then_inc(S["sc_norm"], 1)
                    if b == NB - 1:
                        dve.wait_ge(S["av_hi"], h + 1)
                        tt(h_lo[:, 4 + h, :], ps[4 + h % 2][:, :], h_hi[:, 4 + h, :].bitcast(F32), ALU.subtract
                           ).then_inc(S["av_lo"], 1)
            u0 = PHASES["ev_out"][0]
            own(dve.memset(ssacc[:, :], 0.0))
            for m in range(KT):
                dve.wait_ge(unit_done, used(u0 + m))
                residual(2, ps[4 + m % 2][:, :], m, 0)
                add_square(2, m, 0)
            norm(2)
            ffn_up(1)
            ffn_down(1)
            norm(3)
            ffn_up(2)
            ffn_down(2)
            norm(4)
            u0 = PHASES["od_in"][0]
            dve.wait_ge(unit_done, used(u0))
            dve.tensor_copy(rows, ps[0][:, :]).then_inc(S["odin_free"], 1)
            with dve.Fori(0, 6) as i:
                step.enter(i, 12)
                for j in range(4):
                    dve.wait_ge(unit_done, used(u0 + 1 + j) + i * 4)
                    conv(ps[(1 + j) % 4][:, :], one(mid[:, bass.ds(i * 4 + j, 1), :]), i * 4 + j, "sconv", SSD_CONV, "sconv_b"
                         ).then_inc(S["odin_free"], 1)
                step.leave(6)
            dve.wait_ge(S["dt_t"], 1)

            def s32(ap):
                return ap.rearrange("p (b n) -> p b n", n=SSD_H)
            own(tt(s32(sd("t0")), s32(ps[4][:, 0:P]), per_head(vec[:, VEC["s_dtb"]:VEC["s_dtb"] + SSD_H], SSD_H), ALU.add))
            stt(out=sd("t1"), in0=sd("t0"), scalar=-1.0, in1=sd("t0"), op0=ALU.mult, op1=ALU.max).then_inc(S["dt_e"], 1)
            dve.wait_ge(S["dt_a"], 2)
            softplus(sd("dt"), sd("t0"), sd("t2"), sd("t1"), sd("de"), sd("cd"), sd("acs"))
            stt(out=s32(sd("da")), in0=s32(sd("dt")), scalar=-1.0, in1=per_head(sd("t3")[:, 0:SSD_H], SSD_H),
                op0=ALU.mult, op1=ALU.mult).then_inc(S["da_sb"], 1)
            dve.wait_ge(S["acs_ps"], 1)
            own(dve.tensor_copy(sd("acs"), ps[5][:, 0:P]))
            ts(sd("nacs"), sd("acs"), -1.0, None, ALU.mult).then_inc(S["acs_sb"], 1)
            dve.wait_ge(S["acr_ps"], 1)
            split_rows(ps[6], SSD_H, S["acr_sb"])
            dve.wait_ge(S["acl_ps"], 1)
            own(dve.tensor_copy(sd("t0"), ps[7][:, 0:P]))
            tt(sd("t1"), sd("t0"), sd("acs"), ALU.subtract).then_inc(S["acl_d"], 1)
            for b in range(NB - 1):
                dve.wait_ge(S["bt_ps"], 1 + b)
                dve.tensor_copy(mid[:, MIDS - 4 + b, :], ps[4 + b % 2][:, :]).then_inc(S["bt_sb"], 1)

            def heads8(ap):
                return ap.rearrange("p (r n) -> p r n", r=8)

            def by_head(ap):
                return ap.unsqueeze(2).to_broadcast([P, 8, 64])

            def xde(n):
                kind, g, b = aux_all[n]
                if kind == "state":
                    q, c = state_no(g, b), 32 * b + 8 * g
                    if q >= 2:
                        dve.wait_ge(S["aux_ps"], aux_all.index(("state", (q - 2) // 3, (q - 2) % 3)) + 1)
                    tt(heads8(xde_at(q)), heads8(xtok(g, b)), by_head(sd("de")[:, c:c + 8]), ALU.mult).then_inc(S["xde"], 1)

            def aux(n):
                kind, g, b = aux_all[n]
                dve.wait_ge(S["aux_ps"], n + 1)
                if kind == "tok":
                    tt(heads8(xtok(g, b)), heads8(aux_bank(n)[:, :]), by_head(sd("dt")[:, 32 * b + 8 * g:32 * b + 8 * g + 8]),
                       ALU.mult).then_inc(S["aux_sb"], 1)
                elif b:
                    c = 32 * b + 8 * g
                    own(tt(heads8(hst(g, b + 1)), heads8(hst(g, b)), by_head(sd("cd")[:, c:c + 8]), ALU.mult))
                    tt(hst(g, b + 1), hst(g, b + 1), aux_bank(n)[:, :], ALU.add).then_inc(S["aux_sb"], 1)
                else:
                    dve.tensor_copy(hst(g, 1), aux_bank(n)[:, :]).then_inc(S["aux_sb"], 1)
                dve.wait_ge(S["aux_sb"], n + 1)
            dve.wait_ge(S["acl_a"], 2)
            n_aux = len(aux_first)
            for n in range(NB):
                aux(n)
            xde(NB)
            xde(NB + 1)
            for n in range(NB, n_aux):
                aux(n)
                if n + 2 < n_aux:
                    xde(n + 2)
            for j in range(SSD_XT):
                for n in range(len(aux_of[j])):
                    aux(n_aux + n)
                n_aux += len(aux_of[j])
                dve.wait_ge(S["yo_ps"], j + 1)
                dve.wait_ge(S["E_sb"], j + 1)
                off = slice(CH, SEQ)
                e = sq[:, j % 2, off]
                tt(e, ps[6][:, off], e, ALU.mult).then_inc(S["yo_read"], 1)
                dve.wait_ge(S["yo_read"], j + 1)
                y = mid[:, j, :]
                stt(out=y, in0=y, scalar=vcol("ssd_d", j), in1=ps[4 + j % 2][:, :], op0=ALU.mult, op1=ALU.add
                    ).then_inc(S["yd_read"], 1)
                dve.wait_ge(S["yd_read"], j + 1)
                own(tt(y[:, off], y[:, off], e, ALU.add))
                tt(y, y, mid[:, SZ0 + j, :], ALU.mult).then_inc(S["y_done"], 1)
                for n in range(len(aux_of.get(j + 1, []))):
                    xde(n_aux + n)
            dve.wait_ge(S["y_done"], SSD_XT)

            def y_low(q):
                dve.wait_ge(S["yhi"], q + 1)
                tt(mid_lo[:, q, :], h_f[:, q, :], mid_hi[:, q, :].bitcast(F32), ALU.subtract).then_inc(S["ylo"], 1)
            for q in range(SSD_XT):
                if q % 4 == 0:
                    dve.wait_ge(S["yrr"], q // 4 + 1)
                stt(out=h_f[:, q, :], in0=mid[:, q, :], scalar=vcol("ssd_g", q), in1=mid[:, SZ0 + 4 * (q // 4) + 1, :],
                    op0=ALU.mult, op1=ALU.mult).then_inc(S["yt"], 1)
                if q >= 2:
                    y_low(q - 2)
            y_low(14)
            y_low(15)
            u0 = PHASES["od_out"][0]
            own(dve.memset(ssacc[:, :], 0.0))
            for m in range(KT):
                dve.wait_ge(unit_done, used(u0 + 2 * m + 1))
                residual(5, ps[4 + m % 2][:, :], m, 0)
                add_square(5, m, 0)
            norm(5)
            ffn_up(3)
            ffn_down(3)
            norm(6)


def kernel(**inputs):
    import concourse.bacc as bacc
    from concourse.bass_utils import run_bass_kernel_spmd as run

    def tiles(w):
        k, m = w.shape
        return np.ascontiguousarray(w.reshape(k // P, P, m // P, P).transpose(2, 1, 0, 3)).reshape(m // P, P, k)

    def cols(v):
        return v.reshape(-1, P).T

    def everywhere(v):
        return np.broadcast_to(v.reshape(1, -1), (P, v.size))

    a = {k: np.asarray(v) for k, v in inputs.items()}
    f32 = np.float32
    up, down = [], []
    for l in range(DEPTH):
        for j in range(2):
            up.append(np.stack([tiles(a["ffn_w1"][l, j]), tiles(a["ffn_w3"][l, j])], 1).reshape(2 * FT, P, KT * P))
            down.append(tiles(a["ffn_w2"][l, j]).reshape(KT, P, 2, 11 * P).transpose(0, 2, 1, 3).reshape(16, P, 11 * P))
    w = a["ev_w_in"][0]
    ev_in = np.concatenate([w[:, 2048:2056], np.zeros((D, P - 8), f32), w[:, 2056:2760], w[:, 2696:2760], w[:, 0:2048]], 1)
    w = a["mla_w_uq"][0]
    uq = np.concatenate([w[:, :, 0:P].reshape(-1, HEADS * P), w[:, :, P:].reshape(-1, HEADS * 64)], 1)
    uq = tiles(uq).reshape(3, 2, P, 3 * P).transpose(0, 2, 1, 3).reshape(3, P, 6 * P)
    w = a["mla_w_ukv"][0]
    ukv = np.stack([tiles(w[:, :, 0:P].reshape(-1, HEADS * P)).transpose(1, 0, 2).reshape(P, 8 * P),
                    w[:, :, P:].reshape(2, P, HEADS * P).transpose(1, 0, 2).reshape(P, 8 * P)])
    w = a["ssd_w_in"][0]
    od_in = np.concatenate([w[:, 5120:5152], np.zeros((D, P - 32), f32), w[:, 2048:5120], w[:, 0:2048]], 1)
    ada = np.concatenate([a["ada_w"][l].reshape(KT, P, 3 * ADA_G, ADA_COLS).transpose(2, 1, 0, 3).reshape(3 * ADA_G, P, KT * ADA_COLS)
                          for l in range(DEPTH)])
    i = np.arange(P)
    freq = (f32(10000.0) ** (-np.arange(32, dtype=f32) / f32(32))).astype(f32)
    vec = np.concatenate([
        cols(a["c"]), cols(a["ada_b"]), cols(a["norm_g"]), cols(a["final_g"]), cols(a["gdn_conv_w"]), cols(a["gdn_norm_g"]),
        cols(a["mla_q_norm_g"]), cols(a["mla_kv_norm_g"]), cols(a["ssd_conv_w"]), cols(a["ssd_conv_b"]),
        cols(np.repeat(a["ssd_D"][0], 64)), cols(a["ssd_norm_g"]), everywhere(a["gdn_A_log"]), everywhere(a["gdn_dt_bias"]),
        everywhere(a["ssd_A_log"]), everywhere(a["ssd_dt_bias"]), freq[i % 32].reshape(P, 1)], 1)
    assert vec.shape[1] == NVEC
    rot = np.zeros((P, P), f32)
    for m in range(P):
        if m % 64 < 32:
            rot[m + 32, m] = -1.0
        else:
            rot[m - 32, m] = 1.0
    lvl = []
    for s in LEVELS:
        m = ((i[:, None] // s) % 2 == 1) & (i[None, :] // s == i[:, None] // s - 1)
        lvl += [m, m.T]
    arrays = {
        "x": a["x"][0].T.reshape(KT, P, SEQ), "positions": a["positions"].astype(np.int32),
        "ada": ada, "up": np.stack(up), "down": np.stack(down), "ev_in": tiles(ev_in), "uq": uq, "ukv": ukv,
        "ev_out": tiles(a["ev_w_out"][0]), "od_in": tiles(od_in),
        "od_out": tiles(a["ssd_w_out"][0]).reshape(KT, P, 2, 8 * P).transpose(0, 2, 1, 3).reshape(16, P, 8 * P),
        "vec": vec, "ident": np.eye(P, dtype=f32), "ones": np.ones((P, P), f32),
        "tri": np.triu(np.ones((P, P), f32)), "rot": rot,
        "neg": np.where(i[None, :] >= i[:, None], 0.0, BIG_NEG).astype(f32),
        "pos_mask": np.where(i[None, :] < i[:, None], 0.0, -BIG_NEG).astype(f32),
        "qmask": np.where(i[None, :] // 64 <= i[:, None] // 64, 0.0, BIG_NEG).astype(f32),
        "lvl": np.stack(lvl, 1).astype(np.int32).reshape(P, -1),
    }
    nc = bacc.Bacc("TRN2", target_bir_lowering=False, num_devices=1, dynamic_dma_scratch_size=1024)
    arrays = {f"in_{k}": np.ascontiguousarray(v) for k, v in arrays.items()}
    src = {k[3:]: nc.dram_tensor(k, v.shape, mybir.dt.from_np(v.dtype), kind="ExternalInput").ap() for k, v in arrays.items()}
    out = nc.dram_tensor("out", (KT, P, SEQ), F32, kind="ExternalOutput").ap()
    build(nc, src, out, None)
    r = run(nc, [arrays], core_ids=[0])
    return np.ascontiguousarray(r.results[0]["out"].reshape(D, SEQ).T).reshape(1, SEQ, D)
```

```python
from contextlib import ExitStack

import numpy as np

import concourse.bass as bass
from concourse import mybir

F32 = mybir.dt.float32
F32R = mybir.dt.float32r
BF16 = mybir.dt.bfloat16
I32 = mybir.dt.int32
U8 = mybir.dt.uint8
ALU = mybir.AluOpType
ACT = mybir.ActivationFunctionType
AX_X = mybir.AxisListType.X

P = 128
D = 1024
SEQ = 512
DEPTH = 2
D_FF = 2816
EPS = 1e-6
KT = D // P
FT = D_FF // P
CH = 128
NB = SEQ // CH
HEADS = 4
GDN_TILES = 3 * HEADS
EV_FIRST = 1 + 3 + 2 + 1
EV_TILES = EV_FIRST + GDN_TILES + HEADS
MLA_RANKS = (384, 256)
SSD_H = 32
SSD_G = 4
SSD_XT = 16
SSD_CONV = SSD_XT + 2 * SSD_G
OD_TILES = 1 + SSD_CONV + SSD_XT
RAW, HL = 4, 2
BIG_NEG = -3.0e38
LEVELS = [1, 2, 4, 8, 16, 32, 64]
PI = float(np.float32(3.1415925))
ROUND = 12582912.0

PHASES, _u = {}, 0
for _name, _n, _nk in (
        ("up0", 2 * FT, 8), ("down0", 16, 11),
        ("ev_in", EV_TILES, 8), ("uq", 3, 6), ("ukv", 2, 8), ("ev_out", 8, 8),
        ("up1", 2 * FT, 8), ("down1", 16, 11), ("up2", 2 * FT, 8), ("down2", 16, 11),
        ("od_in", OD_TILES, 8), ("od_out", 16, 8),
        ("up3", 2 * FT, 8), ("down3", 16, 11)):
    PHASES[_name] = (_u, _n, _nk)
    _u += _n

HI_AT, _a, _p = {}, 0, 0
for _name, (_u, _n, _nk) in PHASES.items():
    if _name[:2] in ("up", "do"):
        HI_AT[_name] = (_a, None)
        _a += _n
    else:
        HI_AT[_name] = (None, _p)
        _p += _n

ADA_COLS = 384
ADA_G = 3 * D // ADA_COLS
ADA_SLOTS = KT * ADA_COLS // SEQ
ADA_NORM = -(-2 * D // ADA_COLS)
ADA_AT = {"down0": (8, 4), "down1": (24, 2), "down2": (32, 4)}

VEC, _c = {}, 0
for _name, _n in (("c", 8), ("ada_b", 144), ("norm_g", 48), ("final_g", 8), ("gconv", 48), ("gdn_g", 1),
                  ("q_g", 3), ("kv_g", 2), ("sconv", 96), ("sconv_b", 24), ("ssd_d", 16), ("ssd_g", 16),
                  ("g_alog", 4), ("g_dtb", 4), ("s_alog", 32), ("s_dtb", 32), ("inv_freq", 1)):
    VEC[_name] = _c
    _c += _n
NVEC = _c

Q0, K0, V0, Z0, VB0, ST, QN0, QPE0, KN0, VM0, KPE, MT0, AT0 = 0, 4, 8, 12, 16, 20, 21, 25, 27, 31, 35, 36, 40
LAT_HI, CQ0, L2 = 16, 36, 21
B0, C0, SZ0 = 16, 20, 24
MIDS = 44
NT0 = MIDS - KT


class Tally:

    def __init__(self, sem, n=0):
        self.sem, self.n, self.k = sem, n, 0

    def inc(self, ins):
        ins.then_inc(self.sem, 1)
        self.n = self.n + 1
        self.k += 1

    def enter(self, i, per):
        self.base, self.per, self.k0 = self.n, per, self.k
        self.n = self.base + i * per

    def leave(self, count):
        assert self.k - self.k0 == self.per, (self.k - self.k0, self.per)
        self.n = self.base + count * self.per


def one(ap):
    return ap.rearrange("p a n -> p (a n)")


def build(nc, src, out):
    ctx = ExitStack()
    with ctx:
        def sb(name, shape, dt=F32):
            return ctx.enter_context(nc.sbuf_tensor(name, shape, dt))

        def sem(name):
            return ctx.enter_context(nc.semaphore(name))

        with nc.sbuf_tensor("h_f", [P, 16, SEQ], F32) as h_f:
            pass
        with nc.sbuf_tensor("ada_w_sb", [P, 2, KT, ADA_COLS], F32) as ada_sb:
            pass
        h_hi = sb("h_hi", [P, KT, SEQ], F32R)
        h_lo = sb("h_lo", [P, KT, SEQ], F32R)
        with nc.sbuf_tensor("mid_f", [P, MIDS, SEQ], F32) as mid:
            pass
        mid_hi = sb("mid_hi", [P, FT, SEQ], F32R)
        mid_lo = sb("mid_lo", [P, FT, SEQ], F32R)

        x = sb("x_sb", [P, KT, SEQ])
        raw = sb("weight_raw", [P, RAW, 11 * P])
        whi = sb("weight_hi", [P, HL, 11 * P], F32R)
        wlo = sb("weight_lo", [P, HL, 11 * P], F32R)
        ada_acc = sb("ada_acc", [P, 2, ADA_COLS])
        tmp = sb("tmp", [P, 2, SEQ])
        gate_s = sb("gate_s", [P, 2, SEQ])
        sq = sb("sq", [P, 2, SEQ])
        ssacc = sb("ssacc", [P, SEQ])
        rstd = sb("rstd", [P, SEQ])
        vec = sb("vec", [P, NVEC])
        mod = sb("mod", [P, 144])
        moda = sb("moda", [P, 48])
        cact = sb("cact", [P, KT])
        ident = sb("ident", [P, P])
        ones = sb("ones", [P, P])
        tri = sb("tri", [P, P])
        rot = sb("rot", [P, P])
        ident_b = sb("ident_b", [P, P], BF16)
        neg_b = sb("neg_b", [P, P], BF16)
        pos_b = sb("pos_b", [P, P], BF16)
        lvl = sb("lvl", [P, 2 * len(LEVELS), P], U8)
        qmask = sb("qmask", [P, P])
        pos = sb("pos", [P, SEQ], I32)
        small = sb("small", [P, 10, P])
        cols = sb("cols", [P, 16])
        hstate = sb("hstate", [P, NB - 1, SEQ])
        epsc = sb("epsc", [P, 4])
        pick = sb("pick", [96, 32], BF16)
        ps = [ctx.enter_context(nc.psum_tensor(f"bank{i}", [P, SEQ], F32)) for i in range(8)]

        const_in = sem("const_in"); vec_in = sem("vec_in"); eps_ready = sem("eps_ready"); ones_in = sem("ones_in"); x_in = sem("x_in"); stored = sem("stored")
        raw_full = [sem(f"raw_full{i}") for i in range(RAW)]
        hi_done = sem("weight_hi_done"); lo_done = sem("weight_lo_done")
        unit_done = sem("unit_done"); act_hi = sem("act_weight_hi")
        ada_full = [sem("ada_full0"), sem("ada_full1")]
        ada_first_full = [sem(f"ada_first_full{g}") for g in range(ADA_G)]
        ada_done = sem("ada_acc_done"); mod_sum = sem("mod_summed")
        consts = sem("consts_ready"); cact_done = sem("cact_done")
        x_ready = sem("x_ready"); sq_done = sem("sq_done"); ss_add = sem("ss_add"); ss_sum = sem("ss_summed")
        rstd_ready = sem("rstd_ready"); ln_ready = sem("ln_ready")
        ht_ready = sem("h_scaled"); hhi_done = sem("h_hi_done"); hlo_done = sem("h_lo_done")
        silu_done = sem("silu_done"); prod_done = sem("prod_done")
        midhi_done = sem("mid_hi_done"); midlo_done = sem("mid_lo_done")
        dve_step = sem("dve_step"); act_step = sem("act_step")
        out_ready = sem("out_ready")
        S = {}

        def named(*names):
            for n in names:
                S[n] = sem(n)

        named("evin_free", "evsilu", "z_silu", "gate_a", "l2sq", "l2ln", "l2sum", "l2r", "l2done", "ba_t", "ba_e", "g_done",
              "gc_ps", "gc_sb", "gcrow_ps", "gcrow_sb", "glast_ps", "gcols", 
              "rsq", "rsum", "rln", "rr", "rt", "rhi", "rlo", "pj_free",
              "pj_ps", "hd_ps", "hd_exp", "hd_free", 
              "y_ps", "y_sb", "z_ps", "inv_up", "inv_first", "q_scaled", "vb_sb",
              "ks_ps", "r_sb", "vn_ps", "vn_sb", "su_ps", "s_up", "o_ps", "o_sb",
              "osq", "osum", "oln", "orr", "ot", "ohi", "olo",
              "trig_a", "trig_d", "rot_ps", "rope", "sc_ps", "sc_mask", "sc_exp", "sc_norm", "pt_ps", "pt_sb",
              "av_ps", "av_hi", "av_lo", )
        named("odin_free", "odsilu", "z_free", "dt_t", "dt_a", "dt_e", "da_sb", "acs_ps", "acs_sb", "acr_ps", "acr_sb",
              "acl_ps", "acl_d", "acl_a", "bt_ps", "bt_sb", "cb_ps", "cb_sb", "xde", "aux_ps", "aux_sb",
              "L_ps", "L_sb", "G_sb", "E_ps", "E_sb", "yd_ps", "yd_read", "yo_ps", "yo_read", "y_done",
              "ysq", "yss", "ysum", "yln", "yrr", "yt", "yhi", "ylo")

        def vcol(name, i=0):
            return vec[:, VEC[name] + i:VEC[name] + i + 1]

        block = ctx.enter_context(nc.Block())

        def used(u):
            return u + 1 + HL

        def x_at(n, m):
            return KT * n + m + 1

        def ss_at(n, m):
            return KT * n + m + 1 + 2

        def gd(name):
            i = ["beta", "g", "gc", "nbeta", "nbe", "ke", "egl", "ngc", "eg", "glast", "z", "t0", "t1", "t2", "t3",
                 "t4", "t5"].index(name)
            return small[:, i // 8, (i % 8) * 16:(i % 8) * 16 + 16]

        def sd(name):
            return small[:, ["dt", "da", "acs", "nacs", "de", "cd", "t0", "t1", "t2", "t3"].index(name), :]

        rows = gate_s[:, 0, :]
        decay_rows = ssacc[0:96, :].bitcast(BF16)[:, 0:SEQ]
        acc_flat = ada_acc[:, :, :].rearrange("p a n -> p (a n)")[:, 0:SEQ]

        lvl_in = h_f[:, 12:16, :].rearrange("p a n -> p (a n)")[:, 0:2 * len(LEVELS) * P].bitcast(I32)

        def ada_first(g):
            slot = ADA_SLOTS * g if g <= ADA_NORM else 16
            return mid[:, slot:slot + ADA_SLOTS, :].rearrange("p a n -> p (a n)").rearrange("p (k n) -> p k n", k=KT)

        def norm_t(kt):
            return mid[:, NT0 + kt, :]

        def xde_at(q):
            return rstd[:, :] if q % 2 == 0 else acc_flat

        def hst(g, b):
            return h_f[:, 8 + 3 * (g % 2) + b - 1, :]

        def xtok(g, b):
            return h_f[:, 4 * (g % 2) + b, :]

        def g_at(h):
            return gate_s[:, h % 4, :] if h % 4 < 2 else h_f[:, 12 + h % 4, :]

        aux_first = [("tok", 0, b) for b in range(NB)] + [("state", 0, b) for b in range(NB - 1)]
        aux_of = {}
        for _g in range(SSD_G):
            for _t, _items in enumerate(((("tok", 0), ("tok", 1)), (("tok", 2), ("state", 0)), (("tok", 3), ("state", 1)),
                                         (("state", 2),))):
                aux_of[4 * _g + _t] = [(kind, _g + 1, b) for kind, b in _items] if _g + 1 < SSD_G else []
        aux_all = aux_first + [a for j in range(SSD_XT) for a in aux_of[j]]

        def aux_bank(n):
            return ps[3 if n % 2 == 0 else 7]

        def state_no(g, b):
            return 3 * g + b

        def chunk(b):
            return slice(b * CH, (b + 1) * CH)

        NQ = len(LEVELS) * HEADS
        inv_seq = [(lv, h) for lv in range(len(LEVELS)) for h in range(HEADS)]
        def lat_hi(q):
            return mid_hi[:, LAT_HI + q, :]

        def lat_lo(q):
            return mid_lo[:, CQ0 + q - FT, :]

        sine, cosine, rope_t = hstate[:, 0, :], hstate[:, 1, :], hstate[:, 2, :]
        att_seq = [(h, b) for h in range(HEADS) for b in range(NB)]
        NA = len(att_seq)
        PIECES = [(kind, b) for b in range(NB) for kind in ("old", "new", "out") if b or kind != "old"]
        PIECES += [("squares", 0), ("sums", 0), ("sums", 2), ("scale", 0), ("scale", 2), ("low", 0), ("low", 2)]
        probs = [rstd[:, :], ssacc[:, :]]
        probs_t = [acc_flat, rope_t]

        def pj_ready(t):
            u, v = PHASES["uq"][0], PHASES["ukv"][0]
            if t < 6:
                return (unit_done, used(u + t // 2)) if t % 2 else (S["pj_ps"], t // 2 + 1)
            if t < 10:
                return (unit_done, used(v)) if t == 9 else (S["pj_ps"], t - 6 + 4)
            return (unit_done, used(v + 1)) if t == 13 else (S["pj_ps"], t - 10 + 7)

        @block.sync
        def _(sp):
            def unit(u, w_ap, nk):
                u0, di = u
                s = u0 % RAW
                sp.wait_ge(lo_done, u0 + di + 1)
                sp.dma_start(raw[:, s, 0:nk * P], w_ap).then_inc(raw_full[s], 16)

            def run(name, w, f=None, extra=None):
                u0, n, nk = PHASES[name]
                n4 = n // 4 if n >= 8 else 0

                def at(j):
                    a = w[f] if f is not None else w
                    return a[bass.ds(j, 1), :, :].rearrange("a p n -> (a p) n")
                if n4:
                    with sp.Fori(0, n4) as i:
                        for j in range(4):
                            unit((u0 + j, i * 4), at(i * 4 + j), nk)
                            if extra:
                                extra(i, j)
                for j in range(4 * n4, n):
                    unit((u0 + j, 0), w[f, j] if f is not None else w[j], nk)

            def ada(g0, gi):
                sp.wait_ge(ada_done, g0 + gi + 1)
                sp.dma_start(ada_sb[:, g0 % 2, :, :],
                             src["ada"][bass.ds(g0 + gi, 1), :, :].rearrange("a p (k n) -> (a p) k n", k=KT)
                             ).then_inc(ada_full[g0 % 2], 16)

            def ada_extra(name):
                g0, per = ADA_AT[name]
                u0 = PHASES[name][0]

                def extra(i, j):
                    if j == 1:
                        sp.wait_ge(unit_done, used(u0 - 1))
                    if j in (1, 3):
                        h = per // 2
                        for q in range(h):
                            ada(g0 + (j // 2) * h + q, i * per)
                return extra

            def ada_start(g):
                sp.dma_start(ada_first(g), src["ada"][g].rearrange("p (k n) -> p k n", k=KT)).then_inc(ada_first_full[g], 16)
            sp.dma_start(vec[:, :], src["vec"]).then_inc(vec_in, 16)
            sp.dma_start(ones[:, :], src["ones"]).then_inc(ones_in, 16)
            for g in range(ADA_NORM):
                ada_start(g)
            u0, n, nk = PHASES["up0"]
            for j in range(4):
                sp.dma_start(raw[:, j, 0:nk * P], src["up"][0, j]).then_inc(raw_full[j], 16)
            sp.wait_ge(ada_done, ADA_NORM + 2)
            sp.wait_ge(hlo_done, KT)
            for g in range(ADA_NORM, ADA_G):
                ada_start(g)
            with sp.Fori(1, n // 4) as i:
                for j in range(4):
                    unit((u0 + j, i * 4), src["up"][0][bass.ds(i * 4 + j, 1), :, :].rearrange("a p n -> (a p) n"), nk)
            run("down0", src["down"], 0, ada_extra("down0"))
            run("ev_in", src["ev_in"])
            run("uq", src["uq"])
            run("ukv", src["ukv"])
            run("ev_out", src["ev_out"])
            run("up1", src["up"], 1)
            run("down1", src["down"], 1, ada_extra("down1"))
            run("up2", src["up"], 2)
            run("down2", src["down"], 2, ada_extra("down2"))
            run("od_in", src["od_in"])
            run("od_out", src["od_out"])
            run("up3", src["up"], 3)
            run("down3", src["down"], 3)
            for kt in range(KT):
                sp.wait_ge(out_ready, kt + 1)
                sp.dma_start(out[kt], mid[:, kt, :]).then_inc(stored, 16)
            sp.wait_ge(stored, 16 * KT)

        @block.gpsimd
        def _(pool):
            pool.wait_ge(ones_in, 16)
            pool.sem_inc(lo_done, RAW)

            def unit(u0, di, nk, a0, p0):
                s, h = u0 % RAW, u0 % HL
                if a0 is None:
                    pool.wait_ge(raw_full[s], (u0 // RAW + 1) * 16 + di * (16 // RAW))
                    pool.wait_ge(unit_done, u0 + di + 1)
                    pool.tensor_tensor(whi[:, h, 0:nk * P], raw[:, s, 0:nk * P], ones[:, 0:1].to_broadcast([P, nk * P]),
                                       ALU.mult).then_inc(hi_done, 1)
                    pool.wait_ge(hi_done, p0 + di + 1)
                else:
                    pool.wait_ge(act_hi, a0 + di + 1)
                pool.tensor_tensor(wlo[:, h, 0:nk * P], raw[:, s, 0:nk * P], whi[:, h, 0:nk * P].bitcast(F32),
                                   ALU.subtract).then_inc(lo_done, 1)

            def ssd_core():
                pool.wait_ge(S["cb_sb"], SSD_G)

                def add(j):
                    g, t = divmod(j, 4)
                    pool.wait_ge(S["ysq"], j + 1)
                    if t:
                        if t > 1:
                            pool.wait_ge(S["yss"], 3 * g + t - 1)
                        acc = mid[:, SZ0 + 4 * g, :]
                        pool.tensor_tensor(acc, acc, mid[:, SZ0 + j, :], ALU.add).then_inc(S["yss"], 1)
                for j in range(SSD_XT):
                    for h in (2 * j, 2 * j + 1):
                        pool.wait_ge(S["L_sb"], h + 1)
                        if h >= 4:
                            pool.wait_ge(S["yd_ps"], h - 3)
                        pool.tensor_tensor(g_at(h), tmp[:, h % 2, :], mid[:, B0 + h // 8, :], ALU.mult).then_inc(S["G_sb"], 1)
                    if j >= 2:
                        add(j - 2)
                add(SSD_XT - 2)
                add(SSD_XT - 1)

            def gdn_heads():
                pool.wait_ge(unit_done, used(PHASES["ukv"][0] + 1))
                idb = ident[:, :].unsqueeze(1).to_broadcast([P, NB, P])
                for h in range(HEADS):
                    for t in (h_f[:, 4 + h, :], mid[:, MT0 + h, :]):
                        pool.tensor_copy(t.rearrange("p (b n) -> p b n", b=NB), idb).then_inc(S["inv_first"], 1)
                    pool.wait_ge(S["hd_ps"], 2 * h + 2)
                    pool.wait_ge(S["hd_exp"], 3 * h + 3)
                    q = mid[:, Q0 + h, :]
                    pool.tensor_tensor(q, q, tmp[:, h % 2, :], ALU.mult).then_inc(S["q_scaled"], 1)
            for name, (u0, n, nk) in PHASES.items():
                n4 = n // 4 if n >= 8 else 0
                a0, p0 = HI_AT[name]

                def at(j, di):
                    unit(u0 + j, di, nk, None if a0 is None else a0 + j, None if p0 is None else p0 + j)
                first = 0
                if name == "ev_out":
                    gdn_heads()
                if name == "od_out":
                    at(0, 0)
                    at(1, 0)
                    ssd_core()
                    at(2, 0)
                    at(3, 0)
                    first = 1
                if n4:
                    with pool.Fori(first, n4) as i:
                        for j in range(4):
                            at(j, i * 4)
                for j in range(4 * n4, n):
                    at(j, 0)

        @block.tensor
        def _(pe):
            mm = pe.matmul
            pe.sem_inc(unit_done, HL)
            pe.sem_inc(mod_sum, 2)
            pe.wait_ge(ones_in, 16)

            def split_ready(u0, di):
                pe.wait_ge(lo_done, u0 + di + 1 + RAW)

            def passes(bank, u0, k, hi, lo, start, stop, w_at=None):
                s = u0 % HL
                c = slice(k * P, (k + 1) * P) if w_at is None else w_at
                mm(bank, wlo[:, s, c], hi, start=start, stop=False)
                mm(bank, whi[:, s, c], lo, start=False, stop=False)
                return mm(bank, whi[:, s, c], hi, start=False, stop=stop)

            def first_pair(u0, n):
                for w in range(2):
                    split_ready(u0 + w, 0)
                for k in range(KT):
                    c = slice(k * P, (k + 1) * P)
                    pe.wait_ge(hhi_done, KT * n + k + 1)
                    for w in range(2):
                        mm(ps[w][:, :], wlo[:, (u0 + w) % HL, c], h_hi[:, k, :], start=k == 0, stop=False)
                        mm(ps[w][:, :], whi[:, (u0 + w) % HL, c], h_hi[:, k, :], start=False, stop=False)
                for w in range(2):
                    for k in range(KT):
                        pe.wait_ge(hlo_done, KT * n + k + 1)
                        last = mm(ps[w][:, :], whi[:, (u0 + w) % HL, k * P:(k + 1) * P], h_lo[:, k, :], start=False, stop=k == KT - 1)
                    last.then_inc(unit_done, 1)

            def ffn_up(f):
                u0, n, nk = PHASES[f"up{f}"]
                q0 = FT * f

                def body(i, first):
                    for t in range(2):
                        pe.wait_ge(prod_done, q0 + i * 2 + t + 1)
                        if first and t == 0:
                            first_pair(u0, {0: 0, 1: 2, 2: 3, 3: 5}[f])
                            continue
                        for w in range(2):
                            uu = u0 + 2 * t + w
                            split_ready(uu, i * 4)
                            for k in range(KT):
                                last = passes(ps[2 * t + w][:, :], uu, k, h_hi[:, k, :], h_lo[:, k, :], k == 0, k == KT - 1)
                            last.then_inc(unit_done, 1)
                body(0, True)
                with pe.Fori(1, n // 4) as i:
                    body(i, False)

            def mod_group(g0, gi):
                pe.wait_ge(ada_done, g0 + gi + 1 + 2)
                for c in range(3):
                    last = mm(ps[6][:, bass.ds(3 * g0 + c + gi * 3, 1)],
                              ada_acc[:, g0 % 2, c * P:(c + 1) * P], ones[:, 0:1], start=True, stop=True)
                last.then_inc(mod_sum, 1)

            def ffn_down(f):
                name = f"down{f}"
                u0, n, nk = PHASES[name]
                nv = {0: 1, 1: 3, 2: 4, 3: 6}[f]

                def body(i, first):
                    for t in range(2):
                        pe.wait_ge(x_ready, x_at(nv, 0) + i * 2 + t - 2)
                        for w in range(2):
                            uu = u0 + 2 * t + w
                            split_ready(uu, i * 4)
                            if first and t == 0:
                                pe.wait_ge(midlo_done, FT * f + 11 * (w + 1))
                            for k in range(11):
                                kk = 11 * w + k
                                last = passes(ps[4 + t][:, :], uu, k, mid_hi[:, kk, :], mid_lo[:, kk, :], kk == 0, kk == 21)
                            last.then_inc(unit_done, 1)
                        if name in ADA_AT:
                            g0, per = ADA_AT[name]
                            for q in range(per // 2):
                                mod_group(g0 + t * (per // 2) + q, i * per)
                body(0, True)
                with pe.Fori(1, n // 4) as i:
                    body(i, False)

            def norm_sum(n):
                pe.wait_ge(ss_add, ss_at(n, KT - 1))
                mm(ps[7][:, :], ones[:, :], ssacc[:, :], start=True, stop=True).then_inc(ss_sum, 1)

            for g in range(ADA_NORM):
                mod_group(g, 0)
                if g in (ADA_NORM - 3, ADA_NORM - 2):
                    m0 = KT // 2 * (g - ADA_NORM + 3)
                    for m in range(m0, m0 + KT // 2):
                        pe.wait_ge(sq_done, m + 1)
                        mm(ps[7][:, :], ones[:, :], sq[:, m % 2, :], start=m == 0, stop=m == KT - 1).then_inc(ss_add, 1)
            ffn_up(0)
            pe.wait_ge(consts, 1)
            for g in range(ADA_NORM, ADA_G):
                mod_group(g, 0)
            ffn_down(0)
            norm_sum(1)
            u0, n, nk = PHASES["ev_in"]

            def proj_tile(u0, j, di, bank, free, freed):
                pe.wait_ge(free, freed + di + 1)
                split_ready(u0 + j, di)
                for k in range(KT):
                    last = passes(ps[bank][:, :], u0 + j, k, h_hi[:, k, :], h_lo[:, k, :], k == 0, k == KT - 1)
                last.then_inc(unit_done, 1)
            def latent_sum(a, nt):
                for t in range(nt):
                    q = 3 * a + t
                    pe.wait_ge(S["rsq"], q + 1)
                    if q >= 3:
                        pe.wait_ge(S["rln"], 1)
                    mm(ps[6][:, :], ones[:, :], sq[:, q % 2, :], start=t == 0, stop=t == nt - 1).then_inc(S["rsum"], 1)
            pe.wait_ge(S["evin_free"], 2)
            first_pair(u0, 1)
            for j in range(2, EV_FIRST):
                proj_tile(u0, j, 0, j % 4, S["evin_free"], j)
                if j == 4:
                    latent_sum(0, 3)
            for b in range(NB):
                last = pe.transpose(ps[7][:, 8 * b:8 * b + 8], rows[0:8, b * CH:(b + 1) * CH], ident[0:8, 0:8])
            last.then_inc(S["ba_t"], 1)
            latent_sum(1, 2)
            with pe.Fori(0, 3) as i:
                for j in range(4):
                    proj_tile(u0, EV_FIRST + j, i * 4, (EV_FIRST + j) % 4, S["evin_free"], EV_FIRST + j)

            def l2_sums(t0):
                for t in range(t0, t0 + 4):
                    pe.wait_ge(S["l2sq"], t + 1)
                    if t >= 4:
                        pe.wait_ge(S["l2ln"], t - 3)
                    mm(ps[4 + t % 4][:, :], ones[:, :], mid[:, L2 + t, :], start=True, stop=True).then_inc(S["l2sum"], 1)
            pe.wait_ge(S["g_done"], 1)
            mm(ps[4][:, 0:16], tri[:, :], gd("g"), start=True, stop=True).then_inc(S["gc_ps"], 1)
            for k in range(HEADS):
                j = EV_FIRST + GDN_TILES + k
                proj_tile(u0, j, 0, j % 4, S["evin_free"], j)
                if k == 0:
                    pe.wait_ge(S["gc_sb"], 1)
                    for r in (0, 32, 64):
                        for b in range(NB):
                            last = mm(ps[5][r:r + HEADS, chunk(b)], gd("gc")[:, HEADS * b:HEADS * (b + 1)], ident[:, :],
                                      start=True, stop=True)
                    last.then_inc(S["gcrow_ps"], 1)
                    mm(ps[6][:, 0:16], ident[:, P - 1:P].to_broadcast([P, P]), gd("gc"), start=True, stop=True
                       ).then_inc(S["glast_ps"], 1)
                elif k == 2:
                    pe.wait_ge(S["gcols"], 1)
                    pe.wait_ge(S["gcrow_sb"], 1)
                    l2_sums(0)
            l2_sums(4)
            u0 = PHASES["uq"][0]
            tile = 0

            def pj_bank():
                if tile >= 4:
                    pe.wait_ge(S["pj_free"], tile - 3)
                else:
                    pe.wait_ge(S["l2ln"], 5 + tile)
                return ps[4 + tile % 4][:, :]
            for j in range(3):
                split_ready(u0 + j, 0)
                for t in range(2):
                    bank = pj_bank()
                    for k in range(3):
                        if tile == 0:
                            pe.wait_ge(S["rlo"], k + 1)
                        last = passes(bank, u0 + j, 3 * t + k, lat_hi(k), lat_lo(k), k == 0, k == 2)
                    tile += 1
                    if t == 0:
                        last.then_inc(S["pj_ps"], 1)
                last.then_inc(unit_done, 1)
            u0 = PHASES["ukv"][0]
            split_ready(u0, 0)
            pe.wait_ge(S["rlo"], 5)
            for t in range(4):
                bank = pj_bank()
                for k in range(2):
                    last = passes(bank, u0, 2 * t + k, lat_hi(3 + k), lat_lo(3 + k), k == 0, k == 1)
                tile += 1
                last.then_inc(S["pj_ps"] if t < 3 else unit_done, 1)
            split_ready(u0 + 1, 0)
            s = (u0 + 1) % HL
            for b in range(NB):
                bank = pj_bank()
                for k in range(2):
                    c = slice(k * SEQ, (k + 1) * SEQ)
                    tok = chunk(b)
                    mm(bank, lat_lo(3 + k)[:, tok], whi[:, s, c], start=k == 0, stop=False)
                    mm(bank, lat_hi(3 + k)[:, tok], wlo[:, s, c], start=False, stop=False)
                    last = mm(bank, lat_hi(3 + k)[:, tok], whi[:, s, c], start=False, stop=k == 1)
                tile += 1
                last.then_inc(S["pj_ps"] if b < 3 else unit_done, 1)
            pe.wait_ge(S["z_silu"], HEADS)
            pe.wait_ge(S["l2done"], 8)
            pe.wait_ge(S["pj_free"], 14)
            for h in range(HEADS):
                sel = pick[:, h:h + 1].to_broadcast([96, P])
                kh, qh, vh = mid[:, K0 + h, :], mid[:, Q0 + h, :], mid[:, V0 + h, :]
                if h:
                    pe.wait_ge(S["hd_exp"], 3 * h)
                mm(ps[0][:, :], sel, decay_rows, start=True, stop=False)
                mm(ps[0][:, :], ident_b[:, :], pos_b[:, :].unsqueeze(1).to_broadcast([P, NB, P]), start=False, stop=True)
                mm(ps[1][:, :], sel, decay_rows, start=True, stop=False)
                mm(ps[1][:, :], ident_b[:, :], neg_b[:, :].unsqueeze(1).to_broadcast([P, NB, P]), start=False, stop=True)
                mm(ps[2][:, :], sel, decay_rows, start=True, stop=True).then_inc(S["hd_ps"], 1)
                if h:
                    pe.wait_ge(S["hd_free"], 3 * h)
                    pe.wait_ge(S["vb_sb"], h)
                for b in range(NB):
                    tok = chunk(b)
                    mm(ps[3][:, tok], kh[:, tok], kh[:, tok], start=True, stop=True)
                for b in range(NB):
                    tok = chunk(b)
                    mm(ps[4][:, tok], kh[:, tok], qh[:, tok], start=True, stop=True)
                for b in range(NB):
                    tok = chunk(b)
                    pe.transpose(ps[5][:, tok], kh[:, tok], ident[:, :])
                for b in range(NB):
                    tok = chunk(b)
                    last = pe.transpose(ps[6][:, tok], vh[:, tok], ident[:, :])
                last.then_inc(S["hd_ps"], 1)
                if h < 3:
                    if h:
                        pe.wait_ge(S["rope"], h)
                    mm(ps[7][:, :], rot[:, :], mid[:, (QPE0, QPE0 + 1, KPE)[h], :], start=True, stop=True).then_inc(S["rot_ps"], 1)
            pe.wait_ge(S["hd_free"], 3 * HEADS)
            pe.wait_ge(S["hd_exp"], 3 * HEADS)
            pe.wait_ge(S["inv_first"], 2 * HEADS)

            def inv_y(q):
                lv, h = inv_seq[q]
                if lv == 0:
                    return
                pe.wait_ge(S["inv_up"], q + 1 - HEADS)
                if q >= HEADS + 2:
                    pe.wait_ge(S["y_sb"], q - 1 - HEADS)
                for b in range(NB):
                    tok = chunk(b)
                    last = mm(ps[q % 2][:, tok], h_f[:, 0 + h, tok], mid[:, MT0 + h, tok], start=True, stop=True)
                last.then_inc(S["y_ps"], 1)

            def inv_z(q):
                lv, h = inv_seq[q]
                if q >= 2:
                    pe.wait_ge(S["inv_up"], q - 1)
                if lv == 0:
                    for b in range(NB):
                        last = pe.transpose(ps[4 + q % 2][:, chunk(b)], h_f[:, h, chunk(b)], ident[:, :])
                    last.then_inc(S["z_ps"], 1)
                    return
                pe.wait_ge(S["y_sb"], q + 1 - HEADS)
                for b in range(NB):
                    if lv < len(LEVELS) - 1:
                        tok = chunk(b)
                        mm(ps[2 + q % 2][:, tok], h_f[:, 8 + h, tok], h_f[:, 4 + h, tok], start=True, stop=True)
                for b in range(NB):
                    tok = chunk(b)
                    last = mm(ps[4 + q % 2][:, tok], h_f[:, 4 + h, tok], h_f[:, 8 + h, tok], start=True, stop=True)
                last.then_inc(S["z_ps"], 1)
            for q in range(NQ + 1):
                if q < NQ:
                    inv_y(q)
                if q >= 1:
                    inv_z(q - 1)
            pe.wait_ge(S["inv_up"], NQ)
            pe.wait_ge(S["rope"], 3)
            pe.wait_ge(S["q_scaled"], HEADS)

            def scan_piece(kind, b):
                tok = chunk(b)
                heads = [(h, slice(h * P, (h + 1) * P)) for h in range(HEADS)]
                if kind == "old":
                    pe.wait_ge(S["s_up"], b)
                    pe.wait_ge(S["o_sb"], b)
                    for h, hc in heads:
                        last = mm(ps[0][:, hc], mid[:, K0 + h, tok], mid[:, ST, hc], start=True, stop=True)
                    last.then_inc(S["ks_ps"], 1)
                elif kind == "new":
                    pe.wait_ge(S["r_sb"], b + 1)
                    for h, hc in heads:
                        last = mm(ps[0][:, hc], mid[:, MT0 + h, tok], tmp[:, 0, hc], start=True, stop=True)
                    last.then_inc(S["vn_ps"], 1)
                elif kind == "out":
                    pe.wait_ge(S["vn_sb"], b + 1)
                    if b < NB - 1:
                        for h, hc in heads:
                            last = mm(ps[1][:, hc], h_f[:, 12 + h, tok], tmp[:, 1, hc], start=True, stop=True)
                        last.then_inc(S["su_ps"], 1)
                    for h, hc in heads:
                        last = mm(ps[0][:, hc], tmp[:, 1, hc], mid[:, AT0 + h, tok], start=True, stop=b == 0)
                        if b:
                            last = mm(ps[0][:, hc], mid[:, ST, hc], mid[:, Q0 + h, tok], start=False, stop=True)
                    last.then_inc(S["o_ps"], 1)
                elif kind == "sums":
                    for h in (b, b + 1):
                        pe.wait_ge(S["osq"], h + 1)
                        if h >= 2:
                            pe.wait_ge(S["oln"], h - 1)
                        mm(ps[h % 2][:, :], ones[:, :], mid[:, Q0 + h, :], start=True, stop=True).then_inc(S["osum"], 1)

            def att_scores(q):
                h, b = att_seq[q]
                nk = (b + 1) * CH
                tok = chunk(b)
                half = slice(64 * (h % 2), 64 * (h % 2) + 64)
                if q >= 2:
                    pe.wait_ge(S["sc_exp"], q - 1)
                bank = ps[2 + q % 2][:, 0:nk]
                mm(bank, mid[:, QN0 + h, tok], mid[:, KN0 + h, 0:nk], start=True, stop=False)
                mm(bank, mid[half, QPE0 + h // 2, tok], mid[half, KPE, 0:nk], start=False, stop=True).then_inc(S["sc_ps"], 1)

            def att_turn(q):
                h, b = att_seq[q]
                pe.wait_ge(S["sc_norm"], q + 1)
                if q >= 2:
                    pe.wait_ge(S["pt_sb"], q - 1)
                for kb in range(b + 1):
                    last = pe.transpose(ps[4 + q % 2][:, chunk(kb)], probs[q % 2][:, chunk(kb)], ident[:, :])
                last.then_inc(S["pt_ps"], 1)

            def att_values(q):
                h, b = att_seq[q]
                pe.wait_ge(S["pt_sb"], q + 1)
                if b == 0 and h >= 2:
                    pe.wait_ge(S["av_lo"], h - 1)
                for kb in range(b + 1):
                    last = mm(ps[6 + h % 2][:, chunk(b)], mid[:, VM0 + kb, h * P:(h + 1) * P], probs_t[q % 2][:, chunk(kb)],
                              start=kb == 0, stop=kb == b)
                last.then_inc(S["av_ps"], 1)
            for q in range(max(NA + 2, len(PIECES))):
                if q < len(PIECES):
                    scan_piece(*PIECES[q])
                if q < NA:
                    att_scores(q)
                if 1 <= q <= NA:
                    att_turn(q - 1)
                if 2 <= q < NA + 2:
                    att_values(q - 2)
            u0 = PHASES["ev_out"][0]
            pe.wait_ge(S["olo"], HEADS)
            pe.wait_ge(S["av_lo"], HEADS)
            pe.wait_ge(S["av_hi"], HEADS)
            for m in range(KT):
                pe.wait_ge(x_ready, x_at(2, m) - 2)
                split_ready(u0 + m, 0)
                for k in range(KT):
                    last = passes(ps[4 + m % 2][:, :], u0 + m, k, h_hi[:, k, :], h_lo[:, (k + HEADS) % KT, :], k == 0, k == KT - 1)
                last.then_inc(unit_done, 1)
            norm_sum(2)
            ffn_up(1)
            ffn_down(1)
            norm_sum(3)
            ffn_up(2)
            ffn_down(2)
            norm_sum(4)
            u0, n, nk = PHASES["od_in"]
            pe.wait_ge(S["odin_free"], 2)
            first_pair(u0, 4)
            for j in range(2, 5):
                proj_tile(u0, j, 0, j % 4, S["odin_free"], j)
            with pe.Fori(1, 6) as i:
                for j in range(4):
                    proj_tile(u0, 1 + j, i * 4, (1 + j) % 4, S["odin_free"], 1 + j)
            for b in range(NB):
                last = pe.transpose(ps[4][:, 32 * b:32 * b + 32], rows[0:32, b * CH:(b + 1) * CH], ident[0:32, 0:32])
            last.then_inc(S["dt_t"], 1)

            def before_core(k):
                if k == 1:
                    pe.wait_ge(S["da_sb"], 1)
                    mm(ps[5][:, 0:P], tri[:, :], sd("da"), start=True, stop=True).then_inc(S["acs_ps"], 1)
                elif k == 2:
                    pe.wait_ge(S["acs_sb"], 1)
                    for r in (0, 32, 64):
                        for b in range(NB):
                            last = mm(ps[6][r:r + SSD_H, chunk(b)], sd("acs")[:, SSD_H * b:SSD_H * (b + 1)], ident[:, :],
                                      start=True, stop=True)
                    last.then_inc(S["acr_ps"], 1)
                    mm(ps[7][:, 0:P], ident[:, P - 1:P].to_broadcast([P, P]), sd("acs"), start=True, stop=True).then_inc(S["acl_ps"], 1)
                elif 4 <= k < 4 + NB - 1:
                    b = k - 4
                    pe.wait_ge(S["odsilu"], SSD_CONV)
                    if b >= 2:
                        pe.wait_ge(S["bt_sb"], b - 1)
                    for g in range(SSD_G):
                        last = pe.transpose(ps[4 + b % 2][:, g * P:(g + 1) * P], mid[:, B0 + g, chunk(b)], ident[:, :])
                    last.then_inc(S["bt_ps"], 1)
                elif 8 <= k < 8 + SSD_G:
                    g = k - 8
                    pe.wait_ge(S["acr_sb"], 1)
                    pe.wait_ge(S["acl_d"], 1)
                    if g >= 2:
                        pe.wait_ge(S["cb_sb"], g - 1)
                    for b in range(NB):
                        tok = chunk(b)
                        last = mm(ps[6 + g % 2][:, tok], mid[:, B0 + g, tok], mid[:, C0 + g, tok], start=True, stop=True)
                    last.then_inc(S["cb_ps"], 1)
            for k in range(SSD_XT):
                n_odd = 1 + SSD_CONV + k
                if k < 4:
                    proj_tile(u0, n_odd, 0, n_odd % 4, S["odin_free"], n_odd)
                else:
                    proj_tile(u0, n_odd, 0, n_odd % 4, S["z_free"], k - 4)
                before_core(k)
            pe.wait_ge(S["z_free"], SSD_XT)
            pe.wait_ge(S["cb_sb"], SSD_G)
            pe.wait_ge(S["bt_sb"], NB - 1)
            pe.wait_ge(S["acl_a"], 2)

            def ssd_L(h):
                if h >= 2:
                    pe.wait_ge(S["L_sb"], h - 1)
                mm(ps[h % 2][:, :], pick[:, h:h + 1].to_broadcast([96, P]), decay_rows, start=True, stop=False)
                mm(ps[h % 2][:, :], ident_b[:, :], neg_b[:, :].unsqueeze(1).to_broadcast([P, NB, P]), start=False, stop=True
                   ).then_inc(S["L_ps"], 1)

            def ssd_E(j):
                if j:
                    pe.wait_ge(S["E_sb"], j)
                if j % 4 == 0 and j > 4:
                    pe.wait_ge(S["yln"], j // 4 - 1)
                for par in range(2):
                    last = mm(ps[2][64 * par:64 * par + 64, CH:SEQ], pick[:, 2 * j + par:2 * j + par + 1].to_broadcast([96, 64]),
                              decay_rows[:, CH:SEQ], start=True, stop=True)
                last.then_inc(S["E_ps"], 1)

            def aux(n):
                kind, g, b = aux_all[n]
                if n >= 2:
                    pe.wait_ge(S["aux_sb"], n - 1)
                if kind == "tok":
                    for t in range(4):
                        last = pe.transpose(aux_bank(n)[:, t * P:(t + 1) * P], mid[:, 4 * g + t, chunk(b)], ident[:, :])
                else:
                    pe.wait_ge(S["xde"], state_no(g, b) + 1)
                    last = mm(aux_bank(n)[:, :], mid[:, MIDS - 4 + b, g * P:(g + 1) * P], xde_at(state_no(g, b)), start=True, stop=True)
                last.then_inc(S["aux_ps"], 1)

            def ssd_y(j):
                g = j // 4
                if j >= 2:
                    pe.wait_ge(S["yd_read"], j - 1)
                for par in range(2):
                    h = 2 * j + par
                    pe.wait_ge(S["G_sb"], h + 1)
                    for b in range(NB):
                        tok = chunk(b)
                        last = mm(ps[4 + j % 2][64 * par:64 * par + 64, tok], xtok(g, b)[:, (h % 8) * 64:(h % 8) * 64 + 64],
                                  g_at(h)[:, tok], start=True, stop=True)
                    last.then_inc(S["yd_ps"], 1)
                if j:
                    pe.wait_ge(S["yo_read"], j)
                for b in range(1, NB):
                    tok = chunk(b)
                    last = mm(ps[6][:, tok], hst(g, b)[:, (j % 4) * P:(j % 4 + 1) * P], mid[:, C0 + g, tok], start=True, stop=True)
                last.then_inc(S["yo_ps"], 1)

            def group_sum(g):
                pe.wait_ge(S["yss"], 3 * g + 3)
                pe.wait_ge(S["E_sb"], min(4 * g + 8, SSD_XT))
                mm(ps[2][:, :], ones[:, :], mid[:, SZ0 + 4 * g, :], start=True, stop=True).then_inc(S["ysum"], 1)
            ssd_L(0)
            ssd_L(1)
            ssd_E(0)
            for n in range(len(aux_first)):
                aux(n)
            n_aux = len(aux_first)
            pe.wait_ge(S["aux_sb"], n_aux)
            for j in range(SSD_XT):
                if j + 1 < SSD_XT:
                    ssd_L(2 * j + 2)
                    ssd_L(2 * j + 3)
                    ssd_E(j + 1)
                for n in range(len(aux_of[j])):
                    aux(n_aux)
                    n_aux += 1
                if j % 4 == 2 and j > 3:
                    group_sum(j // 4 - 1)
                if j % 4 == 0 and j:
                    pe.wait_ge(S["aux_sb"], n_aux - len(aux_of[j]))
                ssd_y(j)
            group_sum(SSD_G - 1)
            u0 = PHASES["od_out"][0]
            for m in range(KT):
                pe.wait_ge(x_ready, x_at(5, m) - 2)
                for w in range(2):
                    uu = u0 + 2 * m + w
                    split_ready(uu, 0)
                    for k in range(8):
                        kk = 8 * w + k
                        if m == 0:
                            pe.wait_ge(S["ylo"], kk + 1)
                        last = passes(ps[4 + m % 2][:, :], uu, k, mid_hi[:, kk, :], mid_lo[:, kk, :], kk == 0, kk == 15)
                    last.then_inc(unit_done, 1)
            norm_sum(5)
            ffn_up(3)
            ffn_down(3)
            norm_sum(6)

        @block.scalar
        def _(act):
            fn = act.activation
            step = Tally(act_step)
            for kt in range(KT):
                act.dma_start(x[:, kt, :], src["x"][kt]).then_inc(x_in, 16)
            for d, a in ((ident[:, :], src["ident"]), (tri[:, :], src["tri"]), (rot[:, :], src["rot"]), (qmask[:, :], src["qmask"]),
                         (tmp[:, 0, 0:P], src["neg"]), (tmp[:, 0, P:2 * P], src["pos_mask"]), (lvl_in, src["lvl"]),
                         (pos[:, :], src["positions"].to_broadcast([P, SEQ]))):
                act.dma_start(d, a).then_inc(const_in, 16)
            act.wait_ge(vec_in, 16)
            act.wait_ge(eps_ready, 1)
            fn(cact[:, :], vec[:, VEC["c"]:VEC["c"] + KT], ACT.Silu).then_inc(cact_done, 1)
            act.wait_ge(x_in, 16 * KT)

            def squares(n, m, dm):
                act.wait_ge(x_ready, x_at(n, m) + dm)
                act.wait_ge(ss_add, KT * n + m + 1 + dm)
                fn(sq[:, m % 2, :], x[:, bass.ds(m + dm, 1), :].rearrange("p a n -> p (a n)"), ACT.Square
                   ).then_inc(sq_done, 1)

            def inv_root(dst, bank, n_mean, read, ready, count):
                fn(dst, bank, ACT.Ln, bias=epsc[:, 0:1], scale=1.0 / n_mean).then_inc(read, 1)
                act.wait_ge(read, count)
                fn(dst, dst, ACT.Exp, scale=-0.5).then_inc(ready, 1)

            def norm(n):
                if n:
                    act.wait_ge(ss_sum, n)
                else:
                    act.wait_ge(ss_add, ss_at(0, KT - 1))
                inv_root(rstd[:, :], ps[7][:, :], D, ln_ready, rstd_ready, n + 1)
                if n < 6:
                    for kt in range(KT):
                        act.wait_ge(ht_ready, KT * n + kt + 1)
                        fn(h_hi[:, kt, :], norm_t(kt), ACT.Identity,
                           bias=mod[:, 24 * n + kt:24 * n + kt + 1]).then_inc(hhi_done, 1)

            def weight_hi(name, j, di=0):
                u0, n, nk = PHASES[name]
                s = (u0 + j) % RAW
                act.wait_ge(raw_full[s], ((u0 + j) // RAW + 1) * 16 + di * (16 // RAW))
                act.wait_ge(unit_done, u0 + j + di + 1)
                act.copy(whi[:, (u0 + j) % HL, 0:nk * P], raw[:, s, 0:nk * P]).then_inc(act_hi, 1)

            def ffn_up(f):
                name = f"up{f}"
                u0, n, nk = PHASES[name]
                q0 = FT * f

                def body(i, ahead):
                    for t in range(2):
                        ahead(i, t, 0)
                        act.wait_ge(unit_done, used(u0 + 2 * t) + i * 4)
                        act.wait_ge(prod_done, q0 + t + 1 + i * 2)
                        fn(gate_s[:, t, :], ps[2 * t][:, :], ACT.Silu).then_inc(silu_done, 1)
                        ahead(i, t, 1)
                        act.wait_ge(prod_done, q0 + t + 3 + i * 2)
                        act.copy(one(mid_hi[:, bass.ds(i * 2 + t, 1), :]), tmp[:, t, :]).then_inc(midhi_done, 1)
                with act.Fori(0, n // 4 - 1) as i:
                    body(i, lambda i, t, w: weight_hi(name, 2 * t + w + 2, i * 4))
                last = n // 4 - 1
                body(last, lambda i, t, w: weight_hi(name, n - 2 + w) if t == 0 else weight_hi(f"down{f}", w))

            def first_hi(following, w):
                if following:
                    weight_hi(following, w)

            def ffn_down(f, nv, following):
                name = f"down{f}"
                with act.Fori(0, KT // 2 - 1) as i:
                    for t in range(2):
                        weight_hi(name, 2 * t + 2, i * 4)
                        weight_hi(name, 2 * t + 3, i * 4)
                        squares(nv, t, i * 2)
                weight_hi(name, 14)
                weight_hi(name, 15)
                squares(nv, KT - 2, 0)
                first_hi(following, 0)
                squares(nv, KT - 1, 0)
                first_hi(following, 1)

            for m in range(KT):
                squares(0, m, 0)
            first_hi("up0", 0)
            first_hi("up0", 1)
            norm(0)
            ffn_up(0)
            for a in range(2):
                act.wait_ge(S["trig_d"], a + 1)
                fn((sine, cosine)[a], (sine, cosine)[a], ACT.Sin).then_inc(S["trig_a"], 1)
            ffn_down(0, 1, None)
            norm(1)
            for a, nt in enumerate((3, 2)):
                for t in range(nt):
                    q = 3 * a + t
                    act.wait_ge(S["evin_free"], 4 + 1 + q + 1)
                    if q >= 2:
                        act.wait_ge(S["rsum"], q - 1)
                    fn(sq[:, q % 2, :], mid[:, CQ0 + q, :], ACT.Square).then_inc(S["rsq"], 1)
                act.wait_ge(S["rsum"], 3 * a + nt)
                inv_root((rstd, ssacc)[a][:, :], ps[6][:, :], MLA_RANKS[a], S["rln"], S["rr"], a + 1)
            for q in range(5):
                act.wait_ge(S["rt"], q + 1)
                act.copy(lat_hi(q), mid[:, CQ0 + q, :]).then_inc(S["rhi"], 1)
            act.wait_ge(S["ba_e"], 1)
            baT = small[:, 9, 0:32].rearrange("p (b n) -> p b n", n=8)
            fn(gd("t1").rearrange("p (b n) -> p b n", n=4), baT[:, :, 0:4], ACT.Exp, scale=-1.0).then_inc(S["gate_a"], 1)
            fn(gd("t2"), gd("t0"), ACT.Exp, scale=-1.0).then_inc(S["gate_a"], 1)
            fn(cols[:, 0:4], vec[:, VEC["g_alog"]:VEC["g_alog"] + 4], ACT.Exp).then_inc(S["gate_a"], 1)
            with act.Fori(0, 3) as i:
                for j in range(4):
                    t = mid[:, bass.ds(i * 4 + j, 1), :].rearrange("p a n -> p (a n)")
                    act.wait_ge(S["evin_free"], 4 + EV_FIRST + j + 1 + i * 4)
                    fn(t, t, ACT.Silu).then_inc(S["evsilu"], 1)
            for t in range(8):
                act.wait_ge(S["evsilu"], t + 1)
                fn(mid[:, L2 + t, :], mid[:, t, :], ACT.Square).then_inc(S["l2sq"], 1)
            for t in range(8):
                act.wait_ge(S["l2sum"], t + 1)
                fn(mid[:, L2 + t, :], ps[4 + t % 4][:, :], ACT.Ln, bias=epsc[:, 0:1]).then_inc(S["l2ln"], 1)
            for t in range(8):
                act.wait_ge(S["l2ln"], t + 1)
                fn(mid[:, L2 + t, :], mid[:, L2 + t, :], ACT.Exp, scale=-0.5,
                   bias=epsc[:, 1:2] if t < HEADS else epsc[:, 2:3]).then_inc(S["l2r"], 1)
            act.wait_ge(S["gcols"], 1)
            fn(gd("ke"), gd("t0"), ACT.Exp).then_inc(S["gate_a"], 1)
            fn(gd("egl"), gd("glast"), ACT.Exp).then_inc(S["gate_a"], 1)
            fn(gd("eg"), gd("gc"), ACT.Exp).then_inc(S["gate_a"], 1)
            act.wait_ge(S["gate_a"], 6)
            for k in range(HEADS):
                j = EV_FIRST + GDN_TILES + k
                act.wait_ge(unit_done, used(PHASES["ev_in"][0] + j))
                fn(mid[:, Z0 + k, :], ps[j % 4][:, :], ACT.Silu).then_inc(S["z_silu"], 1)
            for h in range(HEADS):
                act.wait_ge(S["hd_ps"], 2 * h + 1)
                if h >= 2:
                    act.wait_ge(S["hd_free"], 3 * (h - 1))
                    act.wait_ge(S["q_scaled"], h - 1)
                for b in range(NB):
                    c = 4 * b + h
                    last = fn(sq[:, h % 2, chunk(b)], ps[0][:, chunk(b)], ACT.Exp, scale=-1.0, bias=gd("gc")[:, c:c + 1])
                last.then_inc(S["hd_exp"], 1)
                for b in range(NB):
                    c = 4 * b + h
                    last = fn(gate_s[:, h % 2, chunk(b)], ps[1][:, chunk(b)], ACT.Exp, bias=gd("ngc")[:, c:c + 1])
                last.then_inc(S["hd_exp"], 1)
                fn(tmp[:, h % 2, :], ps[2][:, :], ACT.Exp).then_inc(S["hd_exp"], 1)
                act.wait_ge(S["hd_ps"], 2 * h + 2)
                for b in range(NB):
                    c = 4 * b + h
                    last = fn(mid[:, VB0 + h, chunk(b)], ps[6][:, chunk(b)], ACT.Identity, scale=gd("beta")[:, c:c + 1])
                last.then_inc(S["vb_sb"], 1)
            for q in range(HEADS, NQ):
                act.wait_ge(S["y_ps"], q + 1 - HEADS)
                act.copy(h_f[:, 8 + q % HEADS, :], ps[q % 2][:, :]).then_inc(S["y_sb"], 1)
            scale = float((P + 64) ** -0.5)

            def scan_piece(kind, b):
                if kind == "new":
                    act.wait_ge(S["vn_ps"], b + 1)
                    if b:
                        act.wait_ge(S["o_ps"], b)
                    act.copy(tmp[:, 1, :], ps[0][:, :]).then_inc(S["vn_sb"], 1)
                elif kind == "out":
                    act.wait_ge(S["o_ps"], b + 1)
                    act.copy(mid[:, V0:V0 + HEADS, chunk(b)], ps[0][:, :].rearrange("p (h n) -> p h n", h=HEADS)
                             ).then_inc(S["o_sb"], 1)
                elif kind == "squares":
                    act.wait_ge(S["o_sb"], NB)
                    for h in range(HEADS):
                        fn(mid[:, Q0 + h, :], mid[:, V0 + h, :], ACT.Square).then_inc(S["osq"], 1)
                elif kind == "sums":
                    for h in (b, b + 1):
                        act.wait_ge(S["osum"], h + 1)
                        fn(mid[:, K0 + h, :], ps[h % 2][:, :], ACT.Ln, bias=epsc[:, 0:1], scale=1.0 / P).then_inc(S["oln"], 1)
                    if b:
                        for h in range(HEADS):
                            act.wait_ge(S["oln"], h + 1)
                            fn(mid[:, K0 + h, :], mid[:, K0 + h, :], ACT.Exp, scale=-0.5).then_inc(S["orr"], 1)
                elif kind == "low":
                    for h in (b, b + 1):
                        act.wait_ge(S["ot"], h + 1)
                        act.copy(h_hi[:, h, :], mid[:, K0 + h, :]).then_inc(S["ohi"], 1)
            for q in range(max(NA + 3, len(PIECES))):
                if q < len(PIECES):
                    scan_piece(*PIECES[q])
                if q < NA:
                    h, b = att_seq[q]
                    nk = (b + 1) * CH
                    act.wait_ge(S["sc_mask"], q + 1)
                    if q >= 2:
                        act.wait_ge(S["pt_ps"], q - 1)
                    fn(probs[q % 2][:, 0:nk], ps[2 + q % 2][:, 0:nk], ACT.Exp, bias=cols[:, 6 + q % 2:7 + q % 2],
                       scale=scale, accum_out=cols[:, 8 + q % 2:9 + q % 2]).then_inc(S["sc_exp"], 1)
                if 1 <= q <= NA:
                    r = q - 1
                    nk = (att_seq[r][1] + 1) * CH
                    act.wait_ge(S["pt_ps"], r + 1)
                    if r >= 2:
                        act.wait_ge(S["av_ps"], r - 1)
                    act.copy(probs_t[r % 2][:, 0:nk], ps[4 + r % 2][:, 0:nk]).then_inc(S["pt_sb"], 1)
                if 3 <= q < NA + 3 and att_seq[q - 3][1] == NB - 1:
                    h = att_seq[q - 3][0]
                    act.wait_ge(S["av_ps"], NB * (h + 1))
                    act.copy(h_hi[:, 4 + h, :], ps[6 + h % 2][:, :]).then_inc(S["av_hi"], 1)
            for m in range(KT):
                if m == KT - 1:
                    first_hi("up1", 0)
                squares(2, m, 0)
            first_hi("up1", 1)
            norm(2)
            ffn_up(1)
            ffn_down(1, 3, "up2")
            norm(3)
            ffn_up(2)
            ffn_down(2, 4, None)
            norm(4)
            with act.Fori(0, 6) as i:
                for j in range(4):
                    t = mid[:, bass.ds(i * 4 + j, 1), :].rearrange("p a n -> p (a n)")
                    act.wait_ge(S["odin_free"], 4 + 1 + j + 1 + i * 4)
                    fn(t, t, ACT.Silu).then_inc(S["odsilu"], 1)
            act.wait_ge(S["dt_e"], 1)
            fn(sd("t2"), sd("t1"), ACT.Exp, scale=-1.0).then_inc(S["dt_a"], 1)
            fn(sd("t3")[:, 0:SSD_H], vec[:, VEC["s_alog"]:VEC["s_alog"] + SSD_H], ACT.Exp).then_inc(S["dt_a"], 1)
            for k in range(SSD_XT):
                n_odd = 1 + SSD_CONV + k
                act.wait_ge(unit_done, used(PHASES["od_in"][0] + n_odd))
                fn(mid[:, SZ0 + k, :], ps[n_odd % 4][:, :], ACT.Silu).then_inc(S["z_free"], 1)
                if k == 3:
                    act.wait_ge(S["acl_d"], 1)
                    fn(sd("de"), sd("t1"), ACT.Exp).then_inc(S["acl_a"], 1)
                    fn(sd("cd"), sd("t0"), ACT.Exp).then_inc(S["acl_a"], 1)
                elif 9 <= k < 9 + SSD_G:
                    g = k - 9
                    act.wait_ge(S["cb_ps"], g + 1)
                    act.copy(mid[:, B0 + g, :], ps[6 + g % 2][:, :]).then_inc(S["cb_sb"], 1)

            def ssd_L(h):
                act.wait_ge(S["L_ps"], h + 1)
                if h >= 2:
                    act.wait_ge(S["G_sb"], h - 1)
                for b in range(NB):
                    c = SSD_H * b + h
                    last = fn(tmp[:, h % 2, chunk(b)], ps[h % 2][:, chunk(b)], ACT.Exp, bias=sd("nacs")[:, c:c + 1])
                last.then_inc(S["L_sb"], 1)

            def ssd_E(j):
                act.wait_ge(S["E_ps"], j + 1)
                if j >= 2:
                    act.wait_ge(S["y_done"], j - 1)
                fn(sq[:, j % 2, CH:SEQ], ps[2][:, CH:SEQ], ACT.Exp).then_inc(S["E_sb"], 1)

            def ssd_square(j):
                act.wait_ge(S["y_done"], j + 1)
                fn(mid[:, SZ0 + j, :], mid[:, j, :], ACT.Square).then_inc(S["ysq"], 1)

            def group_root(g):
                act.wait_ge(S["ysum"], g + 1)
                inv_root(mid[:, SZ0 + 4 * g + 1, :], ps[2][:, :], 4 * P, S["yln"], S["yrr"], g + 1)
            ssd_L(0)
            ssd_L(1)
            ssd_E(0)
            for j in range(SSD_XT):
                if j + 1 < SSD_XT:
                    ssd_L(2 * j + 2)
                    ssd_L(2 * j + 3)
                    ssd_E(j + 1)
                if j:
                    ssd_square(j - 1)
                if j % 4 == 2 and j > 3:
                    group_root(j // 4 - 1)
            ssd_square(SSD_XT - 1)
            for q in range(SSD_XT):
                if q == 6:
                    group_root(SSD_G - 1)
                act.wait_ge(S["yt"], q + 1)
                act.copy(mid_hi[:, q, :], h_f[:, q, :]).then_inc(S["yhi"], 1)
            for m in range(KT):
                if m == KT - 1:
                    first_hi("up3", 0)
                squares(5, m, 0)
            first_hi("up3", 1)
            norm(5)
            ffn_up(3)
            ffn_down(3, 6, None)
            norm(6)

        @block.vector
        def _(dve):
            tt, ts, stt = dve.tensor_tensor, dve.tensor_scalar, dve.scalar_tensor_tensor
            step = Tally(dve_step)

            def own(ins):
                step.inc(ins)
                dve.wait_ge(step.sem, step.n)

            for sm, k in ((x_ready, KT), (ada_done, 2), (ss_add, 2), (prod_done, 2), (S["evin_free"], 4),
                          (S["odin_free"], 4)):
                dve.sem_inc(sm, k)
            own(dve.memset(epsc[:, 0:1], EPS))
            own(dve.memset(epsc[:, 1:2], float(-0.5 * np.log(128.0))))
            dve.memset(epsc[:, 2:3], 0.0).then_inc(eps_ready, 1)
            def add_square(n, m, dm):
                dve.wait_ge(sq_done, KT * n + m + 1 + dm)
                dve.wait_ge(ss_add, KT * n + m + 2 + dm)
                tt(ssacc[:, :], ssacc[:, :], sq[:, m % 2, :], ALU.add).then_inc(ss_add, 1)

            def ada_group(g0, gi):
                s = g0 % 2
                if g0 < ADA_G:
                    dve.wait_ge(ada_first_full[g0], 16)
                    w = ada_first(g0)
                else:
                    dve.wait_ge(ada_full[s], 16 * ((g0 - ADA_G) // 2 + 1) + gi * 8)
                    w = ada_sb[:, s, :, :]
                dve.wait_ge(mod_sum, g0 + 1 + gi)
                acc = ada_acc[:, s, :]
                own(ts(acc, w[:, 0, :], cact[:, 0:1], None, ALU.mult))
                for k in range(1, KT):
                    ins = stt(out=acc, in0=w[:, k, :], scalar=cact[:, k:k + 1], in1=acc, op0=ALU.mult, op1=ALU.add)
                    if k < KT - 1:
                        own(ins)
                ins.then_inc(ada_done, 1)

            def take_mod(s, last):
                dve.wait_ge(mod_sum, ADA_G * (last + 1) + 2)
                c = slice(24 * s, 24 * s + 24)
                b0 = VEC["ada_b"] + 24 * s
                own(tt(mod[:, c], ps[6][:, c], vec[:, b0:b0 + 24], ALU.add))
                g0 = VEC["norm_g"] + KT * s
                own(stt(out=moda[:, KT * s:KT * s + KT], in0=mod[:, 24 * s + 8:24 * s + 16], scalar=1.0,
                        in1=vec[:, g0:g0 + KT], op0=ALU.add, op1=ALU.mult))
                if s not in (0, 1, 4):
                    g = mod[:, 24 * s + 16:24 * s + 24]
                    own(ts(g, g, 0.5, None, ALU.mult))

            def residual(nv, bank, m, dm):
                xm = one(x[:, bass.ds(m + dm, 1), :])
                g0 = 24 * (nv - 1) + 16 + m
                stt(out=xm, in0=bank, scalar=mod[:, bass.ds(g0 + dm, 1)], in1=xm, op0=ALU.mult, op1=ALU.add
                    ).then_inc(x_ready, 1)

            def norm(n):
                dve.wait_ge(rstd_ready, n + 1)
                if n == 6:
                    for kt in range(KT):
                        stt(out=mid[:, kt, :], in0=x[:, kt, :], scalar=vcol("final_g", kt), in1=rstd[:, :],
                            op0=ALU.mult, op1=ALU.mult).then_inc(out_ready, 1)
                    return

                for kt in range(KT):
                    stt(out=norm_t(kt), in0=x[:, kt, :], scalar=moda[:, KT * n + kt:KT * n + kt + 1], in1=rstd[:, :],
                        op0=ALU.mult, op1=ALU.mult).then_inc(ht_ready, 1)
                for kt in range(KT):
                    dve.wait_ge(hhi_done, KT * n + kt + 1)
                    stt(out=h_lo[:, kt, :], in0=norm_t(kt), scalar=mod[:, 24 * n + kt:24 * n + kt + 1],
                        in1=h_hi[:, kt, :].bitcast(F32), op0=ALU.add, op1=ALU.subtract).then_inc(hlo_done, 1)

            def ffn_up(f, between=()):
                u0, n, nk = PHASES[f"up{f}"]
                q0 = FT * f

                def body(i):
                    for t in range(2):
                        dve.wait_ge(silu_done, q0 + t + 1 + i * 2)
                        dve.wait_ge(unit_done, used(u0 + 2 * t + 1) + i * 4)
                        tt(tmp[:, t, :], gate_s[:, t, :], ps[2 * t + 1][:, :], ALU.mult).then_inc(prod_done, 1)
                        dve.wait_ge(midhi_done, q0 + t + 1 + i * 2)
                        k = bass.ds(i * 2 + t, 1)
                        tt(one(mid_lo[:, k, :]), tmp[:, t, :], one(mid_hi[:, k, :]).bitcast(F32), ALU.subtract
                           ).then_inc(midlo_done, 1)
                        dve.wait_ge(midlo_done, q0 + t + 1 + i * 2)
                for i, work in enumerate(between):
                    body(i)
                    work()
                with dve.Fori(len(between), n // 4) as i:
                    body(i)

            def ffn_down(f):
                name = f"down{f}"
                u0 = PHASES[name][0]
                nv = {0: 1, 1: 3, 2: 4, 3: 6}[f]
                if nv > 1:
                    dve.wait_ge(ss_sum, nv - 1)
                own(dve.memset(ssacc[:, :], 0.0))
                g0, per = ADA_AT.get(name, (0, 0))
                with dve.Fori(0, KT // 2) as i:
                    step.enter(i, per * (KT - 1))
                    for t in range(2):
                        for q in range(per // 2):
                            ada_group(g0 + t * (per // 2) + q, i * per)
                        dve.wait_ge(unit_done, used(u0 + 2 * t + 1) + i * 4)
                        residual(nv, ps[4 + t][:, :], t, i * 2)
                        add_square(nv, t, i * 2)
                    step.leave(KT // 2)
                made = {"down0": (1, 2), "down1": (3,), "down2": (4, 5)}.get(name, ())
                for s in made:
                    take_mod(s, made[-1])

            def conv(bank, t, tile, w, n_tiles, bias):
                def tap(j):
                    return vec[:, bass.ds(VEC[w] + j * n_tiles + tile, 1)]
                own(ts(t, bank, tap(3), None if bias is None else vec[:, bass.ds(VEC[bias] + tile, 1)],
                       ALU.mult, ALU.add) if bias is not None else ts(t, bank, tap(3), None, ALU.mult))
                for j in (2, 1, 0):
                    d = 3 - j
                    ins = stt(out=t[:, d:SEQ], in0=bank[:, 0:SEQ - d], scalar=tap(j), in1=t[:, d:SEQ],
                              op0=ALU.mult, op1=ALU.add)
                    if j:
                        own(ins)
                return ins

            def split_rows(bank, n, done):
                part = [slice(r, r + n) for r in (0, 32, 64)]
                own(dve.memset(decay_rows, 0.0))
                for r in part:
                    own(dve.tensor_copy(decay_rows[r, :], bank[r, :]))
                for r in part[1:]:
                    own(tt(sq[r, 0, :], bank[r, :], decay_rows[r, :], ALU.subtract))
                    own(dve.tensor_copy(decay_rows[r, :], sq[r, 0, :]))
                r = part[2]
                own(tt(sq[r, 0, :], sq[r, 0, :], decay_rows[r, :], ALU.subtract))
                dve.tensor_copy(decay_rows[r, :], sq[r, 0, :]).then_inc(done, 1)

            def softplus(dst, z, u, a, b, c, m):
                own(ts(a, u, 2.0, None, ALU.add))
                own(dve.reciprocal(b, a))
                own(tt(a, u, b, ALU.mult))
                own(tt(b, a, a, ALU.mult))
                own(ts(c, b, 1.0 / 15, None, ALU.mult))
                for k in (13, 11, 9, 7, 5, 3):
                    own(stt(out=c, in0=c, scalar=1.0 / k, in1=b, op0=ALU.add, op1=ALU.mult))
                own(stt(out=c, in0=c, scalar=1.0, in1=a, op0=ALU.add, op1=ALU.mult))
                own(ts(m, z, 0.0, None, ALU.max))
                own(stt(out=dst, in0=c, scalar=2.0, in1=m, op0=ALU.mult, op1=ALU.add))

            dve.wait_ge(cact_done, 1)
            dve.wait_ge(vec_in, 16)
            for g in range(ADA_NORM):
                ada_group(g, 0)
            dve.wait_ge(const_in, 16 * 8)
            dve.tensor_copy(ident_b[:, :], ident[:, :])
            dve.tensor_copy(neg_b[:, :], tmp[:, 0, 0:P])
            dve.tensor_copy(pos_b[:, :], tmp[:, 0, P:2 * P])
            dve.tensor_copy(lvl[:, :, :].rearrange("p a n -> p (a n)"), lvl_in)
            own(tt(hstate[0:96, 0, 0:32], ident[0:96, 0:32], ident[0:96, 32:64], ALU.add))
            own(tt(pick[:, :], hstate[0:96, 0, 0:32], ident[0:96, 64:96], ALU.add))
            own(dve.memset(ssacc[:, :], 0.0))
            dve.sem_inc(consts, 1)
            dve.wait_ge(mod_sum, ADA_NORM + 2)
            own(tt(mod[:, 0:16], ps[6][:, 0:16], vec[:, VEC["ada_b"]:VEC["ada_b"] + 16], ALU.add))
            own(stt(out=moda[:, 0:KT], in0=mod[:, 8:16], scalar=1.0, in1=vec[:, VEC["norm_g"]:VEC["norm_g"] + KT],
                    op0=ALU.add, op1=ALU.mult))
            norm(0)
            ang, k = rope_t, mid[:, MIDS - 1, :]
            c1 = 6.28125
            c2 = 4059.0 / 2097152
            c3 = 2 * np.pi - c1 - c2

            def trig(a):
                if a == 0:
                    own(dve.tensor_copy(ang, pos[:, :]))
                    own(ts(ang, ang, vcol("inv_freq"), None, ALU.mult))
                r = (sine, cosine)[a]
                own(ts(k, ang, float(1 / (2 * np.pi)), 0.25 * a, ALU.mult, ALU.add))
                own(ts(k, k, ROUND, None, ALU.add))
                own(ts(k, k, ROUND, None, ALU.subtract))
                own(stt(out=r, in0=k, scalar=-c1, in1=ang, op0=ALU.mult, op1=ALU.add))
                own(stt(out=r, in0=k, scalar=-c2, in1=r, op0=ALU.mult, op1=ALU.add))
                own(stt(out=r, in0=k, scalar=float(-c3), in1=r, op0=ALU.mult, op1=ALU.add))
                own(ts(r, r, float(np.pi / 2) * a, None, ALU.add))
                ts(r, r, PI, -PI, ALU.min, ALU.max).then_inc(S["trig_d"], 1)
            ffn_up(0, [lambda: trig(0), lambda: trig(1), lambda: ada_group(ADA_NORM, 0), lambda: ada_group(ADA_NORM + 1, 0)])
            dve.wait_ge(mod_sum, ADA_G + 2)
            own(tt(mod[:, 16:24], ps[6][:, 16:24], vec[:, VEC["ada_b"] + 16:VEC["ada_b"] + 24], ALU.add))
            own(ts(mod[:, 16:24], mod[:, 16:24], 0.5, None, ALU.mult))
            ffn_down(0)
            norm(1)
            u0 = PHASES["ev_in"][0]
            for j in range(EV_FIRST):
                dve.wait_ge(unit_done, used(u0 + j))
                dst = rows if j == 0 else mid[:, CQ0 + j - 1, :] if j < 6 else mid[:, KPE, :]
                dve.tensor_copy(dst, ps[j % 4][:, :]).then_inc(S["evin_free"], 1)
            for q in range(5):
                dve.wait_ge(S["rr"], 1 if q < 3 else 2)
                gain = vcol("q_g", q) if q < 3 else vcol("kv_g", q - 3)
                t = mid[:, CQ0 + q, :]
                stt(out=t, in0=t, scalar=gain, in1=(rstd if q < 3 else ssacc)[:, :], op0=ALU.mult, op1=ALU.mult
                    ).then_inc(S["rt"], 1)
            for q in range(5):
                dve.wait_ge(S["rhi"], q + 1)
                tt(lat_lo(q), mid[:, CQ0 + q, :], lat_hi(q).bitcast(F32), ALU.subtract).then_inc(S["rlo"], 1)
            dve.wait_ge(S["ba_t"], 1)
            baT = small[:, 9, 0:32]
            own(dve.tensor_copy(baT, ps[7][:, 0:32]))
            baT = baT.rearrange("p (b n) -> p b n", n=8)

            def g4(ap):
                return ap.rearrange("p (b n) -> p b n", n=HEADS)

            def per_head(ap, n=HEADS):
                return ap.unsqueeze(1).to_broadcast([P, NB, n])
            own(tt(g4(gd("z")), baT[:, :, 4:8], per_head(vec[:, VEC["g_dtb"]:VEC["g_dtb"] + 4]), ALU.add))
            stt(out=gd("t0"), in0=gd("z"), scalar=-1.0, in1=gd("z"), op0=ALU.mult, op1=ALU.max).then_inc(S["ba_e"], 1)
            dve.wait_ge(S["gate_a"], 3)
            own(ts(gd("t1"), gd("t1"), 1.0, None, ALU.add))
            own(dve.reciprocal(gd("beta"), gd("t1")))
            softplus(gd("t3"), gd("z"), gd("t2"), gd("t1"), gd("t4"), gd("t5"), gd("t0"))
            stt(out=g4(gd("g")), in0=g4(gd("t3")), scalar=-1.0, in1=per_head(cols[:, 0:4]), op0=ALU.mult, op1=ALU.mult
                ).then_inc(S["g_done"], 1)
            with dve.Fori(0, 3) as i:
                step.enter(i, 12)
                for j in range(4):
                    dve.wait_ge(unit_done, used(u0 + EV_FIRST + j) + i * 4)
                    conv(ps[(EV_FIRST + j) % 4][:, :], one(mid[:, bass.ds(i * 4 + j, 1), :]), i * 4 + j, "gconv", GDN_TILES, None
                         ).then_inc(S["evin_free"], 1)
                step.leave(3)
            dve.wait_ge(S["gc_ps"], 1)
            dve.tensor_copy(gd("gc"), ps[4][:, 0:16]).then_inc(S["gc_sb"], 1)
            dve.wait_ge(S["gcrow_ps"], 1)
            split_rows(ps[5], HEADS, S["gcrow_sb"])
            dve.wait_ge(S["glast_ps"], 1)
            dve.wait_ge(S["gc_sb"], 1)
            own(dve.tensor_copy(gd("glast"), ps[6][:, 0:16]))
            own(tt(gd("t0"), gd("glast"), gd("gc"), ALU.subtract))
            own(ts(gd("nbeta"), gd("beta"), -1.0, None, ALU.mult))
            ts(gd("ngc"), gd("gc"), -1.0, None, ALU.mult).then_inc(S["gcols"], 1)
            for t in range(8):
                dve.wait_ge(S["l2r"], t + 1)
                tt(mid[:, t, :], mid[:, t, :], mid[:, L2 + t, :], ALU.mult).then_inc(S["l2done"], 1)
            for t in range(14):
                sm, v = pj_ready(t)
                dve.wait_ge(sm, v)
                if t == 0:
                    dve.wait_ge(S["l2done"], 8)
                dve.tensor_copy(mid[:, QN0 + t, :], ps[4 + t % 4][:, :]).then_inc(S["pj_free"], 1)
            dve.wait_ge(S["gate_a"], 6)
            own(tt(gd("nbe"), gd("nbeta"), gd("eg"), ALU.mult))
            for h in range(HEADS):
                dve.wait_ge(S["hd_ps"], 2 * h + 2)
                dve.wait_ge(S["hd_exp"], 3 * h + 1)
                for b in range(NB):
                    c = 4 * b + h
                    last = stt(out=h_f[:, h, chunk(b)], in0=ps[3][:, chunk(b)], scalar=gd("nbeta")[:, c:c + 1],
                               in1=sq[:, h % 2, chunk(b)], op0=ALU.mult, op1=ALU.mult)
                last.then_inc(S["hd_free"], 1)
                dve.wait_ge(S["hd_exp"], 3 * h + 3)
                tt(mid[:, AT0 + h, :], ps[4][:, :], gate_s[:, h % 2, :], ALU.mult).then_inc(S["hd_free"], 1)
                for b in range(NB):
                    c = 4 * b + h
                    last = ts(h_f[:, 12 + h, chunk(b)], ps[5][:, chunk(b)], gd("ke")[:, c:c + 1], None, ALU.mult)
                last.then_inc(S["hd_free"], 1)
                if h < 3:
                    t = mid[:, (QPE0, QPE0 + 1, KPE)[h], :]
                    dve.wait_ge(S["trig_a"], 2)
                    dve.wait_ge(S["rot_ps"], h + 1)
                    if h:
                        dve.wait_ge(S["rope"], h)
                    own(tt(rope_t, ps[7][:, :], sine, ALU.mult))
                    own(tt(t, t, cosine, ALU.mult))
                    tt(t, t, rope_t, ALU.add).then_inc(S["rope"], 1)

            def blocks(ap):
                return ap.rearrange("p (b n) -> p b n", b=NB)
            dve.wait_ge(S["inv_first"], 2 * HEADS)
            for q in range(NQ):
                lv, h = inv_seq[q]
                dve.wait_ge(S["z_ps"], q + 1)
                if q >= HEADS:
                    dve.wait_ge(S["inv_up"], q + 1 - HEADS)
                if lv < len(LEVELS) - 1:
                    m = lvl[:, 2 * lv:2 * lv + 1, :].to_broadcast([P, NB, P])
                    z = h_f[:, h, :] if lv == 0 else ps[2 + q % 2][:, :]
                    own(dve.copy_predicated(blocks(h_f[:, 4 + h, :]), m, blocks(z)))
                m = lvl[:, 2 * lv + 1:2 * lv + 2, :].to_broadcast([P, NB, P])
                dve.copy_predicated(blocks(mid[:, MT0 + h, :]), m, blocks(ps[4 + q % 2][:, :])).then_inc(S["inv_up"], 1)
            scale = float((P + 64) ** -0.5)

            def right_side(b):
                if b:
                    dve.wait_ge(S["ks_ps"], b)
                    dve.wait_ge(S["vn_ps"], b)
                else:
                    dve.wait_ge(S["vb_sb"], HEADS)
                for h in range(HEADS):
                    hc = slice(h * P, (h + 1) * P)
                    c = 4 * b + h
                    if b:
                        last = stt(out=tmp[:, 0, hc], in0=ps[0][:, hc], scalar=gd("nbe")[:, c:c + 1],
                                   in1=mid[:, VB0 + h, chunk(b)], op0=ALU.mult, op1=ALU.add)
                    else:
                        last = dve.tensor_copy(tmp[:, 0, hc], mid[:, VB0 + h, chunk(b)])
                last.then_inc(S["r_sb"], 1)

            def scan_piece(kind, b):
                if kind == "old":
                    right_side(b)
                elif kind == "out" and b < NB - 1:
                    dve.wait_ge(S["su_ps"], b + 1)
                    dve.wait_ge(S["o_ps"], b + 1)
                    if b:
                        dve.wait_ge(S["s_up"], b)
                    for h in range(HEADS):
                        hc = slice(h * P, (h + 1) * P)
                        c = 4 * b + h
                        if b:
                            last = stt(out=mid[:, ST, hc], in0=mid[:, ST, hc], scalar=gd("egl")[:, c:c + 1],
                                       in1=ps[1][:, hc], op0=ALU.mult, op1=ALU.add)
                        else:
                            last = dve.tensor_copy(mid[:, ST, hc], ps[1][:, hc])
                    last.then_inc(S["s_up"], 1)
                elif kind == "scale":
                    for h in (b, b + 1):
                        dve.wait_ge(S["orr"], h + 1)
                        t = mid[:, K0 + h, :]
                        own(stt(out=t, in0=mid[:, V0 + h, :], scalar=vcol("gdn_g"), in1=t, op0=ALU.mult, op1=ALU.mult))
                        tt(t, t, mid[:, Z0 + h, :], ALU.mult).then_inc(S["ot"], 1)
                elif kind == "low":
                    for h in (b, b + 1):
                        dve.wait_ge(S["ohi"], h + 1)
                        tt(h_lo[:, 4 + h, :], mid[:, K0 + h, :], h_hi[:, h, :].bitcast(F32), ALU.subtract).then_inc(S["olo"], 1)
            right_side(0)
            for q in range(max(NA + 3, len(PIECES))):
                if q < len(PIECES):
                    scan_piece(*PIECES[q])
                if 1 <= q <= NA:
                    r = q - 1
                    nk = (att_seq[r][1] + 1) * CH
                    dve.wait_ge(S["sc_exp"], r + 1)
                    own(dve.reciprocal(cols[:, 10 + r % 2:11 + r % 2], cols[:, 8 + r % 2:9 + r % 2]))
                    ts(probs[r % 2][:, 0:nk], probs[r % 2][:, 0:nk], cols[:, 10 + r % 2:11 + r % 2], None, ALU.mult
                       ).then_inc(S["sc_norm"], 1)
                if q < NA:
                    h, b = att_seq[q]
                    nk = (b + 1) * CH
                    bank = ps[2 + q % 2]
                    dve.wait_ge(S["sc_ps"], q + 1)
                    own(tt(bank[:, chunk(b)], bank[:, chunk(b)], qmask[:, :], ALU.add))
                    own(dve.tensor_reduce(cols[:, 4 + q % 2:5 + q % 2], bank[:, 0:nk], AX_X, ALU.max))
                    ts(cols[:, 6 + q % 2:7 + q % 2], cols[:, 4 + q % 2:5 + q % 2], -scale, None, ALU.mult
                       ).then_inc(S["sc_mask"], 1)
                if 3 <= q < NA + 3 and att_seq[q - 3][1] == NB - 1:
                    h = att_seq[q - 3][0]
                    dve.wait_ge(S["av_hi"], h + 1)
                    tt(h_lo[:, h, :], ps[6 + h % 2][:, :], h_hi[:, 4 + h, :].bitcast(F32), ALU.subtract).then_inc(S["av_lo"], 1)
            u0 = PHASES["ev_out"][0]
            own(dve.memset(ssacc[:, :], 0.0))
            for m in range(KT):
                dve.wait_ge(unit_done, used(u0 + m))
                residual(2, ps[4 + m % 2][:, :], m, 0)
                add_square(2, m, 0)
            norm(2)
            ffn_up(1)
            ffn_down(1)
            norm(3)
            ffn_up(2)
            ffn_down(2)
            norm(4)
            u0 = PHASES["od_in"][0]
            dve.wait_ge(unit_done, used(u0))
            dve.tensor_copy(rows, ps[0][:, :]).then_inc(S["odin_free"], 1)
            with dve.Fori(0, 6) as i:
                step.enter(i, 12)
                for j in range(4):
                    dve.wait_ge(unit_done, used(u0 + 1 + j) + i * 4)
                    conv(ps[(1 + j) % 4][:, :], one(mid[:, bass.ds(i * 4 + j, 1), :]), i * 4 + j, "sconv", SSD_CONV, "sconv_b"
                         ).then_inc(S["odin_free"], 1)
                step.leave(6)
            dve.wait_ge(S["dt_t"], 1)

            def s32(ap):
                return ap.rearrange("p (b n) -> p b n", n=SSD_H)
            own(tt(s32(sd("t0")), s32(ps[4][:, 0:P]), per_head(vec[:, VEC["s_dtb"]:VEC["s_dtb"] + SSD_H], SSD_H), ALU.add))
            stt(out=sd("t1"), in0=sd("t0"), scalar=-1.0, in1=sd("t0"), op0=ALU.mult, op1=ALU.max).then_inc(S["dt_e"], 1)
            dve.wait_ge(S["dt_a"], 2)
            softplus(sd("dt"), sd("t0"), sd("t2"), sd("t1"), sd("de"), sd("cd"), sd("acs"))
            stt(out=s32(sd("da")), in0=s32(sd("dt")), scalar=-1.0, in1=per_head(sd("t3")[:, 0:SSD_H], SSD_H),
                op0=ALU.mult, op1=ALU.mult).then_inc(S["da_sb"], 1)
            dve.wait_ge(S["acs_ps"], 1)
            own(dve.tensor_copy(sd("acs"), ps[5][:, 0:P]))
            ts(sd("nacs"), sd("acs"), -1.0, None, ALU.mult).then_inc(S["acs_sb"], 1)
            dve.wait_ge(S["acr_ps"], 1)
            split_rows(ps[6], SSD_H, S["acr_sb"])
            dve.wait_ge(S["acl_ps"], 1)
            own(dve.tensor_copy(sd("t0"), ps[7][:, 0:P]))
            tt(sd("t1"), sd("t0"), sd("acs"), ALU.subtract).then_inc(S["acl_d"], 1)
            for b in range(NB - 1):
                dve.wait_ge(S["bt_ps"], 1 + b)
                dve.tensor_copy(mid[:, MIDS - 4 + b, :], ps[4 + b % 2][:, :]).then_inc(S["bt_sb"], 1)

            def heads8(ap):
                return ap.rearrange("p (r n) -> p r n", r=8)

            def by_head(ap):
                return ap.unsqueeze(2).to_broadcast([P, 8, 64])

            def xde(n):
                kind, g, b = aux_all[n]
                if kind == "state":
                    q, c = state_no(g, b), 32 * b + 8 * g
                    if q >= 2:
                        dve.wait_ge(S["aux_ps"], aux_all.index(("state", (q - 2) // 3, (q - 2) % 3)) + 1)
                    tt(heads8(xde_at(q)), heads8(xtok(g, b)), by_head(sd("de")[:, c:c + 8]), ALU.mult).then_inc(S["xde"], 1)

            def aux(n):
                kind, g, b = aux_all[n]
                dve.wait_ge(S["aux_ps"], n + 1)
                if kind == "tok":
                    tt(heads8(xtok(g, b)), heads8(aux_bank(n)[:, :]), by_head(sd("dt")[:, 32 * b + 8 * g:32 * b + 8 * g + 8]),
                       ALU.mult).then_inc(S["aux_sb"], 1)
                elif b:
                    c = 32 * b + 8 * g
                    own(tt(heads8(hst(g, b + 1)), heads8(hst(g, b)), by_head(sd("cd")[:, c:c + 8]), ALU.mult))
                    tt(hst(g, b + 1), hst(g, b + 1), aux_bank(n)[:, :], ALU.add).then_inc(S["aux_sb"], 1)
                else:
                    dve.tensor_copy(hst(g, 1), aux_bank(n)[:, :]).then_inc(S["aux_sb"], 1)
                dve.wait_ge(S["aux_sb"], n + 1)
            dve.wait_ge(S["acl_a"], 2)
            n_aux = len(aux_first)
            for n in range(NB):
                aux(n)
            xde(NB)
            xde(NB + 1)
            for n in range(NB, n_aux):
                aux(n)
                if n + 2 < n_aux:
                    xde(n + 2)
            for j in range(SSD_XT):
                for n in range(len(aux_of[j])):
                    aux(n_aux + n)
                n_aux += len(aux_of[j])
                for n in range(len(aux_of.get(j + 1, []))):
                    xde(n_aux + n)
                dve.wait_ge(S["yo_ps"], j + 1)
                dve.wait_ge(S["E_sb"], j + 1)
                off = slice(CH, SEQ)
                e = sq[:, j % 2, off]
                tt(e, ps[6][:, off], e, ALU.mult).then_inc(S["yo_read"], 1)
                dve.wait_ge(S["yo_read"], j + 1)
                y = mid[:, j, :]
                stt(out=y, in0=y, scalar=vcol("ssd_d", j), in1=ps[4 + j % 2][:, :], op0=ALU.mult, op1=ALU.add
                    ).then_inc(S["yd_read"], 1)
                dve.wait_ge(S["yd_read"], j + 1)
                own(tt(y[:, off], y[:, off], e, ALU.add))
                tt(y, y, mid[:, SZ0 + j, :], ALU.mult).then_inc(S["y_done"], 1)
            dve.wait_ge(S["y_done"], SSD_XT)

            def y_low(q):
                dve.wait_ge(S["yhi"], q + 1)
                tt(mid_lo[:, q, :], h_f[:, q, :], mid_hi[:, q, :].bitcast(F32), ALU.subtract).then_inc(S["ylo"], 1)
            for q in range(SSD_XT):
                if q % 4 == 0:
                    dve.wait_ge(S["yrr"], q // 4 + 1)
                stt(out=h_f[:, q, :], in0=mid[:, q, :], scalar=vcol("ssd_g", q), in1=mid[:, SZ0 + 4 * (q // 4) + 1, :],
                    op0=ALU.mult, op1=ALU.mult).then_inc(S["yt"], 1)
                if q >= 2:
                    y_low(q - 2)
            y_low(14)
            y_low(15)
            u0 = PHASES["od_out"][0]
            own(dve.memset(ssacc[:, :], 0.0))
            for m in range(KT):
                dve.wait_ge(unit_done, used(u0 + 2 * m + 1))
                residual(5, ps[4 + m % 2][:, :], m, 0)
                add_square(5, m, 0)
            norm(5)
            ffn_up(3)
            ffn_down(3)
            norm(6)


def kernel(**inputs):
    import concourse.bacc as bacc
    from concourse.bass_utils import run_bass_kernel_spmd as run

    def tiles(w):
        k, m = w.shape
        return np.ascontiguousarray(w.reshape(k // P, P, m // P, P).transpose(2, 1, 0, 3)).reshape(m // P, P, k)

    def cols(v):
        return v.reshape(-1, P).T

    def everywhere(v):
        return np.broadcast_to(v.reshape(1, -1), (P, v.size))

    a = {k: np.asarray(v) for k, v in inputs.items()}
    f32 = np.float32
    up, down = [], []
    for l in range(DEPTH):
        for j in range(2):
            up.append(np.stack([tiles(a["ffn_w1"][l, j]), tiles(a["ffn_w3"][l, j])], 1).reshape(2 * FT, P, KT * P))
            down.append(tiles(a["ffn_w2"][l, j]).reshape(KT, P, 2, 11 * P).transpose(0, 2, 1, 3).reshape(16, P, 11 * P))
    w = a["ev_w_in"][0]
    ev_in = np.concatenate([w[:, 2048:2056], np.zeros((D, P - 8), f32), w[:, 2056:2760], w[:, 2696:2760], w[:, 0:2048]], 1)
    w = a["mla_w_uq"][0]
    uq = np.concatenate([w[:, :, 0:P].reshape(-1, HEADS * P), w[:, :, P:].reshape(-1, HEADS * 64)], 1)
    uq = tiles(uq).reshape(3, 2, P, 3 * P).transpose(0, 2, 1, 3).reshape(3, P, 6 * P)
    w = a["mla_w_ukv"][0]
    ukv = np.stack([tiles(w[:, :, 0:P].reshape(-1, HEADS * P)).transpose(1, 0, 2).reshape(P, 8 * P),
                    w[:, :, P:].reshape(2, P, HEADS * P).transpose(1, 0, 2).reshape(P, 8 * P)])
    w = a["ssd_w_in"][0]
    od_in = np.concatenate([w[:, 5120:5152], np.zeros((D, P - 32), f32), w[:, 2048:5120], w[:, 0:2048]], 1)
    ada = np.concatenate([a["ada_w"][l].reshape(KT, P, 3 * ADA_G, ADA_COLS).transpose(2, 1, 0, 3).reshape(3 * ADA_G, P, KT * ADA_COLS)
                          for l in range(DEPTH)])
    i = np.arange(P)
    freq = (f32(10000.0) ** (-np.arange(32, dtype=f32) / f32(32))).astype(f32)
    vec = np.concatenate([
        cols(a["c"]), cols(a["ada_b"]), cols(a["norm_g"]), cols(a["final_g"]), cols(a["gdn_conv_w"]), cols(a["gdn_norm_g"]),
        cols(a["mla_q_norm_g"]), cols(a["mla_kv_norm_g"]), cols(a["ssd_conv_w"]), cols(a["ssd_conv_b"]),
        cols(np.repeat(a["ssd_D"][0], 64)), cols(a["ssd_norm_g"]), everywhere(a["gdn_A_log"]), everywhere(a["gdn_dt_bias"]),
        everywhere(a["ssd_A_log"]), everywhere(a["ssd_dt_bias"]), freq[i % 32].reshape(P, 1)], 1)
    assert vec.shape[1] == NVEC
    rot = np.zeros((P, P), f32)
    for m in range(P):
        if m % 64 < 32:
            rot[m + 32, m] = -1.0
        else:
            rot[m - 32, m] = 1.0
    lvl = []
    for s in LEVELS:
        m = ((i[:, None] // s) % 2 == 1) & (i[None, :] // s == i[:, None] // s - 1)
        lvl += [m, m.T]
    arrays = {
        "x": a["x"][0].T.reshape(KT, P, SEQ), "positions": a["positions"].astype(np.int32),
        "ada": ada, "up": np.stack(up), "down": np.stack(down), "ev_in": tiles(ev_in), "uq": uq, "ukv": ukv,
        "ev_out": tiles(a["ev_w_out"][0]), "od_in": tiles(od_in),
        "od_out": tiles(a["ssd_w_out"][0]).reshape(KT, P, 2, 8 * P).transpose(0, 2, 1, 3).reshape(16, P, 8 * P),
        "vec": vec, "ident": np.eye(P, dtype=f32), "ones": np.ones((P, P), f32),
        "tri": np.triu(np.ones((P, P), f32)), "rot": rot,
        "neg": np.where(i[None, :] >= i[:, None], 0.0, BIG_NEG).astype(f32),
        "pos_mask": np.where(i[None, :] < i[:, None], 0.0, -BIG_NEG).astype(f32),
        "qmask": np.where(i[None, :] // 64 <= i[:, None] // 64, 0.0, BIG_NEG).astype(f32),
        "lvl": np.stack(lvl, 1).astype(np.int32).reshape(P, -1),
    }
    nc = bacc.Bacc("TRN2", target_bir_lowering=False, num_devices=1, dynamic_dma_scratch_size=1024)
    arrays = {f"in_{k}": np.ascontiguousarray(v) for k, v in arrays.items()}
    src = {k[3:]: nc.dram_tensor(k, v.shape, mybir.dt.from_np(v.dtype), kind="ExternalInput").ap() for k, v in arrays.items()}
    out = nc.dram_tensor("out", (KT, P, SEQ), F32, kind="ExternalOutput").ap()
    build(nc, src, out)
    r = run(nc, [arrays], core_ids=[0])
    return np.ascontiguousarray(r.results[0]["out"].reshape(D, SEQ).T).reshape(1, SEQ, D)
```
